# Optimizing a Trainium2 kernel written in Bass

```python
import jax, jax.numpy as jnp
from jax import lax
import numpy as np

D_MODEL = 1024
BATCH = 1
SEQ = 1024
DEPTH = 1

CHUNK = 64
RMS_EPS = 1e-6
LN_EPS = 1e-5
D_FF = 2816
DN_HEADS = 8
DN_DK = 128
DN_DV = 128
DN_CONV = 4
DN_QK = DN_HEADS * DN_DK
DN_V = DN_HEADS * DN_DV
GM_GROUPS = 8
GM_WIDTH = 1024
GM_CH = GM_WIDTH // GM_GROUPS
GM_CHUNK = 128
D_IN = 2 * DN_QK + 2 * DN_V + 2 * DN_HEADS + 2 * GM_WIDTH + 2 * D_MODEL

kernel_name = "hybrid_deltanet_gmlp_macaron"

def rmsnorm(x, w):
    x32 = x.astype(jnp.float32)
    y = x32 * lax.rsqrt(jnp.mean(x32 * x32, axis=-1, keepdims=True) + RMS_EPS)
    return (y * w.astype(jnp.float32)).astype(x.dtype)

def layernorm(x, w, b):
    x32 = x.astype(jnp.float32)
    mu = jnp.mean(x32, axis=-1, keepdims=True)
    xc = x32 - mu
    y = xc * lax.rsqrt(jnp.mean(xc * xc, axis=-1, keepdims=True) + LN_EPS)
    return (y * w.astype(jnp.float32) + b.astype(jnp.float32)).astype(x.dtype)

def l2norm(x):
    return x * lax.rsqrt(jnp.sum(x * x, axis=-1, keepdims=True) + 1e-6)

def swiglu_ffn(x, w_gate, w_up, w_down):
    return (jax.nn.silu(x @ w_gate) * (x @ w_up)) @ w_down

def causal_depthwise_conv(x, w):
    k_len, c = w.shape
    return lax.conv_general_dilated(
        x, w[:, None, :].astype(x.dtype), window_strides=(1,),
        padding=[(k_len - 1, 0)], dimension_numbers=("NWC", "WIO", "NWC"),
        feature_group_count=c)

def gated_delta_rule_chunked(q, k, v, beta, log_alpha):
    f32 = jnp.float32
    b, s, h, dk = q.shape
    dv = v.shape[-1]
    n = s // CHUNK

    def chunks(t):
        return jnp.moveaxis(t.astype(f32).reshape((b, n, CHUNK) + t.shape[2:]), 2, 3)

    q = chunks(q) * (dk ** -0.5)
    k = chunks(k)
    v = chunks(v)
    beta = chunks(beta)
    g = jnp.cumsum(chunks(log_alpha), axis=-1)

    idx = jnp.arange(CHUNK)
    causal = idx[:, None] >= idx[None, :]
    strict = idx[:, None] > idx[None, :]
    gdiff = g[..., :, None] - g[..., None, :]
    decay = jnp.where(causal, jnp.exp(jnp.where(causal, gdiff, 0.0)), 0.0)

    kk = jnp.einsum("bnhid,bnhjd->bnhij", k, k)
    a_mat = jnp.where(strict, beta[..., :, None] * kk * decay, 0.0) + jnp.eye(CHUNK, dtype=f32)
    rhs = jnp.concatenate([v * beta[..., None], k * (beta * jnp.exp(g))[..., None]], axis=-1)
    sol = lax.linalg.triangular_solve(a_mat, rhs, left_side=True, lower=True, unit_diagonal=True)
    u, w = sol[..., :dv], sol[..., dv:]

    qk = jnp.einsum("bnhid,bnhjd->bnhij", q, k) * decay
    q_dec = q * jnp.exp(g)[..., None]
    k_dec = k * jnp.exp(g[..., -1:] - g)[..., None]
    g_last = jnp.exp(g[..., -1])

    def step(state, xs):
        qd, kd, u_c, w_c, qk_c, gl = xs
        v_new = u_c - jnp.einsum("bhcd,bhde->bhce", w_c, state)
        o = (jnp.einsum("bhcd,bhde->bhce", qd, state)
             + jnp.einsum("bhij,bhje->bhie", qk_c, v_new))
        state = state * gl[..., None, None] + jnp.einsum("bhcd,bhce->bhde", kd, v_new)
        return state, o

    xs = tuple(jnp.moveaxis(t, 1, 0) for t in (q_dec, k_dec, u, w, qk, g_last))
    state0 = jnp.zeros((b, h, dk, dv), f32)
    _, o = lax.scan(step, state0, xs)
    o = jnp.moveaxis(jnp.moveaxis(o, 0, 1), 3, 2)
    return o.reshape(b, s, h, dv)

def spatial_gating(u, v, norm_w, norm_b, w_s, b_s):
    b, s, _ = v.shape
    n_grp = s // GM_CHUNK
    v = layernorm(v, norm_w, norm_b)
    pos = jnp.arange(GM_CHUNK)
    mask = (pos[None, :] // CHUNK) <= (pos[:, None] // CHUNK)
    w_m = jnp.where(mask[None], w_s, 0.0).astype(v.dtype)
    vg = v.reshape(b, n_grp, GM_CHUNK, GM_GROUPS, GM_CH)
    mixed = (jnp.einsum("hij,bgjhc->bgihc", w_m, vg)
             + jnp.swapaxes(b_s, 0, 1).astype(v.dtype)[None, None, :, :, None])
    return u * mixed.reshape(b, s, GM_WIDTH)

def hybrid_mixer(h, norm_w, w_in, conv_w, a_log, dt_bias, dn_norm_w, dn_w_o,
                 sgu_norm_w, sgu_norm_b, sgu_w_s, sgu_b, gm_w_o, w_out):
    b, s, _ = h.shape
    f32 = jnp.float32
    n = rmsnorm(h, norm_w)
    proj = n @ w_in
    qkv_w = 2 * DN_QK + DN_V
    sizes = (qkv_w, DN_V, DN_HEADS, DN_HEADS, GM_WIDTH, GM_WIDTH, D_MODEL)
    points = [int(p) for p in np.cumsum(sizes)]
    qkv, g_out, b_raw, a_raw, gm_u, gm_v, gate_a, gate_b = jnp.split(proj, points, axis=-1)

    qkv = jax.nn.silu(causal_depthwise_conv(qkv, conv_w))
    q, k, v = jnp.split(qkv, [DN_QK, 2 * DN_QK], axis=-1)
    q = l2norm(q.astype(f32).reshape(b, s, DN_HEADS, DN_DK))
    k = l2norm(k.astype(f32).reshape(b, s, DN_HEADS, DN_DK))
    v = v.reshape(b, s, DN_HEADS, DN_DV)
    beta = jax.nn.sigmoid(b_raw.astype(f32))
    log_alpha = -jnp.exp(a_log.astype(f32)) * jax.nn.softplus(a_raw.astype(f32) + dt_bias.astype(f32))
    o = gated_delta_rule_chunked(q, k, v, beta, log_alpha)
    o = rmsnorm(o, dn_norm_w) * jax.nn.silu(g_out.astype(f32).reshape(b, s, DN_HEADS, DN_DV))
    y_a = o.reshape(b, s, DN_V).astype(h.dtype) @ dn_w_o

    sg = spatial_gating(jax.nn.gelu(gm_u, approximate=False), jax.nn.gelu(gm_v, approximate=False),
                        sgu_norm_w, sgu_norm_b, sgu_w_s, sgu_b)
    y_b = sg @ gm_w_o

    merged = jax.nn.sigmoid(gate_a) * y_a + jax.nn.sigmoid(gate_b) * y_b
    return merged @ w_out

def setup_inputs(seed: int = 0) -> dict:
    key = jax.random.key(seed)
    ks = iter(jax.random.split(key, 32))
    f32 = jnp.float32

    def dense(shape, fan_in):
        return jax.random.normal(next(ks), shape, f32) * (fan_in ** -0.5)

    def gain(shape):
        return 1.0 + 0.05 * jax.random.normal(next(ks), shape, f32)

    L = DEPTH
    x = jax.random.normal(next(ks), (BATCH, SEQ, D_MODEL), f32)
    ffn1_norm_w = gain((L, D_MODEL))
    ffn1_w_gate = dense((L, D_MODEL, D_FF), D_MODEL)
    ffn1_w_up = dense((L, D_MODEL, D_FF), D_MODEL)
    ffn1_w_down = dense((L, D_FF, D_MODEL), D_FF)
    mix_norm_w = gain((L, D_MODEL))
    w_in = dense((L, D_MODEL, D_IN), D_MODEL)
    dn_conv_w = dense((L, DN_CONV, 2 * DN_QK + DN_V), DN_CONV)
    dn_a_log = jnp.log(jax.random.uniform(next(ks), (L, DN_HEADS), f32, 1.0, 16.0))
    dt = jnp.exp(jax.random.uniform(next(ks), (L, DN_HEADS), f32, np.log(1e-3), np.log(1e-1)))
    dn_dt_bias = dt + jnp.log(-jnp.expm1(-dt))
    dn_out_norm_w = gain((L, DN_DV))
    dn_w_o = dense((L, DN_V, D_MODEL), DN_V)
    sgu_norm_w = gain((L, GM_WIDTH))
    sgu_norm_b = 0.02 * jax.random.normal(next(ks), (L, GM_WIDTH), f32)
    sgu_w_s = 0.5 * dense((L, GM_GROUPS, GM_CHUNK, GM_CHUNK), GM_CHUNK)
    sgu_b = gain((L, GM_GROUPS, GM_CHUNK))
    gmlp_w_o = dense((L, GM_WIDTH, D_MODEL), GM_WIDTH)
    w_out = dense((L, D_MODEL, D_MODEL), D_MODEL)
    ffn2_norm_w = gain((L, D_MODEL))
    ffn2_w_gate = dense((L, D_MODEL, D_FF), D_MODEL)
    ffn2_w_up = dense((L, D_MODEL, D_FF), D_MODEL)
    ffn2_w_down = dense((L, D_FF, D_MODEL), D_FF)
    final_norm_w = gain((D_MODEL,))
    return {"x": x, "ffn1_norm_w": ffn1_norm_w, "ffn1_w_gate": ffn1_w_gate, "ffn1_w_up": ffn1_w_up,
            "ffn1_w_down": ffn1_w_down, "mix_norm_w": mix_norm_w, "w_in": w_in, "dn_conv_w": dn_conv_w,
            "dn_a_log": dn_a_log, "dn_dt_bias": dn_dt_bias, "dn_out_norm_w": dn_out_norm_w,
            "dn_w_o": dn_w_o, "sgu_norm_w": sgu_norm_w, "sgu_norm_b": sgu_norm_b, "sgu_w_s": sgu_w_s,
            "sgu_b": sgu_b, "gmlp_w_o": gmlp_w_o, "w_out": w_out, "ffn2_norm_w": ffn2_norm_w,
            "ffn2_w_gate": ffn2_w_gate, "ffn2_w_up": ffn2_w_up, "ffn2_w_down": ffn2_w_down,
            "final_norm_w": final_norm_w}

def reference(x, ffn1_norm_w, ffn1_w_gate, ffn1_w_up, ffn1_w_down, mix_norm_w, w_in, dn_conv_w,
              dn_a_log, dn_dt_bias, dn_out_norm_w, dn_w_o, sgu_norm_w, sgu_norm_b, sgu_w_s, sgu_b,
              gmlp_w_o, w_out, ffn2_norm_w, ffn2_w_gate, ffn2_w_up, ffn2_w_down, final_norm_w):
    h = x
    for l in range(DEPTH):
        h = h + 0.5 * swiglu_ffn(rmsnorm(h, ffn1_norm_w[l]), ffn1_w_gate[l], ffn1_w_up[l], ffn1_w_down[l])
        h = h + hybrid_mixer(h, mix_norm_w[l], w_in[l], dn_conv_w[l], dn_a_log[l], dn_dt_bias[l],
                             dn_out_norm_w[l], dn_w_o[l], sgu_norm_w[l], sgu_norm_b[l], sgu_w_s[l],
                             sgu_b[l], gmlp_w_o[l], w_out[l])
        h = h + 0.5 * swiglu_ffn(rmsnorm(h, ffn2_norm_w[l]), ffn2_w_gate[l], ffn2_w_up[l], ffn2_w_down[l])
    return rmsnorm(h, final_norm_w)


_drawn_inputs = setup_inputs


def setup_inputs(seed=0):
    import zlib

    import numpy as np

    out = dict(_drawn_inputs(seed))
    spreads = {}
    factors = {'dn_out_norm_w': 3.534,
     'sgu_norm_w': 8.0,
     'sgu_norm_b': 32.94,
     'sgu_b': 3.664,
     'ffn2_norm_w': 3.222}
    for name, (base, spread) in spreads.items():
        noise = np.random.default_rng([zlib.crc32(name.encode()), seed]).standard_normal(out[name].shape)
        drawn = base * np.exp(spread * noise) if base else spread * noise
        out[name] = __import__('jax').numpy.asarray(drawn.astype(out[name].dtype))
    for name, factor in factors.items():
        out[name] = (out[name] * factor).astype(out[name].dtype)
    return out
```

```python
import concourse.bass as bass
import numpy as np
from concourse import mybir
from contextlib import ExitStack

P = 128
SEQ = 1024
HALF = 512
D = 1024
DT = D // P
FF = 2816
FT = FF // P
FF_GROUPS = (8, 8, 6)
HEADS = 8
TAPS = 4
C = 128
NC = SEQ // C
HG = 4
LEVELS = 7
LANE_A = 32
RMS_EPS, LN_EPS, L2_EPS = 1e-6, 1e-5, 1e-6

PHASES = []
for _f in (1,):
    for _g, _n in enumerate(FF_GROUPS):
        PHASES += [(f"gu1_{_g}", _n, _n), (f"down1_{_g}", DT // 2, DT // 2)]
PHASES += [("qk", HEADS, HEADS), ("ab", 1, 0), ("v", HEADS // 2, HEADS // 2), ("g", HEADS // 2, HEADS // 2),
           ("gaya", DT, DT), ("uv", DT, DT), ("gb", DT // 2, DT // 2), ("yb", DT // 2, DT // 2),
           ("wo", DT // 2, DT // 2)]
for _g, _n in enumerate(FF_GROUPS):
    PHASES += [(f"gu2_{_g}", _n, _n), (f"down2_{_g}", DT // 2, DT // 2)]
BASE, _a, _b = {}, 0, 0
for _name, _na, _nb in PHASES:
    BASE[_name] = (_a, _b)
    _a, _b = _a + _na, _b + _nb
UNITS = (_a, _b)

V_N1, V_NM, V_N2, V_NF, V_SW, V_SB, V_DN, V_DT, V_AL, V_CW = 0, 8, 16, 24, 32, 40, 48, 49, 50, 51
V_ALL = V_CW + 3 * HEADS * TAPS


def build(nc, x, vec, cst, w_gate1, w_up1, w_down1, w_in, w_ba, w_ya, w_yb, w_out, w_s, b_s,
          w_gate2, w_up2, w_down2, h_spill, m_spill, out):
    f32, f32r = mybir.dt.float32, mybir.dt.float32r
    ALU, ACT = mybir.AluOpType, mybir.ActivationFunctionType
    ds = bass.ds

    ctx = ExitStack()
    with ctx:
        KB = 1024
        start = (nc.sbuf_base + 63) // 64 * 64
        R = [start + 32 * KB * n for n in range(5)]
        W0 = start + 160 * KB
        S0 = W0 + 24 * KB
        S1 = S0 + 4128
        S2 = S1 + 4 * KB
        RS = S2 + 4 * KB
        DC = RS + 4 * KB
        SM = DC + 4 * KB

        def at(name, shape, dt, off):
            return nc.alloc_sbuf_tensor_at(name, shape, dt, offset=off)

        def big(name, dt, r):
            return at(name, [P, DT, SEQ], dt, R[r])

        h1 = big("h1", f32, 0)
        xh1, xl1 = big("xh1", f32r, 3), big("xl1", f32r, 4)
        hh1, hl1 = big("hh1", f32r, 1), big("hl1", f32r, 2)
        qo, kk_, vv_ = big("qo", f32, 0), big("kfeat", f32, 1), big("vfeat", f32, 2)
        xhm, xlm = big("xhm", f32r, 3), big("xlm", f32r, 4)
        oh, ol = big("oh", f32r, 1), big("ol", f32r, 2)
        merged_a = big("merged_a", f32, 0)
        gv, uu = big("gv", f32, 1), big("uu", f32, 2)
        sh, sl = big("sh", f32r, 1), big("sl", f32r, 2)
        sig_b = big("sig_b", f32, 0)
        mh, ml = big("mh", f32r, 3), big("ml", f32r, 4)
        h2 = big("h2", f32, 0)
        xh2, xl2 = big("xh2", f32r, 1), big("xl2", f32r, 2)
        hh2, hl2 = big("hh2", f32r, 3), big("hl2", f32r, 4)
        w_raw = [at(f"w_raw{s}", [P, 8, P], f32, W0 + 4 * KB * s) for s in range(2)]
        w_hi = [at(f"w_hi{s}", [P, 8, P], f32r, W0 + 8 * KB + 4 * KB * s) for s in range(2)]
        w_lo = [at(f"w_lo{s}", [P, 8, P], f32r, W0 + 16 * KB + 4 * KB * s) for s in range(2)]
        s0p = at("s0p", [P, SEQ + 8], f32, S0)
        s0, s1, s2 = (at(n, [P, SEQ], f32, o) for n, o in (("s0", S0), ("s1", S1), ("s2", S2)))
        sc = [s0, s1]
        rstd = at("rstd", [P, SEQ], f32, RS)
        masks = at("masks", [P, 8, P], f32, DC)
        wsT = at("wsT", [P, 8, P], f32, DC)
        o_ = SM
        def small(name, shape):
            nonlocal o_
            n = int(np.prod(shape[1:])) * 4
            t = at(name, shape, f32, o_)
            o_ += (n + 31) // 32 * 32
            return t
        vecs = small("vecs", [P, V_ALL])
        ident = small("ident", [P, P])
        upper = small("upper", [P, P])
        ones = small("ones", [P, P])
        la, beta, gcol, eg, kd, gl = (small(n, [P, NC * HEADS]) for n in ("la", "beta", "gcol", "eg", "kd", "gl"))
        st = small("st", [P, 16])
        bnst = small("bnst", [P, 16])
        consts = small("consts", [P, 8])
        print("SBUF left", nc.sbuf_usable_end - o_)

        dn = {}
        off = W0
        for n in ("S", "kTs", "Ktm", "V", "AT", "NT", "X", "TT", "T"):
            for g in range(2):
                dn[n, g] = at(f"dn_{n}{g}", [P, HG, P], f32, off)
                off += 2 * KB
        assert off <= RS

        acc = [ctx.enter_context(nc.psum_tensor(f"acc{s}", [P, SEQ], f32)) for s in range(2)]
        aux = [ctx.enter_context(nc.psum_tensor(f"aux{s}", [P, SEQ], f32)) for s in range(2)]
        bank = {(g, n): (acc if n < 2 else aux)[g][:, HALF * (n % 2):HALF * (n % 2) + HALF]
                .rearrange("p (h i) -> p h i", h=HG) for g in range(2) for n in range(4)}

        def sem(name):
            return ctx.enter_context(nc.semaphore(name))

        w_loaded = [sem(f"w_loaded{s}") for s in range(2)]
        w_hi_done = [sem(f"w_hi_done{s}") for s in range(2)]
        w_ready = [sem(f"w_ready{s}") for s in range(2)]
        acc_done = [sem(f"acc_done{s}") for s in range(2)]
        acc_free = [sem(f"acc_free{s}") for s in range(2)]
        vec_in, cst_in, x_in = sem("vec_in"), sem("cst_in"), [sem(f"x_in{k}") for k in range(DT)]
        spilled, h_back, m_spilled, m_back = sem("spilled"), sem("h_back"), sem("m_spilled"), [sem(f"m_back{s}") for s in range(2)]
        ws_in = sem("ws_in")
        setup = sem("setup")
        out_sem = sem("out_sem")

        class Chain:
            def __init__(self, eng, s, i, per):
                self.eng, self.s, self.i, self.per, self.k = eng, s, i, per, 0
            def link(self, ins):
                self.k += 1
                ins.then_inc(self.s, 1)
                self.eng.wait_ge(self.s, self.i * self.per + self.k)
            def end(self):
                assert self.k == self.per, (self.k, self.per)

        norm_sems = {n: sem(f"norm_{n}") for n in (
            "xt",
            "hi",
            "ready",
            "h",
            "sq",
            "added",
            "sums",
            "root",
            "inv",
            "diag",
            "bc",
            "rstd",
            "zero",
        )}

        class Norm:
            def __init__(self, n):
                self.n, self.tile, self.h_tile = n, DT * n, DT * (n - 1)
                self.xt = norm_sems["xt"]
                self.hi = norm_sems["hi"]
                self.ready = norm_sems["ready"]
                self.h = norm_sems["h"]
                self.sq = norm_sems["sq"]
                self.added = norm_sems["added"]
                self.sums = norm_sems["sums"]
                self.root = norm_sems["root"]
                self.inv = norm_sems["inv"]
                self.diag = norm_sems["diag"]
                self.bc = norm_sems["bc"]
                self.rstd = norm_sems["rstd"]
                self.zero = norm_sems["zero"]
        norms = [Norm(n) for n in range(4)]

        class Ffn:
            def __init__(self, f):
                self.gate = sem(f"f{f}_gate")
                self.silu = sem(f"f{f}_silu")
                self.prod = sem(f"f{f}_prod")
                self.hi = sem(f"f{f}_hi")
                self.ready = sem(f"f{f}_ready")
                self.up = sem(f"f{f}_up")
        ffns = [Ffn(1), Ffn(2)]

        s_conv_a, s_conv = sem("conv_chain_a"), sem("conv_chain_b")
        conv_done, silu_done, sq_done = sem("conv_done"), sem("silu_done"), sem("sq_done")
        l2_sum, l2_ln, l2_inv, l2_used = sem("l2_sum"), sem("l2_ln"), sem("l2_inv"), sem("l2_used")
        v_chain, v_conv, v_done = sem("v_chain"), sem("v_conv"), sem("v_done")
        ab = {n: sem(f"ab_{n}") for n in ("z", "act", "dve", "t", "cols", "g", "gv", "gact")}
        g_s = {n: sem(f"g_{n}") for n in ("sq", "sum", "ln", "inv", "gate", "silu", "norm", "prod", "hi", "ready")}
        y_s = {n: sem(f"y_{n}") for n in ("gate", "sig", "out")}
        u_s = {n: sem(f"u_{n}") for n in ("arg", "done", "bias", "w", "rows")}
        b_s_ = {n: sem(f"b_{n}") for n in ("gate", "sig", "copy", "tr", "bn", "var", "root", "inv", "z", "mix",
                                           "chain", "prod", "hi", "ready")}
        yb_s = {n: sem(f"yb_{n}") for n in ("t", "m", "hi", "ready")}
        w_x = sem("prologue_x")

        def wait(eng, s, v):
            if not isinstance(v, int) or v > 0:
                eng.wait_ge(s, v)

        def stand_alone(eng):
            eng.wait_ge(setup, 7)

        def loop(eng, n, body, first=False, last=True):
            lo, hi = int(first), n - int(last)
            if first:
                body(0)
            if hi - lo == 1:
                body(lo)
            elif hi > lo:
                with eng.Fori(lo, hi) as i:
                    body(i)
            if last and hi >= lo:
                body(n - 1)

        def is_last(i, n):
            return isinstance(i, int) and i == n - 1

        def bc_row(t, n):
            return t.unsqueeze(2).to_broadcast([P, n, P])

        def bc_mid(t, n):
            return t.unsqueeze(1).to_broadcast([P, n, P])

        def kt_next(name, s, i, n):
            if is_last(i, n):
                if name == "v" or name == f"down2_{len(FF_GROUPS) - 1}":
                    return 0
                if name.startswith("gu"):
                    return FF_GROUPS[int(name[-1])]
                return 8
            return FF_GROUPS[int(name[-1])] if name.startswith("down") else 8

        dn_s = {n: sem(f"dn_{n}") for n in (
            "kTs", "vTs", "laU", "G", "EG", "argA", "arg", "D", "kk", "qk", "qd", "tk", "tv", "NTa", "NT", "AT",
            "TTa", "TT", "tT", "T", "X", "xp", "up", "Kd", "V", "KS", "eKS", "Rr", "TR", "vn", "o", "oc", "Kv",
            "Sg", "S")}
        dn_done = sem("dn_done")

        block = ctx.enter_context(nc.Block())

        @block.sync
        def _(sp):
            sp.dma_start(vecs[:, :], vec).then_inc(vec_in, 16)
            for k in range(DT):
                sp.dma_start(h1[:, k, :], x[k]).then_inc(x_in[k], 16)

            def load(name, s, i, n, src, kt):
                u = BASE[name][s] + i
                wait(sp, w_ready[s], u)
                if name == "g" and isinstance(i, int) and i == 0 and s == 0:
                    sp.wait_ge(dn_done, 2)
                    sp.dma_start(wsT[:, :, :], w_s).then_inc(ws_in, 16)
                sp.dma_start(w_raw[s][:, 0:kt, :], src).then_inc(w_loaded[s], 16)

            def pick(w, t):
                return w[ds(t, 1)].rearrange("a p k m -> p (a k) m") if not isinstance(t, int) else w[t]

            def two(name, n, a, b, kt=8, first=False):
                def body(i):
                    load(name, 0, i, n, a(i), kt)
                    load(name, 1, i, n, b(i), kt)
                loop(sp, n, body, first=first, last=False)

            def ffn_loads(f, wg, wu, wd):
                t0 = 0
                for g, n in enumerate(FF_GROUPS):
                    two(f"gu{f}_{g}", n, lambda i: pick(wg, i + t0), lambda i: pick(wu, i + t0), first=(g == 0))
                    def down(m):
                        return wd[ds(m, 1), :, t0:t0 + n, :].rearrange("a p k m -> p (a k) m")
                    two(f"down{f}_{g}", DT // 2, lambda i: down(i * 2), lambda i: down(i * 2 + 1), kt=n)
                    t0 += n

            ffn_loads(1, w_gate1, w_up1, w_down1)
            two("qk", HEADS, lambda i: pick(w_in, i), lambda i: pick(w_in, i + 8))
            load("ab", 0, 0, 1, w_ba[0], 8)
            two("v", 4, lambda i: pick(w_in, i * 2 + 16), lambda i: pick(w_in, i * 2 + 17))
            two("g", 4, lambda i: pick(w_in, i * 2 + 24), lambda i: pick(w_in, i * 2 + 25), first=True)
            two("gaya", 8, lambda i: pick(w_in, i + 48), lambda i: pick(w_ya, i))
            sp.wait_ge(g_s["norm"], HEADS)
            sp.dma_start(s2[:, :], b_s).then_inc(ws_in, 16)
            two("uv", 8, lambda i: pick(w_in, i + 32), lambda i: pick(w_in, i + 40))
            two("gb", 4, lambda i: pick(w_in, i * 2 + 56), lambda i: pick(w_in, i * 2 + 57))
            two("yb", 4, lambda i: pick(w_yb, i * 2), lambda i: pick(w_yb, i * 2 + 1))
            two("wo", 4, lambda i: pick(w_out, i * 2), lambda i: pick(w_out, i * 2 + 1))
            ffn_loads(2, w_gate2, w_up2, w_down2)
            sp.wait_ge(out_sem, 16 * DT)

        @block.gpsimd
        def _(pool):
            nc.gpsimd.memset(ones[:, :], 1.0).then_inc(setup, 1)
            for n, v in enumerate((RMS_EPS, LN_EPS, L2_EPS, -0.5 * float(np.log(P)), 1.0, 0.0)):
                nc.gpsimd.memset(consts[:, n:n + 1], v).then_inc(setup, 1)
            pool.dma_start(ident[:, :], cst[:, 0, :]).then_inc(cst_in, 16)
            pool.dma_start(upper[:, :], cst[:, 1, :]).then_inc(cst_in, 16)
            pool.dma_start(masks[:, :, :], cst[:, 2:10, :]).then_inc(cst_in, 16)

            def spill(i):
                for b in range(2):
                    pool.wait_ge(norms[1].h, norms[1].h_tile + i * 2 + b + 1)
                    pool.dma_start(h_spill[ds(i * 2 + b, 1)].rearrange("a p t -> p (a t)"),
                                   h1[:, ds(i * 2 + b, 1), :].rearrange("p a t -> p (a t)")).then_inc(spilled, 16)
            loop(pool, 4, spill, last=False)

            def spill_m(i):
                pool.wait_ge(y_s["out"], i + 1)
                pool.dma_start(m_spill[ds(i, 1)].rearrange("a p t -> p (a t)"),
                               merged_a[:, ds(i, 1), :].rearrange("p a t -> p (a t)")).then_inc(m_spilled, 16)
            loop(pool, 8, spill_m, last=False)
            pool.wait_ge(m_spilled, 16 * 8)
            pool.wait_ge(b_s_["ready"], 8)

            def back_m(i):
                for b in range(2):
                    if not isinstance(i, int):
                        pool.wait_ge(yb_s["ready"], i * 2 + b - 1)
                    pool.dma_start(sc[b][:, :], m_spill[ds(i * 2 + b, 1)].rearrange("a p t -> p (a t)"))\
                        .then_inc(m_back[b], 16)
            loop(pool, 4, back_m, first=True, last=False)

            def back_h(m):
                pool.wait_ge(yb_s["m"], m + 1)
                pool.dma_start(h2[:, ds(m, 1), :].rearrange("p a t -> p (a t)"),
                               h_spill[ds(m, 1)].rearrange("a p t -> p (a t)")).then_inc(h_back, 16)
            pool.wait_ge(spilled, 16 * DT)
            loop(pool, 8, back_h, last=False)

        @block.scalar
        def _(act):
            A = nc.scalar.activation

            def split_hi(name, s, i, n):
                kt = kt_next(name, s, i, n)
                if kt:
                    u = BASE[name][s] + i
                    act.wait_ge(acc_done[s], u + 1)
                    act.wait_ge(w_loaded[s], (u + 2) * 16)
                    A(w_hi[s][:, 0:kt, :], w_raw[s][:, 0:kt, :], ACT.Copy).then_inc(w_hi_done[s], 1)

            def first_split(name):
                for s in range(2):
                    u = BASE[name][s]
                    act.wait_ge(w_loaded[s], 16 * (u + 1))
                    A(w_hi[s][:, :, :], w_raw[s][:, :, :], ACT.Copy).then_inc(w_hi_done[s], 1)

            def square_and_hi(nm, h, m, xh, x_only=False):
                stand_alone(act)
                act.wait_ge(nm.h, nm.h_tile + m + 1)
                wait(act, nm.added, nm.tile + m)
                A(s1[:, :], h[:, ds(m, 1), :].rearrange("p a t -> p (a t)"), ACT.Square).then_inc(nm.sq, 1)
                if xh is not None:
                    stand_alone(act)
                    act.wait_ge(nm.xt, nm.tile + m + 1)
                    A(xh[:, ds(m, 1), :].rearrange("p a t -> p (a t)"), s0[:, :], ACT.Copy).then_inc(nm.hi, 1)

            def root(nm):
                act.wait_ge(nm.sums, nm.n + 1)
                A(st[:, 0:DT], aux[0][:, 0:DT], ACT.Sqrt, bias=consts[:, 0:1], scale=1.0 / D).then_inc(nm.root, 1)

            def broadcast(nm):
                act.wait_ge(nm.bc, nm.n + 1)
                A(rstd[:, :], aux[0][:, :], ACT.Copy).then_inc(nm.rstd, 1)

            act.wait_ge(setup, 7)
            first_split("gu1_0")
            for k in range(DT):
                act.wait_ge(x_in[k], 16)
                wait(act, norms[0].added, norms[0].tile + k)
                A(s1[:, :], h1[:, k, :], ACT.Square).then_inc(norms[0].sq, 1)
                act.wait_ge(norms[0].xt, norms[0].tile + k + 1)
                A(xh1[:, k, :], s0[:, :], ACT.Copy).then_inc(norms[0].hi, 1)

            def ffn(f, nm, nm_next, hh, h, xh):
                sg = ffns[f - 1]
                t0 = 0
                for g, n in enumerate(FF_GROUPS):
                    name = f"gu{f}_{g}"
                    def body(i):
                        t = i + t0
                        if g == 0 and isinstance(i, int) and i == 0:
                            root(nm)
                        split_hi(name, 0, i, n)
                        if g == 0 and isinstance(i, int) and i == 0:
                            broadcast(nm)
                        act.wait_ge(sg.gate, t + 1)
                        A(s0[:, :], s0[:, :], ACT.Silu).then_inc(sg.silu, 1)
                        split_hi(name, 1, i, n)
                        stand_alone(act)
                        act.wait_ge(sg.prod, t + 1)
                        A(hh[:, ds(i, 1), :].rearrange("p a t -> p (a t)"), s1[:, :], ACT.Copy).then_inc(sg.hi, 1)
                    loop(act, n, body, first=(g == 0))
                    t0 += n
                    dname = f"down{f}_{g}"
                    lastg = g == len(FF_GROUPS) - 1
                    def dbody(i):
                        for s in range(2):
                            split_hi(dname, s, i, DT // 2)
                            if lastg:
                                square_and_hi(nm_next, h, i * 2 + s, xh)
                    loop(act, DT // 2, dbody, first=lastg)

            ffn(1, norms[0], norms[1], hh1, h1, xhm)

            def l2_inverse(j):
                for b in range(2):
                    act.wait_ge(l2_sum, j * 2 + b + 1)
                    A(sc2[b][:, :], aux[b][:, :], ACT.Ln, bias=consts[:, 2:3]).then_inc(l2_ln, 1)
                for b in range(2):
                    act.wait_ge(l2_ln, j * 2 + b + 1)
                    A(sc2[b][:, :], sc2[b][:, :], ACT.Exp, scale=-0.5,
                      bias=consts[:, 3:4] if b == 0 else 0.0).then_inc(l2_inv, 1)

            sc2 = [s1, s2]

            def qk(i):
                f0 = isinstance(i, int) and i == 0
                if f0:
                    root(norms[1])
                split_hi("qk", 0, i, HEADS)
                if f0:
                    broadcast(norms[1])
                else:
                    l2_inverse(i - 1)
                for b, dst in enumerate((qo, kk_)):
                    if b:
                        split_hi("qk", 1, i, HEADS)
                    row = dst[:, ds(i, 1), :].rearrange("p a t -> p (a t)")
                    stand_alone(act)
                    act.wait_ge(conv_done, i * 2 + b + 1)
                    A(row, row, ACT.Silu).then_inc(silu_done, 1)
                    stand_alone(act)
                    act.wait_ge(silu_done, i * 2 + b + 1)
                    act.wait_ge(l2_used, i * 2 + b + 1)
                    A(sc2[b][:, :], row, ACT.Square).then_inc(sq_done, 1)
            loop(act, HEADS, qk, first=True)

            split_hi("ab", 0, 0, 2)
            l2_inverse(HEADS - 1)

            act.wait_ge(ab["z"], 1)
            act.wait_ge(l2_used, 2 * HEADS + 2)
            lane = slice(LANE_A, LANE_A + HEADS)
            A(s1[0:64, :], s0[0:64, :], ACT.Copy).then_inc(ab["act"], 1)
            A(s2[lane, :], s0[lane, :], ACT.Abs, bias=vecs[lane, V_DT:V_DT + 1]).then_inc(ab["act"], 1)
            A(st[lane, 0:1], vecs[lane, V_AL:V_AL + 1], ACT.Exp).then_inc(ab["act"], 1)
            act.wait_ge(ab["act"], 3)
            A(s2[lane, :], s2[lane, :], ACT.Exp, scale=-1.0).then_inc(ab["act"], 1)
            act.wait_ge(ab["act"], 4)
            A(s2[lane, :], s2[lane, :], ACT.Ln, bias=consts[lane, 4:5]).then_inc(ab["act"], 1)
            A(s1[0:HEADS, :], s1[0:HEADS, :], ACT.Sigmoid).then_inc(ab["act"], 1)

            def v(i):
                for s in range(2):
                    split_hi("v", s, i, 4)
                    row = vv_[:, ds(i * 2 + s, 1), :].rearrange("p a t -> p (a t)")
                    stand_alone(act)
                    act.wait_ge(v_conv, i * 2 + s + 1)
                    A(row, row, ACT.Silu).then_inc(v_done, 1)
                if isinstance(i, int) and i == 0:
                    act.wait_ge(ab["gv"], 2)
                    A(eg[:, :], aux[1][:, 0:64], ACT.Exp).then_inc(ab["gact"], 1)
                    A(gl[:, :], aux[1][:, 64:128], ACT.Exp).then_inc(ab["gact"], 1)
                    A(kd[:, :], kd[:, :], ACT.Exp).then_inc(ab["gact"], 1)
            loop(act, 4, v, first=True)

            act.wait_ge(l2_used, 2 * HEADS + 2)
            act.wait_ge(v_done, HEADS)
            act.wait_ge(acc_done[0], BASE["g"][0])
            act.wait_ge(acc_done[1], BASE["g"][1])
            act.wait_ge(w_ready[0], BASE["g"][0])
            act.wait_ge(w_ready[1], BASE["g"][1])

            def chunk(t, g, c):
                return t[:, HG * g:HG * g + HG, ds(c * C, C)]

            def delta(c):
                for g in range(2):
                    A(dn["kTs", g][:, :, :], chunk(kk_, g, c), ACT.Copy).then_inc(dn_s["kTs"], 1)
                    A(dn["T", g][:, :, :], chunk(vv_, g, c), ACT.Copy).then_inc(dn_s["vTs"], 1)
                for g in range(2):
                    act.wait_ge(dn_s["G"], c * 2 + g + 1)
                    A(dn["TT", g][:, :, :], bank[g, 0], ACT.Exp).then_inc(dn_s["EG"], 1)
                for g in range(2):
                    act.wait_ge(dn_s["tv"], c * 2 + g + 1)
                    A(dn["V", g][:, :, :], bank[g, 3], ACT.Copy).then_inc(dn_s["V"], 1)
                for g in range(2):
                    act.wait_ge(dn_s["arg"], c * 2 + g + 1)
                    A(dn["T", g][:, :, :], dn["X", g][:, :, :], ACT.Exp).then_inc(dn_s["D"], 1)
                for l in range(LEVELS - 1):
                    for g in range(2):
                        act.wait_ge(dn_s["tT"], (c * (LEVELS - 1) + l) * 2 + g + 1)
                        A(dn["T", g][:, :, :], bank[g, 1], ACT.Copy).then_inc(dn_s["T"], 1)
                for g in range(2):
                    stand_alone(act)
                    act.wait_ge(dn_s["o"], c * 2 + g + 1)
                    A(chunk(qo, g, c), bank[g, 2], ACT.Copy).then_inc(dn_s["oc"], 1)
            with act.Fori(0, NC) as c:
                delta(c)

            for g in range(2):
                act.wait_ge(dn_s["S"], 2 * NC + 2)
                act.wait_ge(dn_s["oc"], 2 * NC)
            first_split("g")

            def gate(i):
                for s in range(2):
                    m = i * 2 + s
                    f0 = isinstance(i, int) and m == 0
                    if not f0:
                        stand_alone(act)
                        act.wait_ge(g_s["norm"], m)
                    A(s2[:, :], qo[:, ds(m, 1), :].rearrange("p a t -> p (a t)"), ACT.Square).then_inc(g_s["sq"], 1)
                    split_hi("g", s, i, 4)
                    act.wait_ge(g_s["sum"], m + 1)
                    A(s2[:, :], aux[0][:, :], ACT.Ln, scale=1.0 / P, bias=consts[:, 0:1]).then_inc(g_s["ln"], 1)
                    act.wait_ge(g_s["ln"], m + 1)
                    A(s2[:, :], s2[:, :], ACT.Exp, scale=-0.5).then_inc(g_s["inv"], 1)
                    act.wait_ge(g_s["gate"], m + 1)
                    A(sc[s][:, :], sc[s][:, :], ACT.Silu).then_inc(g_s["silu"], 1)
                    stand_alone(act)
                    act.wait_ge(g_s["prod"], m + 1)
                    A(oh[:, ds(m, 1), :].rearrange("p a t -> p (a t)"), sc[s][:, :], ACT.Copy).then_inc(g_s["hi"], 1)
            loop(act, 4, gate, first=True)

            def gaya(i):
                split_hi("gaya", 0, i, 8)
                act.wait_ge(y_s["gate"], i + 1)
                A(s0[:, :], s0[:, :], ACT.Sigmoid).then_inc(y_s["sig"], 1)
                split_hi("gaya", 1, i, 8)
            loop(act, 8, gaya)

            def uv(i):
                for s, dst in ((0, uu), (1, gv)):
                    split_hi("uv", s, i, 8)
                    stand_alone(act)
                    act.wait_ge(u_s["arg"], i * 2 + s + 1)
                    A(dst[:, ds(i, 1), :].rearrange("p a t -> p (a t)"), sc[s][:, :], ACT.Gelu).then_inc(u_s["done"], 1)
            loop(act, 8, uv)

            def gb(i):
                for s in range(2):
                    n = i * 2 + s
                    f0 = isinstance(i, int) and n == 0
                    if not f0:
                        stand_alone(act)
                        act.wait_ge(b_s_["tr"], n)
                    A(s0[:, :].rearrange("p (m t) -> p m t", m=DT), gv[:, :, ds(n * C, C)], ACT.Copy)\
                        .then_inc(b_s_["copy"], 1)
                    split_hi("gb", s, i, 4)
                    stand_alone(act)
                    act.wait_ge(b_s_["gate"], n + 1)
                    row = sig_b[:, ds(n, 1), :].rearrange("p a t -> p (a t)")
                    A(row, row, ACT.Sigmoid).then_inc(b_s_["sig"], 1)
                    act.wait_ge(b_s_["var"], n + 1)
                    A(st[:, 10:11], st[:, 9:10], ACT.Sqrt, bias=consts[:, 1:2]).then_inc(b_s_["root"], 1)
                    if not f0:
                        mix_hi(n - 1)

            def mix_hi(n):
                stand_alone(act)
                act.wait_ge(b_s_["prod"], n + 1)
                A(sh[:, :, ds(n * C, C)], uu[:, :, ds(n * C, C)], ACT.Copy).then_inc(b_s_["hi"], 1)
            act.wait_ge(u_s["done"], 16)
            loop(act, 4, gb, first=True)
            mix_hi(7)

            def yb(i):
                for s in range(2):
                    n = i * 2 + s
                    split_hi("yb", s, i, 4)
                    stand_alone(act)
                    act.wait_ge(yb_s["m"], n + 1)
                    A(mh[:, ds(n, 1), :].rearrange("p a t -> p (a t)"), sc[s][:, :], ACT.Copy).then_inc(yb_s["hi"], 1)
            loop(act, 4, yb)

            def wo(i):
                for s in range(2):
                    split_hi("wo", s, i, 4)
                    square_and_hi(norms[2], h2, i * 2 + s, xh2)
            loop(act, 4, wo, first=True)

            ffn(2, norms[2], norms[3], hh2, h2, None)
            root(norms[3])
            broadcast(norms[3])
            for k in range(DT):
                act.wait_ge(norms[3].ready, norms[3].tile + k + 1)
                act.dma_start(out[k], h2[:, k, :]).then_inc(out_sem, 16)

        @block.vector
        def _(dve):
            TT, TS, STT = nc.vector.tensor_tensor, nc.vector.tensor_scalar, nc.vector.scalar_tensor_tensor
            mult, add, sub = ALU.mult, ALU.add, ALU.subtract

            def split_lo(name, s, i, n):
                kt = kt_next(name, s, i, n)
                if kt:
                    u = BASE[name][s] + i
                    dve.wait_ge(w_hi_done[s], u + 2)
                    TT(w_lo[s][:, 0:kt, :], w_raw[s][:, 0:kt, :], w_hi[s][:, 0:kt, :].bitcast(f32), sub)\
                        .then_inc(w_ready[s], 1)

            def first_split(name):
                for s in range(2):
                    dve.wait_ge(w_hi_done[s], BASE[name][s] + 1)
                    TT(w_lo[s][:, :, :], w_raw[s][:, :, :], w_hi[s][:, :, :].bitcast(f32), sub)\
                        .then_inc(w_ready[s], 1)

            def row(t, m):
                return t[:, ds(m, 1), :].rearrange("p a t -> p (a t)")

            def statistics(nm, h, m, vcol, xh, xl):
                if xh is not None:
                    dve.wait_ge(nm.h, nm.h_tile + m + 1)
                    wait(dve, nm.ready, nm.tile + m)
                    TS(s0[:, :], row(h, m), vecs[:, ds(m + vcol, 1)], None, mult).then_inc(nm.xt, 1)
                dve.wait_ge(nm.sq, nm.tile + m + 1)
                wait(dve, nm.added, nm.tile + m)
                TT(s2[:, :], s2[:, :], s1[:, :], add).then_inc(nm.added, 1)
                if xh is not None:
                    dve.wait_ge(nm.hi, nm.tile + m + 1)
                    TT(row(xl, m), s0[:, :], row(xh, m).bitcast(f32), sub).then_inc(nm.ready, 1)

            def zero_sum(nm):
                nc.vector.memset(s2[:, :], 0.0).then_inc(nm.zero, 1)
                dve.wait_ge(nm.zero, nm.n + 1)

            def inverse(nm):
                dve.wait_ge(nm.root, nm.n + 1)
                nc.vector.reciprocal(st[:, 0:DT], st[:, 0:DT]).then_inc(nm.inv, 1)
                dve.wait_ge(nm.inv, nm.n + 1)
                TT(s2[:, :].rearrange("p (c i) -> p c i", c=NC), bc_mid(ident[:, :], NC), bc_row(st[:, 0:DT], DT), mult)\
                    .then_inc(nm.diag, 1)

            first_split("gu1_0")
            dve.wait_ge(vec_in, 16)
            dve.wait_ge(cst_in, 48)
            zero_sum(norms[0])
            for k in range(DT):
                dve.wait_ge(x_in[k], 16)
                nm = norms[0]
                wait(dve, nm.ready, nm.tile + k)
                TS(s0[:, :], h1[:, k, :], vecs[:, V_N1 + k:V_N1 + k + 1], None, mult).then_inc(nm.xt, 1)
                dve.wait_ge(nm.sq, nm.tile + k + 1)
                wait(dve, nm.added, nm.tile + k)
                TT(s2[:, :], s2[:, :], s1[:, :], add).then_inc(nm.added, 1)
                dve.wait_ge(nm.hi, nm.tile + k + 1)
                TT(xl1[:, k, :], s0[:, :], xh1[:, k, :].bitcast(f32), sub).then_inc(nm.ready, 1)

            def ffn(f, nm, nm_next, hh, hl, h, vcol, xh, xl):
                sg = ffns[f - 1]
                t0 = 0
                for g, n in enumerate(FF_GROUPS):
                    name = f"gu{f}_{g}"
                    def body(i):
                        t = i + t0
                        u = [BASE[name][s] + i for s in range(2)]
                        f0 = g == 0 and isinstance(i, int) and i == 0
                        if f0:
                            inverse(nm)
                        split_lo(name, 0, i, n)
                        if f0:
                            dve.wait_ge(nm.rstd, nm.n + 1)
                        dve.wait_ge(acc_done[0], u[0] + 1)
                        TT(s0[:, :], acc[0][:, :], rstd[:, :], mult).then_inc(sg.gate, 1)
                        dve.wait_ge(sg.gate, t + 1)
                        dve.sem_inc(acc_free[0], 1)
                        split_lo(name, 1, i, n)
                        dve.wait_ge(acc_done[1], u[1] + 1)
                        wait(dve, sg.ready, t)
                        TT(s1[:, :], acc[1][:, :], rstd[:, :], mult).then_inc(acc_free[1], 1)
                        dve.wait_ge(acc_free[1], u[1] + 1)
                        dve.wait_ge(sg.silu, t + 1)
                        TT(s1[:, :], s0[:, :], s1[:, :], mult).then_inc(sg.prod, 1)
                        dve.wait_ge(sg.hi, t + 1)
                        TT(row(hl, i), s1[:, :], row(hh, i).bitcast(f32), sub).then_inc(sg.ready, 1)
                    loop(dve, n, body, first=(g == 0))
                    t0 += n
                    dname = f"down{f}_{g}"
                    lastg = g == len(FF_GROUPS) - 1
                    if lastg:
                        zero_sum(nm_next)
                    def dbody(i):
                        for s in range(2):
                            m = i * 2 + s
                            u = BASE[dname][s] + i
                            split_lo(dname, s, i, DT // 2)
                            dve.wait_ge(acc_done[s], u + 1)
                            ins = STT(row(h, m), acc[s][:, :], 0.5, row(h, m), mult, add)
                            ins.then_inc(acc_free[s], 1)
                            if lastg:
                                dve.wait_ge(acc_free[s], u + 1)
                                dve.sem_inc(nm_next.h, 1)
                                statistics(nm_next, h, m, vcol, xh, xl)
                    loop(dve, DT // 2, dbody, first=lastg)

            ffn(1, norms[0], norms[1], hh1, hl1, h1, V_NM, xhm, xlm)

            def conv(ch, s, dst, wrow):
                ch.link(TT(s0p[:, 3:3 + SEQ], acc[s][:, :], rstd[:, :], mult))
                dve.sem_inc(acc_free[s], 1)
                ch.link(TS(dst, s0p[:, 3:3 + SEQ], vecs[:, ds(wrow * TAPS + (V_CW + TAPS - 1), 1)], None, mult))
                for j in range(TAPS - 2, -1, -1):
                    ins = STT(dst, s0p[:, j:j + SEQ], vecs[:, ds(wrow * TAPS + (V_CW + j), 1)], dst, mult, add)
                    if j:
                        ch.link(ins)
                return ins

            def l2_scale(j):
                for b, dst in enumerate((qo, kk_)):
                    dve.wait_ge(l2_inv, j * 2 + b + 1)
                    dve.wait_ge(silu_done, j * 2 + b + 1)
                    TT(row(dst, j), row(dst, j), sc2[b][:, :], mult).then_inc(l2_used, 1)

            sc2 = [s1, s2]
            padded = [False]

            def qk(i):
                f0 = isinstance(i, int) and i == 0
                ch = Chain(dve, s_conv, i, 8)
                if f0:
                    inverse(norms[1])
                split_lo("qk", 0, i, HEADS)
                if f0:
                    dve.wait_ge(spilled, 16 * DT)
                    nc.vector.memset(s0p[:, 0:3], 0.0).then_inc(s_conv_a, 1)
                    dve.wait_ge(s_conv_a, 1)
                    dve.sem_inc(l2_used, 2)
                    dve.wait_ge(norms[1].rstd, norms[1].n + 1)
                dve.wait_ge(acc_done[0], BASE["qk"][0] + i + 1)
                conv(ch, 0, row(qo, i), i).then_inc(conv_done, 1)
                if not f0:
                    l2_scale(i - 1)
                split_lo("qk", 1, i, HEADS)
                dve.wait_ge(acc_done[1], BASE["qk"][1] + i + 1)
                conv(ch, 1, row(kk_, i), i + HEADS).then_inc(conv_done, 1)
                ch.end()
            loop(dve, HEADS, qk, first=True)

            split_lo("ab", 0, 0, 2)
            dve.wait_ge(acc_done[0], BASE["ab"][0] + 1)
            dve.wait_ge(conv_done, 2 * HEADS)
            TT(s0[:, :], acc[0][:, :], rstd[:, :], mult).then_inc(ab["z"], 1)
            dve.wait_ge(ab["z"], 1)
            dve.sem_inc(acc_free[0], 1)
            l2_scale(HEADS - 1)
            lane = slice(LANE_A, LANE_A + HEADS)
            dve.wait_ge(ab["act"], 6)
            TS(s1[lane, :], s0[lane, :], vecs[lane, V_DT:V_DT + 1], 0.0, add, ALU.max).then_inc(ab["dve"], 1)
            dve.wait_ge(ab["dve"], 1)
            TT(s1[lane, :], s1[lane, :], s2[lane, :], add).then_inc(ab["dve"], 1)
            dve.wait_ge(ab["dve"], 2)
            TS(s1[lane, :], s1[lane, :], st[lane, 0:1], -1.0, mult, mult).then_inc(ab["dve"], 1)
            nc.vector.memset(s0p[:, 0:3], 0.0).then_inc(ab["dve"], 1)
            dve.wait_ge(ab["dve"], 4)

            def v(i):
                for s in range(2):
                    ch = Chain(dve, v_chain, i * 2 + s, 4)
                    split_lo("v", s, i, 4)
                    dve.wait_ge(acc_done[s], BASE["v"][s] + i + 1)
                    conv(ch, s, row(vv_, i * 2 + s), i * 2 + s + 2 * HEADS).then_inc(v_conv, 1)
                    dve.wait_ge(v_conv, i * 2 + s + 1)
                    ch.end()
                    if isinstance(i, int) and i == 0 and s == 0:
                        dve.wait_ge(ab["t"], 1)
                        t = aux[0][:, 0:512].rearrange("p (c x) -> p c x", c=NC)
                        nc.vector.tensor_copy(beta[:, :].rearrange("p (c h) -> p c h", c=NC), t[:, :, 0:HEADS])\
                            .then_inc(ab["cols"], 1)
                        nc.vector.tensor_copy(la[:, :].rearrange("p (c h) -> p c h", c=NC), t[:, :, LANE_A:LANE_A + HEADS])\
                            .then_inc(ab["cols"], 1)
                if isinstance(i, int) and i == 0:
                    dve.wait_ge(ab["g"], 1)
                    nc.vector.tensor_copy(gcol[:, :], aux[1][:, 0:64]).then_inc(ab["gv"], 1)
                    dve.wait_ge(ab["gv"], 1)
                    TT(kd[:, :], aux[1][:, 64:128], gcol[:, :], sub).then_inc(ab["gv"], 1)
            loop(dve, 4, v, first=True)

            dve.wait_ge(ab["gact"], 3)
            dve.wait_ge(v_done, HEADS)
            for s in range(2):
                dve.wait_ge(acc_done[s], BASE["g"][s])
            for g in range(2):
                nc.vector.memset(dn["S", g][:, :, :], 0.0).then_inc(dn_s["S"], 1)

            def cols(t, g, c):
                return t[:, ds(c * HEADS + HG * g, HG)].unsqueeze(2).to_broadcast([P, HG, P])

            def mask(n):
                return bc_mid(masks[:, n, :], HG)

            def delta(c):
                B = lambda n, g: dn[n, g][:, :, :]
                for g in range(2):
                    TT(B("X", g), bc_mid(upper[:, :], HG), cols(la, g, c), mult).then_inc(dn_s["laU"], 1)
                for g in range(2):
                    dve.wait_ge(dn_s["EG"], c * 2 + g + 1)
                    TT(B("X", g), bank[g, 0], cols(gcol, g, c), sub).then_inc(dn_s["argA"], 1)
                for g in range(2):
                    dve.wait_ge(dn_s["argA"], c * 2 + g + 1)
                    TT(B("X", g), B("X", g), mask(0), ALU.min).then_inc(dn_s["arg"], 1)
                for g in range(2):
                    dve.wait_ge(dn_s["tk"], c * 2 + g + 1)
                    TT(B("Ktm", g), bank[g, 3], cols(kd, g, c), mult).then_inc(dn_s["Kd"], 1)
                for g in range(2):
                    dve.wait_ge(dn_s["qk"], c * 2 + g + 1)
                    dve.wait_ge(dn_s["EG"], c * 2 + g + 1)
                    q = qo[:, HG * g:HG * g + HG, ds(c * C, C)]
                    TT(q, q, B("TT", g), mult).then_inc(dn_s["qd"], 1)
                for g in range(2):
                    dve.wait_ge(dn_s["D"], c * 2 + g + 1)
                    dve.wait_ge(dn_s["kk"], c * 2 + g + 1)
                    TT(B("NT", g), bank[g, 1], B("T", g), mult).then_inc(dn_s["NTa"], 1)
                for g in range(2):
                    TT(B("AT", g), bank[g, 2], B("T", g), mult).then_inc(dn_s["AT"], 1)
                for g in range(2):
                    dve.wait_ge(dn_s["NTa"], c * 2 + g + 1)
                    TT(B("NT", g), B("NT", g), cols(beta, g, c), mult).then_inc(dn_s["NT"], 1)
                for g in range(2):
                    dve.wait_ge(dn_s["NT"], c * 2 + g + 1)
                    dve.wait_ge(dn_s["qd"], c * 2 + g + 1)
                    TT(B("TT", g), B("NT", g), mask(1), mult).then_inc(dn_s["TTa"], 1)
                for g in range(2):
                    dve.wait_ge(dn_s["TTa"], c * 2 + g + 1)
                    TT(B("TT", g), bc_mid(ident[:, :], HG), B("TT", g), sub).then_inc(dn_s["TT"], 1)
                for l in range(1, LEVELS):
                    for g in range(2):
                        dve.wait_ge(dn_s["xp"], (c * (LEVELS - 1) + l - 1) * 2 + g + 1)
                        TT(B("X", g), bank[g, 0], mask(1 + l), mult).then_inc(dn_s["X"], 1)
                    for g in range(2):
                        dve.wait_ge(dn_s["up"], (c * (LEVELS - 1) + l - 1) * 2 + g + 1)
                        dve.wait_ge(dn_s["TT"], (c * LEVELS + l - 1) * 2 + g + 1)
                        TT(B("TT", g), B("TT", g), bank[g, 2], sub).then_inc(dn_s["TT"], 1)
                for g in range(2):
                    dve.wait_ge(dn_s["KS"], c * 2 + g + 1)
                    TT(B("X", g), bank[g, 1], cols(eg, g, c), mult).then_inc(dn_s["eKS"], 1)
                for g in range(2):
                    dve.wait_ge(dn_s["eKS"], c * 2 + g + 1)
                    dve.wait_ge(dn_s["V"], c * 2 + g + 1)
                    TT(B("V", g), B("V", g), B("X", g), sub).then_inc(dn_s["Rr"], 1)
                for g in range(2):
                    dve.wait_ge(dn_s["TR"], c * 2 + g + 1)
                    TT(B("X", g), bank[g, 0], cols(beta, g, c), mult).then_inc(dn_s["vn"], 1)
                for g in range(2):
                    dve.wait_ge(dn_s["o"], c * 2 + g + 1)
                    dve.wait_ge(dn_s["S"], c * 2 + g + 1)
                    TT(B("S", g), B("S", g), cols(gl, g, c), mult).then_inc(dn_s["Sg"], 1)
                for g in range(2):
                    dve.wait_ge(dn_s["Sg"], c * 2 + g + 1)
                    dve.wait_ge(dn_s["Kv"], c * 2 + g + 1)
                    TT(B("S", g), B("S", g), bank[g, 3], add).then_inc(dn_s["S"], 1)
            with dve.Fori(0, NC) as c:
                delta(c)
            for g in range(2):
                dve.wait_ge(dn_s["S"], 2 * NC + 2)
                dve.wait_ge(dn_s["oc"], 2 * NC)
                dve.sem_inc(dn_done, 1)

            first_split("g")

            def gate(i):
                for s in range(2):
                    m = i * 2 + s
                    split_lo("g", s, i, 4)
                    dve.wait_ge(acc_done[s], BASE["g"][s] + i + 1)
                    TT(sc[s][:, :], acc[s][:, :], rstd[:, :], mult).then_inc(g_s["gate"], 1)
                    dve.wait_ge(g_s["gate"], m + 1)
                    dve.sem_inc(acc_free[s], 1)
                    dve.wait_ge(g_s["inv"], m + 1)
                    TT(row(qo, m), row(qo, m), s2[:, :], mult).then_inc(g_s["norm"], 1)
                    dve.wait_ge(g_s["norm"], m + 1)
                    dve.wait_ge(g_s["silu"], m + 1)
                    STT(sc[s][:, :], row(qo, m), vecs[:, V_DN:V_DN + 1], sc[s][:, :], mult, mult).then_inc(g_s["prod"], 1)
                    dve.wait_ge(g_s["hi"], m + 1)
                    TT(row(ol, m), sc[s][:, :], row(oh, m).bitcast(f32), sub).then_inc(g_s["ready"], 1)
            loop(dve, 4, gate, first=True)
            dve.wait_ge(g_s["ready"], 8)

            def gaya(i):
                split_lo("gaya", 0, i, 8)
                dve.wait_ge(acc_done[0], BASE["gaya"][0] + i + 1)
                wait(dve, y_s["out"], i)
                TT(s0[:, :], acc[0][:, :], rstd[:, :], mult).then_inc(y_s["gate"], 1)
                dve.wait_ge(y_s["gate"], i + 1)
                dve.sem_inc(acc_free[0], 1)
                split_lo("gaya", 1, i, 8)
                dve.wait_ge(acc_done[1], BASE["gaya"][1] + i + 1)
                dve.wait_ge(y_s["sig"], i + 1)
                TT(row(merged_a, i), acc[1][:, :], s0[:, :], mult).then_inc(y_s["out"], 1)
                dve.wait_ge(y_s["out"], i + 1)
                dve.sem_inc(acc_free[1], 1)
            loop(dve, 8, gaya, first=True)

            def spatial_prep_a():
                dve.wait_ge(ws_in, 32)
                nc.vector.memset(wsT[CH:P, :, 0:CH], 0.0).then_inc(u_s["w"], 1)

            def spatial_prep_b():
                dve.wait_ge(u_s["rows"], 1)
                for m in range(DT):
                    STT(s2[:, m * P:m * P + P], aux[1][:, m * P:m * P + P], vecs[:, V_SB + m:V_SB + m + 1],
                        s2[:, m * P:m * P + P], mult, add).then_inc(u_s["bias"], 1)

            CH = 64
            def uv(i):
                for s in range(2):
                    k = i * 2 + s
                    split_lo("uv", s, i, 8)
                    dve.wait_ge(acc_done[s], BASE["uv"][s] + i + 1)
                    if isinstance(i, int) and i == 0:
                        pass
                    else:
                        dve.wait_ge(u_s["done"], k - 1)
                    TT(sc[s][:, :], acc[s][:, :], rstd[:, :], mult).then_inc(u_s["arg"], 1)
                    dve.wait_ge(u_s["arg"], k + 1)
                    dve.sem_inc(acc_free[s], 1)
                if isinstance(i, int) and i == 0:
                    spatial_prep_a()
                if isinstance(i, int) and i == 7:
                    spatial_prep_b()
            loop(dve, 8, uv, first=True)
            dve.wait_ge(u_s["bias"], 8)
            dve.wait_ge(u_s["done"], 16)
            dve.wait_ge(m_spilled, 16 * 8)

            def mix_out(n):
                at_n = slice(None), slice(None), ds(n * C, C)
                ch = Chain(dve, b_s_["chain"], n, 2)
                dve.wait_ge(b_s_["mix"], n + 1)
                ch.link(TT(gv[at_n], aux[1][:, :].rearrange("p (m t) -> p m t", m=DT),
                           bc_row(vecs[:, V_SW:V_SW + DT], DT), mult))
                ch.link(TT(gv[at_n], gv[at_n], s2[:, :].rearrange("p (m t) -> p m t", m=DT), add))
                TT(uu[at_n], gv[at_n], uu[at_n], mult).then_inc(b_s_["prod"], 1)
                dve.wait_ge(b_s_["hi"], n + 1)
                TT(sl[at_n], uu[at_n], sh[at_n].bitcast(f32), sub).then_inc(b_s_["ready"], 1)

            def gb(i):
                for s in range(2):
                    n = i * 2 + s
                    f0 = isinstance(i, int) and n == 0
                    split_lo("gb", s, i, 4)
                    dve.wait_ge(acc_done[s], BASE["gb"][s] + i + 1)
                    TT(row(sig_b, n), acc[s][:, :], rstd[:, :], mult).then_inc(b_s_["gate"], 1)
                    dve.wait_ge(b_s_["gate"], n + 1)
                    dve.sem_inc(acc_free[s], 1)
                    dve.wait_ge(b_s_["tr"], n + 1)
                    for b in range(2):
                        last = nc.vector.bn_stats(bnst[:, 6 * b:6 * b + 6], aux[0][:, HALF * b:HALF * b + HALF])
                    last.then_inc(b_s_["bn"], 1)
                    stand_alone(dve)
                    dve.wait_ge(b_s_["bn"], n + 1)
                    nc.vector.bn_aggr(st[:, 8:10], bnst[:, 0:12]).then_inc(b_s_["var"], 1)
                    dve.wait_ge(b_s_["root"], n + 1)
                    nc.vector.reciprocal(st[:, 10:11], st[:, 10:11]).then_inc(b_s_["inv"], 1)
                    dve.wait_ge(b_s_["inv"], n + 1)
                    dve.wait_ge(b_s_["var"], n + 1)
                    if not f0:
                        dve.wait_ge(b_s_["mix"], n)
                    TS(s1[:, :], aux[0][:, :], st[:, 8:9], st[:, 10:11], sub, mult).then_inc(b_s_["z"], 1)
                    if not f0:
                        mix_out(n - 1)
            loop(dve, 4, gb, first=True)
            mix_out(7)
            dve.wait_ge(b_s_["ready"], 8)

            def yb(i):
                for s in range(2):
                    n = i * 2 + s
                    split_lo("yb", s, i, 4)
                    dve.wait_ge(acc_done[s], BASE["yb"][s] + i + 1)
                    TT(row(sig_b, n), row(sig_b, n), acc[s][:, :], mult).then_inc(yb_s["t"], 1)
                    dve.wait_ge(yb_s["t"], n + 1)
                    dve.sem_inc(acc_free[s], 1)
                    dve.wait_ge(m_back[s], i * 16 + 16)
                    TT(sc[s][:, :], sc[s][:, :], row(sig_b, n), add).then_inc(yb_s["m"], 1)
                    dve.wait_ge(yb_s["hi"], n + 1)
                    TT(row(ml, n), sc[s][:, :], row(mh, n).bitcast(f32), sub).then_inc(yb_s["ready"], 1)
            loop(dve, 4, yb)
            dve.wait_ge(yb_s["ready"], 8)
            zero_sum(norms[2])

            def wo(i):
                for s in range(2):
                    m = i * 2 + s
                    split_lo("wo", s, i, 4)
                    dve.wait_ge(acc_done[s], BASE["wo"][s] + i + 1)
                    dve.wait_ge(h_back, 16 * DT)
                    TT(row(h2, m), row(h2, m), acc[s][:, :], add).then_inc(norms[2].h, 1)
                    dve.wait_ge(norms[2].h, norms[2].h_tile + m + 1)
                    dve.sem_inc(acc_free[s], 1)
                    statistics(norms[2], h2, m, V_N2, xh2, xl2)
            loop(dve, 4, wo, first=True)

            ffn(2, norms[2], norms[3], hh2, hl2, h2, 0, None, None)
            inverse(norms[3])
            dve.wait_ge(norms[3].rstd, norms[3].n + 1)
            for k in range(DT):
                STT(h2[:, k, :], h2[:, k, :], vecs[:, V_NF + k:V_NF + k + 1], rstd[:, :], mult, mult)\
                    .then_inc(norms[3].ready, 1)

        @block.tensor
        def _(pe):
            MM = nc.tensor.matmul

            def unit(name, s, i, xh, xl, kt=8, ready=None, mid=None):
                u = BASE[name][s] + i
                pe.wait_ge(w_ready[s], u + 1)
                wait(pe, acc_free[s], u)
                for b in range(2):
                    o = acc[s][:, HALF * b:HALF * b + HALF]
                    for k in range(kt):
                        if ready is not None and b == 0:
                            pe.wait_ge(ready[0], ready[1] + k + 1)
                        a, z = (t[:, k, HALF * b:HALF * b + HALF] for t in (xh, xl))
                        MM(o, w_hi[s][:, k, :], a, start=(k == 0), stop=False)
                        MM(o, w_hi[s][:, k, :], z, start=False, stop=False)
                        last = MM(o, w_lo[s][:, k, :], a, start=False, stop=(k == kt - 1))
                    if b == 0 and mid is not None:
                        mid()
                last.then_inc(acc_done[s], 1)

            def sums(nm):
                pe.wait_ge(nm.added, nm.tile + DT)
                for c in range(NC):
                    last = MM(aux[0][:, c:c + 1], s2[:, c * P:c * P + P], ones[:, 0:1], start=True, stop=True)
                last.then_inc(nm.sums, 1)

            def spread(nm):
                pe.wait_ge(nm.diag, nm.n + 1)
                for b in range(2):
                    last = MM(aux[0][:, HALF * b:HALF * b + HALF], ones[:, :], s2[:, HALF * b:HALF * b + HALF],
                              start=True, stop=True)
                last.then_inc(nm.bc, 1)

            def ffn(f, nm, hh, hl, xh, xl, n_ready):
                sg = ffns[f - 1]
                t0 = 0
                for g, n in enumerate(FF_GROUPS):
                    name = f"gu{f}_{g}"
                    def body(i):
                        f0 = g == 0 and isinstance(i, int) and i == 0
                        unit(name, 0, i, xh, xl, ready=(nm.ready, nm.tile) if f0 else None)
                        if f0:
                            sums(nm)
                        unit(name, 1, i, xh, xl, mid=(lambda: spread(nm)) if f0 else None)
                    loop(pe, n, body, first=(g == 0), last=False)
                    dname = f"down{f}_{g}"
                    def dbody(i):
                        for s in range(2):
                            f0 = isinstance(i, int) and s == 0
                            unit(dname, s, i, hh, hl, kt=n, ready=(sg.ready, t0) if f0 else None)
                    loop(pe, DT // 2, dbody, first=True, last=False)
                    t0 += n

            pe.wait_ge(setup, 7)
            pe.wait_ge(cst_in, 48)
            ffn(1, norms[0], hh1, hl1, xh1, xl1, None)

            def l2_sums(j):
                for b, t in enumerate((s1, s2)):
                    pe.wait_ge(sq_done, j * 2 + b + 1)
                    for hf in range(2):
                        last = MM(aux[b][:, HALF * hf:HALF * hf + HALF], ones[:, :], t[:, HALF * hf:HALF * hf + HALF],
                                  start=True, stop=True)
                    last.then_inc(l2_sum, 1)

            def qk(i):
                f0 = isinstance(i, int) and i == 0
                unit("qk", 0, i, xhm, xlm, ready=(norms[1].ready, norms[1].tile) if f0 else None)
                if f0:
                    sums(norms[1])
                else:
                    l2_sums(i - 1)
                unit("qk", 1, i, xhm, xlm, mid=(lambda: spread(norms[1])) if f0 else None)
            loop(pe, HEADS, qk, first=True, last=False)
            unit("ab", 0, 0, xhm, xlm)
            l2_sums(HEADS - 1)

            def v(i):
                f0 = isinstance(i, int)
                unit("v", 0, i, xhm, xlm)
                if f0:
                    pe.wait_ge(ab["dve"], 3)
                    pe.wait_ge(l2_ln, 2 * HEADS)
                    for c in range(NC):
                        last = nc.tensor.transpose(aux[0][:, 64 * c:64 * c + 64], s1[0:64, c * P:c * P + P],
                                                   ident[0:64, 0:64])
                    last.then_inc(ab["t"], 1)
                unit("v", 1, i, xhm, xlm)
                if f0:
                    pe.wait_ge(ab["cols"], 2)
                    MM(aux[1][:, 0:64], upper[:, :], la[:, :], start=True, stop=True)
                    MM(aux[1][:, 64:128], ones[:, :], la[:, :], start=True, stop=True).then_inc(ab["g"], 1)
            loop(pe, 4, v, first=True, last=False)

            pe.wait_ge(ab["gact"], 3)
            pe.wait_ge(ab["gv"], 2)
            for s in range(2):
                pe.wait_ge(acc_free[s], BASE["g"][s])

            def delta(c):
                B = lambda n, g: dn[n, g]
                for g in range(2):
                    pe.wait_ge(dn_s["laU"], c * 2 + g + 1)
                    MM(bank[g, 0], ones[:, :], B("X", g)[:, :, :], start=True, stop=True).then_inc(dn_s["G"], 1)
                for g in range(2):
                    pe.wait_ge(dn_s["kTs"], c * 2 + g + 1)
                    for h in range(HG):
                        last = nc.tensor.transpose(bank[g, 3][:, h, :], B("kTs", g)[:, h, :], ident[:, :])
                    last.then_inc(dn_s["tk"], 1)
                for g in range(2):
                    for h in range(HG):
                        last = MM(bank[g, 1][:, h, :], B("kTs", g)[:, h, :], B("kTs", g)[:, h, :], start=True, stop=True)
                    last.then_inc(dn_s["kk"], 1)
                for g in range(2):
                    for h in range(HG):
                        last = MM(bank[g, 2][:, h, :], B("kTs", g)[:, h, :], qo[:, HG * g + h, ds(c * C, C)],
                                  start=True, stop=True)
                    last.then_inc(dn_s["qk"], 1)
                for g in range(2):
                    pe.wait_ge(dn_s["vTs"], c * 2 + g + 1)
                    pe.wait_ge(dn_s["Kd"], c * 2 + g + 1)
                    for h in range(HG):
                        last = nc.tensor.transpose(bank[g, 3][:, h, :], B("T", g)[:, h, :], ident[:, :])
                    last.then_inc(dn_s["tv"], 1)
                for l in range(1, LEVELS):
                    for g in range(2):
                        pe.wait_ge(dn_s["TT"], (c * LEVELS + l - 1) * 2 + g + 1)
                        for h in range(HG):
                            last = nc.tensor.transpose(bank[g, 1][:, h, :], B("TT", g)[:, h, :], ident[:, :])
                        last.then_inc(dn_s["tT"], 1)
                    for g in range(2):
                        pe.wait_ge(dn_s["T"], (c * (LEVELS - 1) + l - 1) * 2 + g + 1)
                        for h in range(HG):
                            last = MM(bank[g, 0][:, h, :], B("NT", g)[:, h, :], B("T", g)[:, h, :], start=True, stop=True)
                        last.then_inc(dn_s["xp"], 1)
                    for g in range(2):
                        pe.wait_ge(dn_s["X"], (c * (LEVELS - 1) + l - 1) * 2 + g + 1)
                        if l == 1:
                            pe.wait_ge(dn_s["AT"], c * 2 + g + 1)
                        for h in range(HG):
                            last = MM(bank[g, 2][:, h, :], B("X", g)[:, h, :], B("TT", g)[:, h, :], start=True, stop=True)
                        last.then_inc(dn_s["up"], 1)
                for g in range(2):
                    pe.wait_ge(dn_s["S"], c * 2 + g + 1)
                    for h in range(HG):
                        last = MM(bank[g, 1][:, h, :], B("kTs", g)[:, h, :], B("S", g)[:, h, :], start=True, stop=True)
                    last.then_inc(dn_s["KS"], 1)
                for g in range(2):
                    pe.wait_ge(dn_s["Rr"], c * 2 + g + 1)
                    pe.wait_ge(dn_s["TT"], (c * LEVELS + LEVELS - 1) * 2 + g + 1)
                    for h in range(HG):
                        last = MM(bank[g, 0][:, h, :], B("TT", g)[:, h, :], B("V", g)[:, h, :], start=True, stop=True)
                    last.then_inc(dn_s["TR"], 1)
                for g in range(2):
                    pe.wait_ge(dn_s["qd"], c * 2 + g + 1)
                    pe.wait_ge(dn_s["vn"], c * 2 + g + 1)
                    for h in range(HG):
                        MM(bank[g, 2][:, h, :], B("S", g)[:, h, :], qo[:, HG * g + h, ds(c * C, C)], start=True, stop=False)
                        last = MM(bank[g, 2][:, h, :], B("X", g)[:, h, :], B("AT", g)[:, h, :], start=False, stop=True)
                    last.then_inc(dn_s["o"], 1)
                for g in range(2):
                    pe.wait_ge(dn_s["V"], c * 2 + g + 1)
                    for h in range(HG):
                        last = MM(bank[g, 3][:, h, :], B("Ktm", g)[:, h, :], B("X", g)[:, h, :], start=True, stop=True)
                    last.then_inc(dn_s["Kv"], 1)
            with pe.Fori(0, NC) as c:
                delta(c)
            pe.wait_ge(dn_done, 2)

            def gate(i):
                for s in range(2):
                    m = i * 2 + s
                    unit("g", s, i, xhm, xlm)
                    pe.wait_ge(g_s["sq"], m + 1)
                    for hf in range(2):
                        last = MM(aux[0][:, HALF * hf:HALF * hf + HALF], ones[:, :], s2[:, HALF * hf:HALF * hf + HALF],
                                  start=True, stop=True)
                    last.then_inc(g_s["sum"], 1)
            loop(pe, 4, gate, last=False)

            def gaya(i):
                f0 = isinstance(i, int)
                unit("gaya", 0, i, xhm, xlm)
                unit("gaya", 1, i, oh, ol, ready=(g_s["ready"], 0) if f0 else None)
            loop(pe, 8, gaya, first=True, last=False)

            def uv(i):
                unit("uv", 0, i, xhm, xlm)
                unit("uv", 1, i, xhm, xlm)
                if isinstance(i, int) and i == 6:
                    pe.wait_ge(u_s["w"], 1)
                    ws = wsT[:, :, :].rearrange("p m t -> p (m t)")
                    for hf in range(2):
                        last = MM(aux[1][:, HALF * hf:HALF * hf + HALF], ones[:, :], ws[:, HALF * hf:HALF * hf + HALF],
                                  start=True, stop=True)
                    last.then_inc(u_s["rows"], 1)
            loop(pe, 7, uv)
            uv(7)

            def mix(n):
                pe.wait_ge(b_s_["z"], n + 1)
                if isinstance(n, int) and n == 0:
                    pe.wait_ge(u_s["bias"], 8)
                else:
                    pe.wait_ge(b_s_["prod"], n)
                for m in range(DT):
                    last = MM(aux[1][:, m * P:m * P + P], s1[:, m * P:m * P + P], wsT[:, m, :], start=True, stop=True)
                last.then_inc(b_s_["mix"], 1)

            def gb(i):
                for s in range(2):
                    n = i * 2 + s
                    unit("gb", s, i, xhm, xlm)
                    pe.wait_ge(b_s_["copy"], n + 1)
                    if not (isinstance(i, int) and n == 0):
                        pe.wait_ge(b_s_["z"], n)
                    for m in range(DT):
                        last = nc.tensor.transpose(aux[0][:, m * P:m * P + P], s0[:, m * P:m * P + P], ident[:, :])
                    last.then_inc(b_s_["tr"], 1)
                    if not (isinstance(i, int) and n == 0):
                        mix(n - 1)
            loop(pe, 4, gb, first=True, last=False)
            mix(7)

            def yb(i):
                for s in range(2):
                    if isinstance(i, int) and s == 0:
                        pe.wait_ge(b_s_["ready"], 8)
                    unit("yb", s, i, sh, sl)
            loop(pe, 4, yb, first=True, last=False)

            def wo(i):
                for s in range(2):
                    unit("wo", s, i, mh, ml, ready=(yb_s["ready"], 0) if isinstance(i, int) and s == 0 else None)
            loop(pe, 4, wo, first=True, last=False)

            ffn(2, norms[2], hh2, hl2, xh2, xl2, None)
            sums(norms[3])
            spread(norms[3])


def _level_masks():
    i = np.arange(P)
    later = (i[None, :] >= i[:, None]).astype(np.float32)
    bound = np.where(later > 0, 0.0, -1e30).astype(np.float32)
    def level(l):
        b, o = i >> (l + 1), (i >> l) & 1
        return ((b[:, None] == b[None, :]) & (o[:, None] == 1) & (o[None, :] == 0)).astype(np.float32)
    parts = [np.eye(P, dtype=np.float32), later, bound, level(0).T] + [level(l) for l in range(1, LEVELS)]
    return np.ascontiguousarray(np.stack(parts, axis=1))


def _tiles(w):
    k, n = w.shape
    return np.ascontiguousarray(w.reshape(k // P, P, n // P, P).transpose(2, 1, 0, 3))


def kernel(**inputs):
    import concourse.bacc as bacc
    from concourse.bass_utils import run_bass_kernel_spmd

    a = {k: np.asarray(v) for k, v in inputs.items()}
    col = lambda v: v.reshape(-1, P).T
    vec = np.zeros((P, V_ALL), np.float32)
    for at, name in ((V_N1, "ffn1_norm_w"), (V_NM, "mix_norm_w"), (V_N2, "ffn2_norm_w"), (V_SW, "sgu_norm_w"),
                     (V_SB, "sgu_norm_b")):
        vec[:, at:at + DT] = col(a[name][0])
    vec[:, V_NF:V_NF + DT] = col(a["final_norm_w"])
    vec[:, V_DN] = a["dn_out_norm_w"][0]
    vec[LANE_A:LANE_A + HEADS, V_DT] = a["dn_dt_bias"][0]
    vec[LANE_A:LANE_A + HEADS, V_AL] = a["dn_a_log"][0]
    vec[:, V_CW:] = a["dn_conv_w"][0].reshape(TAPS, 3 * HEADS, P).transpose(2, 1, 0).reshape(P, -1)
    w_in = a["w_in"][0]
    nb = 4 * D
    w_ba = np.zeros((D, P), np.float32)
    w_ba[:, 0:HEADS] = w_in[:, nb:nb + HEADS]
    w_ba[:, LANE_A:LANE_A + HEADS] = w_in[:, nb + HEADS:nb + 2 * HEADS]
    arrays = {
        "x": np.ascontiguousarray(a["x"][0].T).reshape(DT, P, SEQ),
        "vec": vec, "cst": _level_masks(),
        "w_gate1": _tiles(a["ffn1_w_gate"][0]), "w_up1": _tiles(a["ffn1_w_up"][0]),
        "w_down1": _tiles(a["ffn1_w_down"][0]),
        "w_in": _tiles(np.concatenate([w_in[:, :nb], w_in[:, nb + 2 * HEADS:]], axis=1)),
        "w_ba": _tiles(w_ba), "w_ya": _tiles(a["dn_w_o"][0]), "w_yb": _tiles(a["gmlp_w_o"][0]),
        "w_out": _tiles(a["w_out"][0]),
        "w_s": np.ascontiguousarray(a["sgu_w_s"][0].transpose(2, 0, 1)),
        "b_s": np.ascontiguousarray(np.broadcast_to(a["sgu_b"][0].reshape(1, -1), (P, D))),
        "w_gate2": _tiles(a["ffn2_w_gate"][0]), "w_up2": _tiles(a["ffn2_w_up"][0]),
        "w_down2": _tiles(a["ffn2_w_down"][0]),
    }
    nc = bacc.Bacc("TRN2", target_bir_lowering=False, num_devices=1)
    f32 = mybir.dt.float32
    aps = [nc.dram_tensor(f"in_{k}", v.shape, f32, kind="ExternalInput").ap() for k, v in arrays.items()]
    h_spill = nc.dram_tensor("h_spill", (DT, P, SEQ), f32, kind="Internal").ap()
    m_spill = nc.dram_tensor("m_spill", (DT, P, SEQ), f32, kind="Internal").ap()
    out = nc.dram_tensor("out", (DT, P, SEQ), f32, kind="ExternalOutput").ap()
    build(nc, *aps, h_spill, m_spill, out)
    r = run_bass_kernel_spmd(nc, [{f"in_{k}": v for k, v in arrays.items()}], core_ids=[0])
    y = np.asarray(r.results[0]["out"]).reshape(D, SEQ)
    return np.ascontiguousarray(y.T).reshape(1, SEQ, D)
```

```python
import concourse.bass as bass
import numpy as np
from concourse import mybir
from contextlib import ExitStack

P = 128
SEQ = 1024
HALF = 512
D = 1024
DT = D // P
FF = 2816
FT = FF // P
FF_GROUPS = (8, 8, 6)
HEADS = 8
TAPS = 4
C = 128
NC = SEQ // C
HG = 4
LEVELS = 7
LANE_A = 32
RMS_EPS, LN_EPS, L2_EPS = 1e-6, 1e-5, 1e-6

PHASES = []
for _f in (1,):
    for _g, _n in enumerate(FF_GROUPS):
        PHASES += [(f"gu1_{_g}", _n, _n), (f"down1_{_g}", DT // 2, DT // 2)]
PHASES += [("qk", HEADS, HEADS), ("ab", 1, 0), ("v", HEADS // 2, HEADS // 2), ("uv", DT, DT),
           ("g", HEADS // 2, HEADS // 2), ("gaya", DT, DT), ("gb", DT // 2, DT // 2), ("yb", DT // 2, DT // 2),
           ("wo", DT // 2, DT // 2)]
for _g, _n in enumerate(FF_GROUPS):
    PHASES += [(f"gu2_{_g}", _n, _n), (f"down2_{_g}", DT // 2, DT // 2)]
BASE, _a, _b = {}, 0, 0
for _name, _na, _nb in PHASES:
    BASE[_name] = (_a, _b)
    _a, _b = _a + _na, _b + _nb
UNITS = (_a, _b)

V_N1, V_NM, V_N2, V_NF, V_SW, V_SB, V_DN, V_DT, V_AL, V_CW = 0, 8, 16, 24, 32, 40, 48, 49, 50, 51
V_ALL = V_CW + 3 * HEADS * TAPS


B32 = 32


def build(nc, x, vec, cst, w_gate1, w_up1, w_down1, w_in, w_ba, w_ya, w_yb, w_out, w_s, b_s,
          w_gate2, w_up2, w_down2, h_spill, m_spill, q_spill, k_spill, v_spill, u_spill, o_spill, out):
    f32, f32r = mybir.dt.float32, mybir.dt.float32r
    ALU, ACT = mybir.AluOpType, mybir.ActivationFunctionType
    ds = bass.ds

    ctx = ExitStack()
    with ctx:
        KB = 1024
        start = (nc.sbuf_base + 63) // 64 * 64
        R = [start + 32 * KB * n for n in range(5)]
        W0 = start + 160 * KB
        S0 = W0 + 24 * KB
        S1 = S0 + 4128
        S2 = S1 + 4 * KB
        RS = S2 + 4 * KB
        DC = RS + 4 * KB
        SM = DC + 4 * KB

        def at(name, shape, dt, off):
            return nc.alloc_sbuf_tensor_at(name, shape, dt, offset=off)

        def big(name, dt, r):
            return at(name, [P, DT, SEQ], dt, R[r])

        h1 = big("h1", f32, 0)
        xh1, xl1 = big("xh1", f32r, 3), big("xl1", f32r, 4)
        hh1, hl1 = big("hh1", f32r, 1), big("hl1", f32r, 2)
        qo, kk_, vv_ = big("qo", f32, 0), big("kfeat", f32, 1), big("vfeat", f32, 2)
        xhm, xlm = big("xhm", f32r, 3), big("xlm", f32r, 4)
        oo = big("oo", f32, 0)
        oh, ol = big("oh", f32r, 1), big("ol", f32r, 0)
        gv, uu = big("gv", f32, 2), big("uu", f32, 1)
        sh, sl = big("sh", f32r, 2), big("sl", f32r, 1)
        sig_b = big("sig_b", f32, 0)
        mh, ml = big("mh", f32r, 3), big("ml", f32r, 4)
        h2 = big("h2", f32, 0)
        xh2, xl2 = big("xh2", f32r, 1), big("xl2", f32r, 2)
        hh2, hl2 = big("hh2", f32r, 3), big("hl2", f32r, 4)
        w_raw = [at(f"w_raw{s}", [P, 8, P], f32, W0 + 4 * KB * s) for s in range(2)]
        w_hi = [at(f"w_hi{s}", [P, 8, P], f32r, W0 + 8 * KB + 4 * KB * s) for s in range(2)]
        w_lo = [at(f"w_lo{s}", [P, 8, P], f32r, W0 + 16 * KB + 4 * KB * s) for s in range(2)]
        s0p = at("s0p", [P, SEQ + 8], f32, S0)
        s0, s1, s2 = (at(n, [P, SEQ], f32, o) for n, o in (("s0", S0), ("s1", S1), ("s2", S2)))
        sc = [s0, s1]
        rstd = at("rstd", [P, SEQ], f32, RS)
        wsT = at("wsT", [P, 8, P], f32, DC)
        o_ = SM
        def small(name, shape):
            nonlocal o_
            n = int(np.prod(shape[1:])) * 4
            t = at(name, shape, f32, o_)
            o_ += (n + 31) // 32 * 32
            return t
        vecs = small("vecs", [P, V_ALL])
        ident = small("ident", [P, P])
        upper = small("upper", [P, P])
        ones = small("ones", [P, P])
        beta, gcol, eg, kd, gl = (small(n, [P, NC * HEADS]) for n in ("beta", "gcol", "eg", "kd", "gl"))
        la = small("la", [P, (NC + 1) * HEADS])
        st = small("st", [P, 16])
        bnst = small("bnst", [P, 16])
        consts = small("consts", [P, 8])
        assert o_ <= nc.sbuf_usable_end

        dn_at = R[0]
        def dn_tile(name, shape):
            nonlocal dn_at
            t = at(name, shape, f32, dn_at)
            dn_at += int(np.prod(shape[1:])) * 4
            return t
        qc, kc, vc, ost = (dn_tile(n, [P, HEADS, C]) for n in ("qc", "kc", "vc", "ost"))
        dn = {(n, g): dn_tile(f"dn_{n}{g}", [P, HG, w]) for g in range(2) for n, w in (
            ("S", P), ("Ktm", P), ("V", P), ("AT", P), ("NT", P), ("TT", P), ("X", P), ("D", P), ("LU", P),
            ("TTc", B32), ("Tc", B32), ("Xc", B32), ("Tf", 2 * B32), ("X6", 2 * B32))}
        bound = dn_tile("bound", [P, P])
        blocks = dn_tile("blocks", [P, 6, B32])
        assert dn_at <= R[2]

        acc = [ctx.enter_context(nc.psum_tensor(f"acc{s}", [P, SEQ], f32)) for s in range(2)]
        aux = [ctx.enter_context(nc.psum_tensor(f"aux{s}", [P, SEQ], f32)) for s in range(2)]
        bank = {(g, n): aux[g][:, HALF * n:HALF * n + HALF].rearrange("p (h i) -> p h i", h=HG)
                for g in range(2) for n in range(2)}
        bankc = {k: v.rearrange("p h i -> p (h i)")[:, 0:HG * B32].rearrange("p (h i) -> p h i", h=HG)
                 for k, v in bank.items()}
        bank64 = {k: v.rearrange("p h i -> p (h i)")[:, 0:HG * 2 * B32].rearrange("p (h i) -> p h i", h=HG)
                  for k, v in bank.items()}
        bankt = {k: v.rearrange("p h i -> p (h i)")[:, HALF // 2:HALF // 2 + HG * B32]
                 .rearrange("p (h i) -> p h i", h=HG) for k, v in bank.items()}
        quad = [slice(B32 * b, B32 * b + B32) for b in range(P // B32)]

        def sem(name):
            return ctx.enter_context(nc.semaphore(name))

        w_loaded = [sem(f"w_loaded{s}") for s in range(2)]
        w_hi_done = [sem(f"w_hi_done{s}") for s in range(2)]
        w_ready = [sem(f"w_ready{s}") for s in range(2)]
        acc_done = [sem(f"acc_done{s}") for s in range(2)]
        acc_free = [sem(f"acc_free{s}") for s in range(2)]
        cst_in, x_in = sem("cst_in"), [sem(f"x_in{k}") for k in range(DT // 2)]
        spilled, h_back, m_spilled, m_back = sem("spilled"), sem("h_back"), sem("m_spilled"), [sem(f"m_back{s}") for s in range(2)]
        ws_in, bs_in = sem("ws_in"), sem("bs_in")
        q_out, k_out, v_out, masks_in = sem("q_out"), sem("k_out"), sem("v_out"), sem("masks_in")
        q_in, k_in, v_in = sem("q_in"), sem("k_in"), sem("v_in")
        u_out, o_out, u_freed, o_freed = sem("u_out"), sem("o_out"), sem("u_freed"), sem("o_freed")
        o_back, u_back = [sem(f"o_back{n}") for n in range(2)], [sem(f"u_back{n}") for n in range(2)]
        setup = sem("setup")
        out_sem = sem("out_sem")

        class Chain:
            def __init__(self, eng, s, i, per):
                self.eng, self.s, self.i, self.per, self.k = eng, s, i, per, 0
            def link(self, ins):
                self.k += 1
                ins.then_inc(self.s, 1)
                self.eng.wait_ge(self.s, self.i * self.per + self.k)
            def end(self):
                assert self.k == self.per, (self.k, self.per)

        norm_sems = {n: sem(f"norm_{n}") for n in (
            "xt",
            "hi",
            "ready",
            "h",
            "sq",
            "added",
            "sums",
            "root",
            "inv",
            "diag",
            "bc",
            "rstd",
            "zero",
        )}

        class Norm:
            def __init__(self, n):
                self.n, self.tile, self.h_tile = n, DT * n, DT * (n - 1)
                self.xt = norm_sems["xt"]
                self.hi = norm_sems["hi"]
                self.ready = norm_sems["ready"]
                self.h = norm_sems["h"]
                self.sq = norm_sems["sq"]
                self.added = norm_sems["added"]
                self.sums = norm_sems["sums"]
                self.root = norm_sems["root"]
                self.inv = norm_sems["inv"]
                self.diag = norm_sems["diag"]
                self.bc = norm_sems["bc"]
                self.rstd = norm_sems["rstd"]
                self.zero = norm_sems["zero"]
        norms = [Norm(n) for n in range(4)]

        ffn_sems = {n: sem(f"ffn_{n}") for n in (
            "gate",
            "silu",
            "prod",
            "hi",
            "ready",
        )}

        class Ffn:
            def __init__(self, f):
                self.tile = FT * (f - 1)
                self.gate, self.silu, self.prod, self.hi, self.ready = ffn_sems.values()
        ffns = [Ffn(1), Ffn(2)]

        s_conv_a, s_conv = sem("conv_chain_a"), sem("conv_chain_b")
        conv_done, silu_done, sq_done = sem("conv_done"), sem("silu_done"), sem("sq_done")
        l2_sum, l2_ln, l2_inv, l2_used = sem("l2_sum"), sem("l2_ln"), sem("l2_inv"), sem("l2_used")
        v_chain, v_conv, v_done = sem("v_chain"), sem("v_conv"), sem("v_done")
        ab = {n: sem(f"ab_{n}") for n in ("z", "act", "dve", "t", "cols", "g", "gv", "gact")}
        g_s = {n: sem(f"g_{n}") for n in ("sq", "sum", "ln", "inv", "gate", "silu", "norm", "prod", "hi", "ready")}
        y_s = {n: sem(f"y_{n}") for n in ("gate", "sig", "out")}
        u_s = {n: sem(f"u_{n}") for n in ("arg0", "arg1", "done0", "done1", "bias", "w", "rows")}
        b_s_ = {n: sem(f"b_{n}") for n in ("gate", "sig", "copy", "tr", "bn", "var", "root", "inv", "z", "mix",
                                           "chain", "prod", "hi", "ready")}
        yb_s = {n: sem(f"yb_{n}") for n in ("t", "m", "hi", "ready")}

        def wait(eng, s, v):
            if not isinstance(v, int) or v > 0:
                eng.wait_ge(s, v)

        def stand_alone(eng):
            eng.wait_ge(setup, 7)

        carrier = sem("carrier")

        def carry(eng):
            eng.sem_inc(carrier, 1)

        def loop(eng, n, body, first=False, last=True):
            lo, hi = int(first), n - int(last)
            if first:
                body(0)
            if hi - lo == 1:
                body(lo)
            elif hi > lo:
                with eng.Fori(lo, hi) as i:
                    body(i)
            if last and hi >= lo:
                body(n - 1)

        def is_last(i, n):
            return isinstance(i, int) and i == n - 1

        def bc_row(t, n):
            return t.unsqueeze(2).to_broadcast([P, n, P])

        def bc_mid(t, n):
            return t.unsqueeze(1).to_broadcast([P, n, P])

        def kt_next(name, s, i, n):
            if is_last(i, n):
                if name == f"down2_{len(FF_GROUPS) - 1}":
                    return 0
                if name.startswith("gu"):
                    return FF_GROUPS[int(name[-1])]
                return 8
            return FF_GROUPS[int(name[-1])] if name.startswith("down") else 8

        dn_s = {n: sem(f"dn_{n}") for n in (
            "laU", "G", "EG", "argA", "arg", "D", "kk", "qk", "qd", "tk", "tv", "NTa", "NT", "AT", "V", "KS",
            "eKS", "Rr", "L0", "TT", "T", "xp", "X", "up", "x5", "X5", "u5", "T5", "x6", "X6", "u6", "T6",
            "TR", "vn", "o", "oc", "Kd", "Kv", "Sg", "S")}
        dn_done = sem("dn_done")

        block = ctx.enter_context(nc.Block())

        @block.sync
        def _(sp):
            for k in range(DT):
                sp.dma_start(h1[:, k, :], x[k]).then_inc(x_in[k // 2], 16)

            def load(name, s, i, n, src, kt):
                u = BASE[name][s] + i
                wait(sp, w_ready[s], u)
                sp.dma_start(w_raw[s][:, 0:kt, :], src).then_inc(w_loaded[s], 16)

            def pick(w, t):
                return w[ds(t, 1)].rearrange("a p k m -> p (a k) m") if not isinstance(t, int) else w[t]

            def two(name, n, a, b, kt=8, first=False):
                def body(i):
                    load(name, 0, i, n, a(i), kt)
                    load(name, 1, i, n, b(i), kt)
                loop(sp, n, body, first=first, last=False)

            def ffn_loads(f, wg, wu, wd):
                t0 = 0
                for g, n in enumerate(FF_GROUPS):
                    two(f"gu{f}_{g}", n, lambda i: pick(wg, i + t0), lambda i: pick(wu, i + t0), first=(g == 0))
                    def down(m):
                        return wd[ds(m, 1), :, t0:t0 + n, :].rearrange("a p k m -> p (a k) m")
                    two(f"down{f}_{g}", DT // 2, lambda i: down(i * 2), lambda i: down(i * 2 + 1), kt=n)
                    t0 += n

            ffn_loads(1, w_gate1, w_up1, w_down1)
            two("qk", HEADS, lambda i: pick(w_in, i), lambda i: pick(w_in, i + 8))
            load("ab", 0, 0, 1, w_ba[0], 8)
            two("v", 4, lambda i: pick(w_in, i * 2 + 16), lambda i: pick(w_in, i * 2 + 17))
            two("uv", 8, lambda i: pick(w_in, i + 32), lambda i: pick(w_in, i + 40))
            two("g", 4, lambda i: pick(w_in, i * 2 + 24), lambda i: pick(w_in, i * 2 + 25))
            two("gaya", 8, lambda i: pick(w_in, i + 48), lambda i: pick(w_ya, i))
            two("gb", 4, lambda i: pick(w_in, i * 2 + 56), lambda i: pick(w_in, i * 2 + 57))
            two("yb", 4, lambda i: pick(w_yb, i * 2), lambda i: pick(w_yb, i * 2 + 1))
            two("wo", 4, lambda i: pick(w_out, i * 2), lambda i: pick(w_out, i * 2 + 1))
            ffn_loads(2, w_gate2, w_up2, w_down2)
            sp.wait_ge(out_sem, 16 * DT)

        @block.gpsimd
        def _(pool):
            nc.gpsimd.memset(ones[:, :], 1.0).then_inc(setup, 1)
            for n, v in enumerate((RMS_EPS, LN_EPS, L2_EPS, -0.5 * float(np.log(P)), 1.0, 0.0)):
                nc.gpsimd.memset(consts[:, n:n + 1], v).then_inc(setup, 1)
            pool.dma_start(vecs[:, :], vec).then_inc(cst_in, 16)
            pool.dma_start(ident[:, :], cst[:, 0, :]).then_inc(cst_in, 16)
            pool.dma_start(upper[:, :], cst[:, 1, :]).then_inc(cst_in, 16)
            pool.dma_start(wsT[:, :, :], w_s).then_inc(ws_in, 16)

            def spill(i):
                for b in range(2):
                    pool.wait_ge(norms[1].h, norms[1].h_tile + i * 2 + b + 1)
                    pool.dma_start(h_spill[ds(i * 2 + b, 1)].rearrange("a p t -> p (a t)"),
                                   h1[:, ds(i * 2 + b, 1), :].rearrange("p a t -> p (a t)")).then_inc(spilled, 16)
            loop(pool, 4, spill, last=False)

            def rows(t, m):
                return t[:, ds(m, 1), :].rearrange("p a t -> p (a t)")

            def dram(t, m):
                return t[ds(m, 1)].rearrange("a p t -> p (a t)")

            def qk_out(i):
                pool.wait_ge(l2_used, i * 2 + 3)
                pool.dma_start(dram(q_spill, i), rows(qo, i)).then_inc(q_out, 16)
                pool.wait_ge(l2_used, i * 2 + 4)
                pool.dma_start(dram(k_spill, i), rows(kk_, i)).then_inc(k_out, 16)
            loop(pool, HEADS, qk_out, last=False)
            pool.wait_ge(q_out, 16 * HEADS)
            pool.wait_ge(k_out, 16 * HEADS)
            pool.dma_start(bound[:, :], cst[:, 2, :]).then_inc(masks_in, 16)
            pool.dma_start(blocks[:, :, :].rearrange("p l i -> p (l i)"),
                           cst[:, 3:5, :].rearrange("p a i -> p (a i)")[:, 0:6 * B32]).then_inc(masks_in, 16)

            def v_out_(n):
                pool.wait_ge(v_done, n + 1)
                pool.dma_start(dram(v_spill, n), rows(vv_, n)).then_inc(v_out, 16)
            loop(pool, HEADS, v_out_, last=False)

            def chunk_in(c):
                pos = slice(None), slice(None), ds(c * C, C)
                for t, spilled_, here in ((kc, k_spill, k_in), (qc, q_spill, q_in), (vc, v_spill, v_in)):
                    pool.dma_start(t[:, :, :], spilled_[pos].rearrange("h p t -> p h t")).then_inc(here, 16)
            pool.wait_ge(v_out, 16 * HEADS)
            chunk_in(0)
            pool.sem_inc(u_freed, 1)
            pool.sem_inc(o_freed, 1)

            def delta_dmas(c, more=True):
                if more:
                    pool.wait_ge(dn_s["KS"], c * 2 + 2)
                    pool.wait_ge(dn_s["qd"], c * 2 + 2)
                    pool.wait_ge(dn_s["tv"], c * 2 + 2)
                    chunk_in(c + 1)
                pool.wait_ge(dn_s["oc"], c * 2 + 4)
                pool.dma_start(o_spill[:, :, ds(c * C, C)].rearrange("h p t -> p h t"), ost[:, :, :]).then_inc(o_out, 16)
                pool.wait_ge(o_out, c * 16 + 16)
                pool.sem_inc(o_freed, 1)
                pool.wait_ge(u_s["done0"], c + 1)
                pool.dma_start(dram(u_spill, c), s0[:, :]).then_inc(u_out, 16)
                pool.wait_ge(u_out, c * 16 + 16)
                pool.sem_inc(u_freed, 1)
            with pool.Fori(0, NC - 1) as c:
                delta_dmas(c)
            delta_dmas(NC - 1, more=False)

            pool.wait_ge(dn_done, 1)
            pool.wait_ge(o_out, 16 * NC)
            for h in range(HEADS):
                pool.dma_start(oo[:, h, :], o_spill[h]).then_inc(o_back[int(h >= 2)], 16)

            pool.wait_ge(g_s["norm"], HEADS)
            pool.dma_start(s2[:, :], b_s).then_inc(bs_in, 16)

            def spill_m(i):
                pool.wait_ge(y_s["out"], i + 1)
                pool.dma_start(dram(m_spill, i), s1[:, :]).then_inc(m_spilled, 16)
            loop(pool, 8, spill_m, last=False)
            pool.wait_ge(acc_done[1], BASE["gb"][1])
            for b in range(2):
                pool.dma_start(uu[:, :, HALF * b:HALF * b + HALF],
                               u_spill[:, :, HALF * b:HALF * b + HALF].rearrange("h p t -> p h t")).then_inc(u_back[b], 16)
            pool.wait_ge(m_spilled, 16 * 8)
            pool.wait_ge(b_s_["ready"], 8)

            def back_m(i):
                for b in range(2):
                    if not isinstance(i, int):
                        pool.wait_ge(yb_s["ready"], i * 2 + b - 1)
                    pool.dma_start(sc[b][:, :], m_spill[ds(i * 2 + b, 1)].rearrange("a p t -> p (a t)"))\
                        .then_inc(m_back[b], 16)
            loop(pool, 4, back_m, first=True, last=False)

            def back_h(m):
                pool.wait_ge(yb_s["m"], m + 1)
                pool.dma_start(h2[:, ds(m, 1), :].rearrange("p a t -> p (a t)"),
                               h_spill[ds(m, 1)].rearrange("a p t -> p (a t)")).then_inc(h_back, 16)
            pool.wait_ge(spilled, 16 * DT)
            loop(pool, 8, back_h, last=False)

        @block.scalar
        def _(act):
            A = nc.scalar.activation

            def split_hi(name, s, i, n):
                kt = kt_next(name, s, i, n)
                if kt:
                    u = BASE[name][s] + i
                    act.wait_ge(acc_done[s], u + 1)
                    act.wait_ge(w_loaded[s], (u + 2) * 16)
                    A(w_hi[s][:, 0:kt, :], w_raw[s][:, 0:kt, :], ACT.Copy).then_inc(w_hi_done[s], 1)

            def first_split(name):
                for s in range(2):
                    u = BASE[name][s]
                    act.wait_ge(w_loaded[s], 16 * (u + 1))
                    A(w_hi[s][:, :, :], w_raw[s][:, :, :], ACT.Copy).then_inc(w_hi_done[s], 1)

            def square_and_hi(nm, h, m, xh, x_only=False):
                stand_alone(act)
                act.wait_ge(nm.h, nm.h_tile + m + 1)
                wait(act, nm.added, nm.tile + m)
                A(s1[:, :], h[:, ds(m, 1), :].rearrange("p a t -> p (a t)"), ACT.Square).then_inc(nm.sq, 1)
                if xh is not None:
                    stand_alone(act)
                    act.wait_ge(nm.xt, nm.tile + m + 1)
                    A(xh[:, ds(m, 1), :].rearrange("p a t -> p (a t)"), s0[:, :], ACT.Copy).then_inc(nm.hi, 1)

            def root(nm):
                act.wait_ge(nm.sums, nm.n + 1)
                A(st[:, 0:DT], aux[0][:, 0:DT], ACT.Sqrt, bias=consts[:, 0:1], scale=1.0 / D).then_inc(nm.root, 1)

            def broadcast(nm):
                act.wait_ge(nm.bc, nm.n + 1)
                A(rstd[:, :], aux[0][:, :], ACT.Copy).then_inc(nm.rstd, 1)

            act.wait_ge(setup, 7)
            act.wait_ge(cst_in, 48)
            first_split("gu1_0")
            for k in range(DT):
                act.wait_ge(x_in[k // 2], 32)
                wait(act, norms[0].added, norms[0].tile + k)
                A(s1[:, :], h1[:, k, :], ACT.Square).then_inc(norms[0].sq, 1)
                act.wait_ge(norms[0].xt, norms[0].tile + k + 1)
                A(xh1[:, k, :], s0[:, :], ACT.Copy).then_inc(norms[0].hi, 1)

            def ffn(f, nm, nm_next, hh, h, xh):
                sg = ffns[f - 1]
                t0 = 0
                for g, n in enumerate(FF_GROUPS):
                    name = f"gu{f}_{g}"
                    def body(i):
                        t = i + t0
                        if g == 0 and isinstance(i, int) and i == 0:
                            root(nm)
                        split_hi(name, 0, i, n)
                        if g == 0 and isinstance(i, int) and i == 0:
                            broadcast(nm)
                        act.wait_ge(sg.gate, sg.tile + t + 1)
                        A(s0[:, :], s0[:, :], ACT.Silu).then_inc(sg.silu, 1)
                        split_hi(name, 1, i, n)
                        stand_alone(act)
                        act.wait_ge(sg.prod, sg.tile + t + 1)
                        A(hh[:, ds(i, 1), :].rearrange("p a t -> p (a t)"), s1[:, :], ACT.Copy).then_inc(sg.hi, 1)
                    loop(act, n, body, first=(g == 0))
                    t0 += n
                    dname = f"down{f}_{g}"
                    lastg = g == len(FF_GROUPS) - 1
                    def dbody(i):
                        for s in range(2):
                            split_hi(dname, s, i, DT // 2)
                            if lastg:
                                square_and_hi(nm_next, h, i * 2 + s, xh)
                    loop(act, DT // 2, dbody, first=lastg)

            ffn(1, norms[0], norms[1], hh1, h1, xhm)

            def l2_inverse(j):
                for b in range(2):
                    act.wait_ge(l2_sum, j * 2 + b + 1)
                    A(sc2[b][:, :], aux[b][:, :], ACT.Ln, bias=consts[:, 2:3]).then_inc(l2_ln, 1)
                for b in range(2):
                    act.wait_ge(l2_ln, j * 2 + b + 1)
                    A(sc2[b][:, :], sc2[b][:, :], ACT.Exp, scale=-0.5,
                      bias=consts[:, 3:4] if b == 0 else 0.0).then_inc(l2_inv, 1)

            sc2 = [s1, s2]

            def qk(i):
                f0 = isinstance(i, int) and i == 0
                if f0:
                    root(norms[1])
                split_hi("qk", 0, i, HEADS)
                if f0:
                    broadcast(norms[1])
                else:
                    l2_inverse(i - 1)
                for b, dst in enumerate((qo, kk_)):
                    if b:
                        split_hi("qk", 1, i, HEADS)
                    row = dst[:, ds(i, 1), :].rearrange("p a t -> p (a t)")
                    stand_alone(act)
                    act.wait_ge(conv_done, i * 2 + b + 1)
                    A(row, row, ACT.Silu).then_inc(silu_done, 1)
                    stand_alone(act)
                    act.wait_ge(silu_done, i * 2 + b + 1)
                    act.wait_ge(l2_used, i * 2 + b + 1)
                    A(sc2[b][:, :], row, ACT.Square).then_inc(sq_done, 1)
            loop(act, HEADS, qk, first=True)

            split_hi("ab", 0, 0, 2)
            l2_inverse(HEADS - 1)

            act.wait_ge(ab["z"], 1)
            act.wait_ge(l2_used, 2 * HEADS + 2)
            lane = slice(LANE_A, LANE_A + HEADS)
            A(s1[0:64, :], s0[0:64, :], ACT.Copy).then_inc(ab["act"], 1)
            A(s2[lane, :], s0[lane, :], ACT.Abs, bias=vecs[lane, V_DT:V_DT + 1]).then_inc(ab["act"], 1)
            A(st[lane, 0:1], vecs[lane, V_AL:V_AL + 1], ACT.Exp).then_inc(ab["act"], 1)
            act.wait_ge(ab["act"], 3)
            A(s2[lane, :], s2[lane, :], ACT.Exp, scale=-1.0).then_inc(ab["act"], 1)
            act.wait_ge(ab["act"], 4)
            A(s2[lane, :], s2[lane, :], ACT.Ln, bias=consts[lane, 4:5]).then_inc(ab["act"], 1)
            A(s1[0:HEADS, :], s1[0:HEADS, :], ACT.Sigmoid).then_inc(ab["act"], 1)

            def v(i):
                for s in range(2):
                    if not (s == 1 and is_last(i, 4)):
                        split_hi("v", s, i, 4)
                    row = vv_[:, ds(i * 2 + s, 1), :].rearrange("p a t -> p (a t)")
                    stand_alone(act)
                    act.wait_ge(v_conv, i * 2 + s + 1)
                    A(row, row, ACT.Silu).then_inc(v_done, 1)
                if isinstance(i, int) and i == 0:
                    act.wait_ge(ab["gv"], 2)
                    A(eg[:, :], aux[1][:, 0:64], ACT.Exp).then_inc(ab["gact"], 1)
                    A(gl[:, :], aux[1][:, 64:128], ACT.Exp).then_inc(ab["gact"], 1)
                    A(kd[:, :], kd[:, :], ACT.Exp).then_inc(ab["gact"], 1)
            loop(act, 4, v, first=True)

            def gelus(c):
                stand_alone(act)
                act.wait_ge(u_s["arg0"], c + 1)
                A(s0[:, :], s0[:, :], ACT.Gelu).then_inc(u_s["done0"], 1)
                stand_alone(act)
                act.wait_ge(u_s["arg1"], c + 1)
                A(gv[:, ds(c, 1), :].rearrange("p a t -> p (a t)"), s1[:, :], ACT.Gelu).then_inc(u_s["done1"], 1)

            def split_hi_1(c):
                act.wait_ge(acc_done[1], BASE["uv"][1] + c)
                act.wait_ge(w_loaded[1], (BASE["uv"][1] + c + 1) * 16)
                A(w_hi[1][:, :, :], w_raw[1][:, :, :], ACT.Copy).then_inc(w_hi_done[1], 1)

            act.sem_inc(dn_s["oc"], 2)

            def delta(c):
                B = lambda n, g: dn[n, g][:, :, :]
                for g in range(2):
                    act.wait_ge(dn_s["G"], c * 2 + g + 1)
                    A(B("V", g), bank[g, 1], ACT.Exp).then_inc(dn_s["EG"], 1)
                split_hi_1(c)
                for g in range(2):
                    act.wait_ge(dn_s["arg"], c * 2 + g + 1)
                    A(B("D", g), B("X", g), ACT.Exp).then_inc(dn_s["D"], 1)
                for g in range(2):
                    act.wait_ge(dn_s["tv"], c * 2 + g + 1)
                    act.wait_ge(dn_s["qd"], c * 2 + g + 1)
                    A(B("V", g), bank[g, 1], ACT.Copy).then_inc(dn_s["V"], 1)
                if not (isinstance(c, int) and c == 0):
                    gelus(c - 1)
                for g in range(2):
                    act.wait_ge(dn_s["T"], (c * 5 + 4) * 2 + g + 1)
                    for b, q in enumerate(quad):
                        A(dn["TT", g][q, :, q], dn["TTc", g][q, :, :], ACT.Copy)
                    for b in range(2):
                        A(dn["Tf", g][quad[b], :, quad[b]], dn["Tc", g][quad[b], :, :], ACT.Copy)
                for g in range(2):
                    act.wait_ge(dn_s["x5"], c * 2 + g + 1)
                    for b in (1, 3):
                        last = A(dn["Xc", g][quad[b], :, :], bankc[g, 1][quad[b], :, :], ACT.Copy)
                    last.then_inc(dn_s["X5"], 1)
                for g in range(2):
                    act.wait_ge(dn_s["u5"], c * 2 + g + 1)
                    A(dn["TT", g][quad[0], :, quad[1]], bankc[g, 0][quad[0], :, :], ACT.Copy, scale=-1.0)
                    A(dn["TT", g][quad[2], :, quad[3]], bankc[g, 0][quad[2], :, :], ACT.Copy, scale=-1.0)
                    A(dn["Tf", g][quad[1], :, quad[0]], bankt[g, 0][quad[1], :, :], ACT.Copy, scale=-1.0)\
                        .then_inc(dn_s["T5"], 1)
                for g in range(2):
                    act.wait_ge(dn_s["x6"], c * 2 + g + 1)
                    A(dn["X6", g][64:128, :, :], bank64[g, 1][64:128, :, :], ACT.Copy).then_inc(dn_s["X6"], 1)
                for g in range(2):
                    act.wait_ge(dn_s["u6"], c * 2 + g + 1)
                    A(dn["TT", g][0:64, :, 64:128], bank64[g, 0][0:64, :, :], ACT.Copy, scale=-1.0)\
                        .then_inc(dn_s["T6"], 1)
                split_hi("uv", 0, c, 0)
                act.wait_ge(o_freed, c + 1)
                for g in range(2):
                    act.wait_ge(dn_s["o"], c * 2 + g + 1)
                    A(ost[:, HG * g:HG * g + HG, :], bank[g, 1], ACT.Copy).then_inc(dn_s["oc"], 1)
            delta(0)
            with act.Fori(1, NC) as c:
                delta(c)
            split_hi("uv", 1, NC - 1, 0)
            gelus(NC - 1)

            def gate(i):
                for s in range(2):
                    m = i * 2 + s
                    f0 = isinstance(i, int) and m == 0
                    if not f0:
                        stand_alone(act)
                        act.wait_ge(g_s["norm"], m)
                    if f0:
                        act.wait_ge(o_back[0], 32)
                    if isinstance(i, int) and m == 2:
                        act.wait_ge(o_back[1], 16 * (HEADS - 2))
                    A(s2[:, :], oo[:, ds(m, 1), :].rearrange("p a t -> p (a t)"), ACT.Square).then_inc(g_s["sq"], 1)
                    split_hi("g", s, i, 4)
                    act.wait_ge(g_s["sum"], m + 1)
                    A(s2[:, :], aux[0][:, :], ACT.Ln, scale=1.0 / P, bias=consts[:, 0:1]).then_inc(g_s["ln"], 1)
                    act.wait_ge(g_s["ln"], m + 1)
                    A(s2[:, :], s2[:, :], ACT.Exp, scale=-0.5).then_inc(g_s["inv"], 1)
                    act.wait_ge(g_s["gate"], m + 1)
                    A(sc[s][:, :], sc[s][:, :], ACT.Silu).then_inc(g_s["silu"], 1)
                    stand_alone(act)
                    act.wait_ge(g_s["prod"], m + 1)
                    A(oh[:, ds(m, 1), :].rearrange("p a t -> p (a t)"), sc[s][:, :], ACT.Copy).then_inc(g_s["hi"], 1)
            gate(0)
            gate(1)
            with act.Fori(2, 4) as i:
                gate(i)

            def gaya(i):
                split_hi("gaya", 0, i, 8)
                act.wait_ge(y_s["gate"], i + 1)
                A(s0[:, :], s0[:, :], ACT.Sigmoid).then_inc(y_s["sig"], 1)
                split_hi("gaya", 1, i, 8)
            loop(act, 8, gaya)

            def gb(i):
                for s in range(2):
                    n = i * 2 + s
                    f0 = isinstance(i, int) and n == 0
                    if not f0:
                        stand_alone(act)
                        act.wait_ge(b_s_["tr"], n)
                    A(s0[:, :].rearrange("p (m t) -> p m t", m=DT), gv[:, :, ds(n * C, C)], ACT.Copy)\
                        .then_inc(b_s_["copy"], 1)
                    split_hi("gb", s, i, 4)
                    stand_alone(act)
                    act.wait_ge(b_s_["gate"], n + 1)
                    row = sig_b[:, ds(n, 1), :].rearrange("p a t -> p (a t)")
                    A(row, row, ACT.Sigmoid).then_inc(b_s_["sig"], 1)
                    act.wait_ge(b_s_["var"], n + 1)
                    A(st[:, 10:11], st[:, 9:10], ACT.Sqrt, bias=consts[:, 1:2]).then_inc(b_s_["root"], 1)
                    if not f0:
                        mix_hi(n - 1)

            def mix_hi(n):
                stand_alone(act)
                act.wait_ge(b_s_["prod"], n + 1)
                A(sh[:, :, ds(n * C, C)], uu[:, :, ds(n * C, C)], ACT.Copy).then_inc(b_s_["hi"], 1)
            act.wait_ge(u_s["done1"], 8)
            act.wait_ge(y_s["out"], 8)
            loop(act, 4, gb, first=True)
            mix_hi(7)

            def yb(i):
                for s in range(2):
                    n = i * 2 + s
                    split_hi("yb", s, i, 4)
                    stand_alone(act)
                    act.wait_ge(yb_s["m"], n + 1)
                    A(mh[:, ds(n, 1), :].rearrange("p a t -> p (a t)"), sc[s][:, :], ACT.Copy).then_inc(yb_s["hi"], 1)
            loop(act, 4, yb)

            def wo(i):
                for s in range(2):
                    split_hi("wo", s, i, 4)
                    square_and_hi(norms[2], h2, i * 2 + s, xh2)
            loop(act, 4, wo, first=True)

            ffn(2, norms[2], norms[3], hh2, h2, None)
            root(norms[3])
            broadcast(norms[3])
            for k in range(DT):
                act.wait_ge(norms[3].ready, norms[3].tile + k + 1)
                act.dma_start(out[k], h2[:, k, :]).then_inc(out_sem, 16)

        @block.vector
        def _(dve):
            TT, TS, STT = nc.vector.tensor_tensor, nc.vector.tensor_scalar, nc.vector.scalar_tensor_tensor
            mult, add, sub = ALU.mult, ALU.add, ALU.subtract

            def split_lo(name, s, i, n):
                kt = kt_next(name, s, i, n)
                if kt:
                    u = BASE[name][s] + i
                    dve.wait_ge(w_hi_done[s], u + 2)
                    TT(w_lo[s][:, 0:kt, :], w_raw[s][:, 0:kt, :], w_hi[s][:, 0:kt, :].bitcast(f32), sub)\
                        .then_inc(w_ready[s], 1)

            def first_split(name):
                for s in range(2):
                    dve.wait_ge(w_hi_done[s], BASE[name][s] + 1)
                    TT(w_lo[s][:, :, :], w_raw[s][:, :, :], w_hi[s][:, :, :].bitcast(f32), sub)\
                        .then_inc(w_ready[s], 1)

            def row(t, m):
                return t[:, ds(m, 1), :].rearrange("p a t -> p (a t)")

            def statistics(nm, h, m, vcol, xh, xl):
                if xh is not None:
                    dve.wait_ge(nm.h, nm.h_tile + m + 1)
                    wait(dve, nm.ready, nm.tile + m)
                    TS(s0[:, :], row(h, m), vecs[:, ds(m + vcol, 1)], None, mult).then_inc(nm.xt, 1)
                dve.wait_ge(nm.sq, nm.tile + m + 1)
                wait(dve, nm.added, nm.tile + m)
                TT(s2[:, :], s2[:, :], s1[:, :], add).then_inc(nm.added, 1)
                if xh is not None:
                    dve.wait_ge(nm.hi, nm.tile + m + 1)
                    TT(row(xl, m), s0[:, :], row(xh, m).bitcast(f32), sub).then_inc(nm.ready, 1)

            def zero_sum(nm):
                nc.vector.memset(s2[:, :], 0.0).then_inc(nm.zero, 1)
                dve.wait_ge(nm.zero, nm.n + 1)

            def inverse(nm):
                dve.wait_ge(nm.root, nm.n + 1)
                nc.vector.reciprocal(st[:, 0:DT], st[:, 0:DT]).then_inc(nm.inv, 1)
                dve.wait_ge(nm.inv, nm.n + 1)
                TT(s2[:, :].rearrange("p (c i) -> p c i", c=NC), bc_mid(ident[:, :], NC), bc_row(st[:, 0:DT], DT), mult)\
                    .then_inc(nm.diag, 1)

            first_split("gu1_0")
            dve.wait_ge(cst_in, 48)
            zero_sum(norms[0])
            for k in range(DT):
                dve.wait_ge(x_in[k // 2], 32)
                nm = norms[0]
                wait(dve, nm.ready, nm.tile + k)
                TS(s0[:, :], h1[:, k, :], vecs[:, V_N1 + k:V_N1 + k + 1], None, mult).then_inc(nm.xt, 1)
                dve.wait_ge(nm.sq, nm.tile + k + 1)
                wait(dve, nm.added, nm.tile + k)
                TT(s2[:, :], s2[:, :], s1[:, :], add).then_inc(nm.added, 1)
                dve.wait_ge(nm.hi, nm.tile + k + 1)
                TT(xl1[:, k, :], s0[:, :], xh1[:, k, :].bitcast(f32), sub).then_inc(nm.ready, 1)

            def ffn(f, nm, nm_next, hh, hl, h, vcol, xh, xl):
                sg = ffns[f - 1]
                t0 = 0
                for g, n in enumerate(FF_GROUPS):
                    name = f"gu{f}_{g}"
                    def body(i):
                        t = i + t0
                        u = [BASE[name][s] + i for s in range(2)]
                        f0 = g == 0 and isinstance(i, int) and i == 0
                        if f0:
                            inverse(nm)
                        split_lo(name, 0, i, n)
                        if f0:
                            dve.wait_ge(nm.rstd, nm.n + 1)
                        dve.wait_ge(acc_done[0], u[0] + 1)
                        TT(s0[:, :], acc[0][:, :], rstd[:, :], mult).then_inc(sg.gate, 1)
                        dve.wait_ge(sg.gate, sg.tile + t + 1)
                        dve.sem_inc(acc_free[0], 1)
                        split_lo(name, 1, i, n)
                        dve.wait_ge(acc_done[1], u[1] + 1)
                        wait(dve, sg.ready, sg.tile + t)
                        TT(s1[:, :], acc[1][:, :], rstd[:, :], mult).then_inc(acc_free[1], 1)
                        dve.wait_ge(acc_free[1], u[1] + 1)
                        dve.wait_ge(sg.silu, sg.tile + t + 1)
                        TT(s1[:, :], s0[:, :], s1[:, :], mult).then_inc(sg.prod, 1)
                        dve.wait_ge(sg.hi, sg.tile + t + 1)
                        TT(row(hl, i), s1[:, :], row(hh, i).bitcast(f32), sub).then_inc(sg.ready, 1)
                    loop(dve, n, body, first=(g == 0))
                    t0 += n
                    dname = f"down{f}_{g}"
                    lastg = g == len(FF_GROUPS) - 1
                    if lastg:
                        zero_sum(nm_next)
                    def dbody(i):
                        for s in range(2):
                            m = i * 2 + s
                            u = BASE[dname][s] + i
                            split_lo(dname, s, i, DT // 2)
                            dve.wait_ge(acc_done[s], u + 1)
                            ins = STT(row(h, m), acc[s][:, :], 0.5, row(h, m), mult, add)
                            ins.then_inc(acc_free[s], 1)
                            if lastg:
                                dve.wait_ge(acc_free[s], u + 1)
                                dve.sem_inc(nm_next.h, 1)
                                statistics(nm_next, h, m, vcol, xh, xl)
                    loop(dve, DT // 2, dbody, first=lastg)

            ffn(1, norms[0], norms[1], hh1, hl1, h1, V_NM, xhm, xlm)

            def conv(ch, s, dst, wrow):
                ch.link(TT(s0p[:, 3:3 + SEQ], acc[s][:, :], rstd[:, :], mult))
                dve.sem_inc(acc_free[s], 1)
                ch.link(TS(dst, s0p[:, 3:3 + SEQ], vecs[:, ds(wrow * TAPS + (V_CW + TAPS - 1), 1)], None, mult))
                for j in range(TAPS - 2, -1, -1):
                    ins = STT(dst, s0p[:, j:j + SEQ], vecs[:, ds(wrow * TAPS + (V_CW + j), 1)], dst, mult, add)
                    if j:
                        ch.link(ins)
                return ins

            def l2_scale(j):
                for b, dst in enumerate((qo, kk_)):
                    dve.wait_ge(l2_inv, j * 2 + b + 1)
                    dve.wait_ge(silu_done, j * 2 + b + 1)
                    TT(row(dst, j), row(dst, j), sc2[b][:, :], mult).then_inc(l2_used, 1)

            sc2 = [s1, s2]
            padded = [False]

            def qk(i):
                f0 = isinstance(i, int) and i == 0
                ch = Chain(dve, s_conv, i, 8)
                if f0:
                    inverse(norms[1])
                split_lo("qk", 0, i, HEADS)
                if f0:
                    dve.wait_ge(spilled, 16 * DT)
                    nc.vector.memset(s0p[:, 0:3], 0.0).then_inc(s_conv_a, 1)
                    dve.wait_ge(s_conv_a, 1)
                    dve.sem_inc(l2_used, 2)
                    dve.wait_ge(norms[1].rstd, norms[1].n + 1)
                dve.wait_ge(acc_done[0], BASE["qk"][0] + i + 1)
                conv(ch, 0, row(qo, i), i).then_inc(conv_done, 1)
                if not f0:
                    l2_scale(i - 1)
                split_lo("qk", 1, i, HEADS)
                dve.wait_ge(acc_done[1], BASE["qk"][1] + i + 1)
                conv(ch, 1, row(kk_, i), i + HEADS).then_inc(conv_done, 1)
                ch.end()
            loop(dve, HEADS, qk, first=True)

            split_lo("ab", 0, 0, 2)
            dve.wait_ge(acc_done[0], BASE["ab"][0] + 1)
            dve.wait_ge(conv_done, 2 * HEADS)
            TT(s0[:, :], acc[0][:, :], rstd[:, :], mult).then_inc(ab["z"], 1)
            dve.wait_ge(ab["z"], 1)
            dve.sem_inc(acc_free[0], 1)
            l2_scale(HEADS - 1)
            lane = slice(LANE_A, LANE_A + HEADS)
            dve.wait_ge(ab["act"], 6)
            TS(s1[lane, :], s0[lane, :], vecs[lane, V_DT:V_DT + 1], 0.0, add, ALU.max).then_inc(ab["dve"], 1)
            dve.wait_ge(ab["dve"], 1)
            TT(s1[lane, :], s1[lane, :], s2[lane, :], add).then_inc(ab["dve"], 1)
            dve.wait_ge(ab["dve"], 2)
            TS(s1[lane, :], s1[lane, :], st[lane, 0:1], -1.0, mult, mult).then_inc(ab["dve"], 1)
            nc.vector.memset(s0p[:, 0:3], 0.0).then_inc(ab["dve"], 1)
            dve.wait_ge(ab["dve"], 4)

            def v(i):
                for s in range(2):
                    ch = Chain(dve, v_chain, i * 2 + s, 4)
                    if not (s == 1 and is_last(i, 4)):
                        split_lo("v", s, i, 4)
                    dve.wait_ge(acc_done[s], BASE["v"][s] + i + 1)
                    conv(ch, s, row(vv_, i * 2 + s), i * 2 + s + 2 * HEADS).then_inc(v_conv, 1)
                    dve.wait_ge(v_conv, i * 2 + s + 1)
                    ch.end()
                    if isinstance(i, int) and i == 0 and s == 0:
                        dve.wait_ge(ab["t"], 1)
                        t = aux[0][:, 0:512].rearrange("p (c x) -> p c x", c=NC)
                        nc.vector.tensor_copy(beta[:, :].rearrange("p (c h) -> p c h", c=NC), t[:, :, 0:HEADS])\
                            .then_inc(ab["cols"], 1)
                        nc.vector.tensor_copy(la[:, 0:NC * HEADS].rearrange("p (c h) -> p c h", c=NC), t[:, :, LANE_A:LANE_A + HEADS])\
                            .then_inc(ab["cols"], 1)
                if isinstance(i, int) and i == 0:
                    dve.wait_ge(ab["g"], 1)
                    nc.vector.tensor_copy(gcol[:, :], aux[1][:, 0:64]).then_inc(ab["gv"], 1)
                    dve.wait_ge(ab["gv"], 1)
                    TT(kd[:, :], aux[1][:, 64:128], gcol[:, :], sub).then_inc(ab["gv"], 1)
            loop(dve, 4, v, first=True)

            dve.wait_ge(ab["gact"], 3)
            dve.wait_ge(v_done, HEADS)
            dve.wait_ge(q_out, 16 * HEADS)
            dve.wait_ge(k_out, 16 * HEADS)
            for g in range(2):
                nc.vector.memset(dn["TT", g][:, :, :], 0.0)
                nc.vector.memset(dn["Tf", g][0:64, :, :], 0.0)
                nc.vector.memset(dn["S", g][:, :, :], 0.0).then_inc(dn_s["S"], 1)
            dve.wait_ge(dn_s["S"], 2)
            dve.wait_ge(masks_in, 32)
            dve.wait_ge(v_out, 16 * HEADS)

            def split_lo_1(c):
                dve.wait_ge(w_hi_done[1], BASE["uv"][1] + c + 1)
                TT(w_lo[1][:, :, :], w_raw[1][:, :, :], w_hi[1][:, :, :].bitcast(f32), sub).then_inc(w_ready[1], 1)

            def log_decay(c):
                for g in range(2):
                    TT(dn["LU", g][:, :, :], bc_mid(upper[:, :], HG), cols(la, g, c), mult).then_inc(dn_s["laU"], 1)

            def cols(t, g, c):
                return t[:, ds(c * HEADS + HG * g, HG)].unsqueeze(2).to_broadcast([P, HG, P])

            def block(n, part=slice(0, P)):
                w = part.stop - part.start
                return blocks[part, n, :].unsqueeze(1).to_broadcast([w, HG, B32])

            def heads(g):
                return slice(HG * g, HG * g + HG)

            def delta(c):
                B = lambda n, g: dn[n, g][:, :, :]
                for g in range(2):
                    dve.wait_ge(dn_s["EG"], c * 2 + g + 1)
                    TT(B("X", g), bank[g, 1], cols(gcol, g, c), sub).then_inc(dn_s["argA"], 1)
                for g in range(2):
                    dve.wait_ge(dn_s["argA"], c * 2 + g + 1)
                    TT(B("X", g), B("X", g), bc_mid(bound[:, :], HG), ALU.min).then_inc(dn_s["arg"], 1)
                for g in range(2):
                    dve.wait_ge(dn_s["tk"], c * 2 + g + 1)
                    TT(B("Ktm", g), bank[g, 0], cols(kd, g, c), mult).then_inc(dn_s["Kd"], 1)
                for g in range(2):
                    dve.wait_ge(dn_s["D"], c * 2 + g + 1)
                    dve.wait_ge(dn_s["kk"], c * 2 + g + 1)
                    TT(B("NT", g), bank[g, 1], B("D", g), mult).then_inc(dn_s["NTa"], 1)
                for g in range(2):
                    dve.wait_ge(dn_s["qk"], c * 2 + g + 1)
                    TT(B("AT", g), bank[g, 0], B("D", g), mult).then_inc(dn_s["AT"], 1)
                for g in range(2):
                    dve.wait_ge(dn_s["NTa"], c * 2 + g + 1)
                    TT(B("NT", g), B("NT", g), cols(beta, g, c), mult).then_inc(dn_s["NT"], 1)
                for g in range(2):
                    dve.wait_ge(dn_s["AT"], c * 2 + g + 1)
                    TT(B("D", g), qc[:, heads(g), :], B("V", g), mult).then_inc(dn_s["qd"], 1)
                for g in range(2):
                    dve.wait_ge(dn_s["NT"], c * 2 + g + 1)
                    for q in quad:
                        last = TT(dn["TTc", g][q, :, :], dn["NT", g][q, :, q], block(1, q), mult)
                    last.then_inc(dn_s["L0"], 1)
                for g in range(2):
                    dve.wait_ge(dn_s["L0"], c * 2 + g + 1)
                    TT(B("TTc", g), block(0), B("TTc", g), sub).then_inc(dn_s["TT"], 1)
                for g in range(2):
                    dve.wait_ge(dn_s["TT"], c * 10 + g + 1)
                    nc.vector.transpose(flat(dn["Tc", g]), flat(dn["TTc", g])).then_inc(dn_s["T"], 1)
                for g in range(2):
                    dve.wait_ge(dn_s["KS"], c * 2 + g + 1)
                    TT(B("X", g), bank[g, 0], cols(eg, g, c), mult).then_inc(dn_s["eKS"], 1)
                for g in range(2):
                    dve.wait_ge(dn_s["eKS"], c * 2 + g + 1)
                    dve.wait_ge(dn_s["V"], c * 2 + g + 1)
                    TT(B("V", g), B("V", g), B("X", g), sub).then_inc(dn_s["Rr"], 1)
                for l in range(1, 5):
                    for g in range(2):
                        dve.wait_ge(dn_s["xp"], (c * 4 + l - 1) * 2 + g + 1)
                        TT(B("Xc", g), bankc[g, 1], block(1 + l), mult).then_inc(dn_s["X"], 1)
                    for g in range(2):
                        dve.wait_ge(dn_s["up"], (c * 4 + l - 1) * 2 + g + 1)
                        dve.wait_ge(dn_s["T"], (c * 5 + l - 1) * 2 + g + 1)
                        TT(B("TTc", g), B("TTc", g), bankc[g, 0], sub).then_inc(dn_s["TT"], 1)
                    for g in range(2):
                        dve.wait_ge(dn_s["TT"], (c * 5 + l) * 2 + g + 1)
                        nc.vector.transpose(flat(dn["Tc", g]), flat(dn["TTc", g])).then_inc(dn_s["T"], 1)
                    if l == 1:
                        split_lo_1(c)
                    if l == 2:
                        log_decay(c + 1)
                dve.wait_ge(acc_done[0], BASE["uv"][0] + c + 1)
                dve.wait_ge(u_freed, c + 1)
                TT(s0[:, :], acc[0][:, :], rstd[:, :], mult).then_inc(u_s["arg0"], 1)
                dve.wait_ge(u_s["arg0"], c + 1)
                dve.sem_inc(acc_free[0], 1)
                for g in range(2):
                    dve.wait_ge(dn_s["TR"], c * 2 + g + 1)
                    TT(B("X", g), bank[g, 0], cols(beta, g, c), mult).then_inc(dn_s["vn"], 1)
                split_lo("uv", 0, c, 0)
                for g in range(2):
                    dve.wait_ge(dn_s["o"], c * 2 + g + 1)
                    dve.wait_ge(dn_s["S"], c * 2 + g + 1)
                    TT(B("S", g), B("S", g), cols(gl, g, c), mult).then_inc(dn_s["Sg"], 1)
                for g in range(2):
                    dve.wait_ge(dn_s["Sg"], c * 2 + g + 1)
                    dve.wait_ge(dn_s["Kv"], c * 2 + g + 1)
                    TT(B("S", g), B("S", g), bank[g, 0], add).then_inc(dn_s["S"], 1)
                dve.wait_ge(acc_done[1], BASE["uv"][1] + c + 1)
                if not (isinstance(c, int) and c == 0):
                    dve.wait_ge(u_s["done1"], c)
                TT(s1[:, :], acc[1][:, :], rstd[:, :], mult).then_inc(u_s["arg1"], 1)
                dve.wait_ge(u_s["arg1"], c + 1)
                dve.sem_inc(acc_free[1], 1)

            def flat(t):
                return t[:, :, :].rearrange("p h i -> p (h i)")
            nc.vector.memset(la[:, NC * HEADS:], 0.0).then_inc(dn_s["laU"], 1)
            log_decay(0)
            dve.wait_ge(dn_s["laU"], 1)
            delta(0)
            with dve.Fori(1, NC) as c:
                delta(c)
            split_lo("uv", 1, NC - 1, 0)
            dve.wait_ge(dn_s["S"], 2 * NC + 2)
            dve.wait_ge(dn_s["oc"], 2 * NC + 2)
            dve.wait_ge(u_freed, NC + 1)
            dve.wait_ge(u_s["done1"], NC)
            dve.sem_inc(dn_done, 1)


            def gate(i):
                for s in range(2):
                    m = i * 2 + s
                    split_lo("g", s, i, 4)
                    dve.wait_ge(acc_done[s], BASE["g"][s] + i + 1)
                    TT(sc[s][:, :], acc[s][:, :], rstd[:, :], mult).then_inc(g_s["gate"], 1)
                    dve.wait_ge(g_s["gate"], m + 1)
                    dve.sem_inc(acc_free[s], 1)
                    dve.wait_ge(g_s["inv"], m + 1)
                    TT(row(oo, m), row(oo, m), s2[:, :], mult).then_inc(g_s["norm"], 1)
                    dve.wait_ge(g_s["norm"], m + 1)
                    dve.wait_ge(g_s["silu"], m + 1)
                    STT(sc[s][:, :], row(oo, m), vecs[:, V_DN:V_DN + 1], sc[s][:, :], mult, mult).then_inc(g_s["prod"], 1)
                    dve.wait_ge(g_s["hi"], m + 1)
                    TT(row(ol, m), sc[s][:, :], row(oh, m).bitcast(f32), sub).then_inc(g_s["ready"], 1)
            loop(dve, 4, gate, first=True)
            dve.wait_ge(g_s["ready"], 8)

            def gaya(i):
                split_lo("gaya", 0, i, 8)
                dve.wait_ge(acc_done[0], BASE["gaya"][0] + i + 1)
                TT(s0[:, :], acc[0][:, :], rstd[:, :], mult).then_inc(y_s["gate"], 1)
                dve.wait_ge(y_s["gate"], i + 1)
                dve.sem_inc(acc_free[0], 1)
                split_lo("gaya", 1, i, 8)
                dve.wait_ge(acc_done[1], BASE["gaya"][1] + i + 1)
                dve.wait_ge(y_s["sig"], i + 1)
                if isinstance(i, int) and i == 0:
                    dve.wait_ge(ws_in, 16)
                    nc.vector.memset(wsT[CH:P, :, 0:CH], 0.0).then_inc(u_s["w"], 1)
                else:
                    dve.wait_ge(m_spilled, i * 16)
                TT(s1[:, :], acc[1][:, :], s0[:, :], mult).then_inc(y_s["out"], 1)
                dve.wait_ge(y_s["out"], i + 1)
                dve.sem_inc(acc_free[1], 1)
                if isinstance(i, int) and i == 7:
                    dve.wait_ge(bs_in, 16)
                    dve.wait_ge(u_s["rows"], 1)
                    for m in range(DT):
                        STT(s2[:, m * P:m * P + P], aux[1][:, m * P:m * P + P], vecs[:, V_SB + m:V_SB + m + 1],
                            s2[:, m * P:m * P + P], mult, add).then_inc(u_s["bias"], 1)

            CH = 64
            loop(dve, 8, gaya, first=True)
            dve.wait_ge(u_s["bias"], 8)
            dve.wait_ge(m_spilled, 16 * 8)

            def mix_out(n):
                at_n = slice(None), slice(None), ds(n * C, C)
                ch = Chain(dve, b_s_["chain"], n, 2)
                dve.wait_ge(b_s_["mix"], n + 1)
                ch.link(TT(gv[at_n], aux[1][:, :].rearrange("p (m t) -> p m t", m=DT),
                           bc_row(vecs[:, V_SW:V_SW + DT], DT), mult))
                ch.link(TT(gv[at_n], gv[at_n], s2[:, :].rearrange("p (m t) -> p m t", m=DT), add))
                if isinstance(n, int) and n == 0:
                    dve.wait_ge(u_back[0], 16)
                    dve.wait_ge(u_back[1], 16)
                TT(uu[at_n], gv[at_n], uu[at_n], mult).then_inc(b_s_["prod"], 1)
                dve.wait_ge(b_s_["hi"], n + 1)
                TT(sl[at_n], uu[at_n], sh[at_n].bitcast(f32), sub).then_inc(b_s_["ready"], 1)

            def gb(i):
                for s in range(2):
                    n = i * 2 + s
                    f0 = isinstance(i, int) and n == 0
                    split_lo("gb", s, i, 4)
                    dve.wait_ge(acc_done[s], BASE["gb"][s] + i + 1)
                    TT(row(sig_b, n), acc[s][:, :], rstd[:, :], mult).then_inc(b_s_["gate"], 1)
                    dve.wait_ge(b_s_["gate"], n + 1)
                    dve.sem_inc(acc_free[s], 1)
                    dve.wait_ge(b_s_["tr"], n + 1)
                    for b in range(2):
                        last = nc.vector.bn_stats(bnst[:, 6 * b:6 * b + 6], aux[0][:, HALF * b:HALF * b + HALF])
                    last.then_inc(b_s_["bn"], 1)
                    stand_alone(dve)
                    dve.wait_ge(b_s_["bn"], n + 1)
                    nc.vector.bn_aggr(st[:, 8:10], bnst[:, 0:12]).then_inc(b_s_["var"], 1)
                    dve.wait_ge(b_s_["root"], n + 1)
                    nc.vector.reciprocal(st[:, 10:11], st[:, 10:11]).then_inc(b_s_["inv"], 1)
                    dve.wait_ge(b_s_["inv"], n + 1)
                    dve.wait_ge(b_s_["var"], n + 1)
                    if not f0:
                        dve.wait_ge(b_s_["mix"], n)
                    TS(s1[:, :], aux[0][:, :], st[:, 8:9], st[:, 10:11], sub, mult).then_inc(b_s_["z"], 1)
                    if not f0:
                        mix_out(n - 1)
            loop(dve, 4, gb, first=True)
            mix_out(7)
            dve.wait_ge(b_s_["ready"], 8)

            def yb(i):
                for s in range(2):
                    n = i * 2 + s
                    split_lo("yb", s, i, 4)
                    dve.wait_ge(acc_done[s], BASE["yb"][s] + i + 1)
                    TT(row(sig_b, n), row(sig_b, n), acc[s][:, :], mult).then_inc(yb_s["t"], 1)
                    dve.wait_ge(yb_s["t"], n + 1)
                    dve.sem_inc(acc_free[s], 1)
                    dve.wait_ge(m_back[s], i * 16 + 16)
                    TT(sc[s][:, :], sc[s][:, :], row(sig_b, n), add).then_inc(yb_s["m"], 1)
                    dve.wait_ge(yb_s["hi"], n + 1)
                    TT(row(ml, n), sc[s][:, :], row(mh, n).bitcast(f32), sub).then_inc(yb_s["ready"], 1)
            loop(dve, 4, yb)
            dve.wait_ge(yb_s["ready"], 8)
            zero_sum(norms[2])

            def wo(i):
                for s in range(2):
                    m = i * 2 + s
                    split_lo("wo", s, i, 4)
                    dve.wait_ge(acc_done[s], BASE["wo"][s] + i + 1)
                    dve.wait_ge(h_back, 16 * DT)
                    TT(row(h2, m), row(h2, m), acc[s][:, :], add).then_inc(norms[2].h, 1)
                    dve.wait_ge(norms[2].h, norms[2].h_tile + m + 1)
                    dve.sem_inc(acc_free[s], 1)
                    statistics(norms[2], h2, m, V_N2, xh2, xl2)
            loop(dve, 4, wo, first=True)

            ffn(2, norms[2], norms[3], hh2, hl2, h2, 0, None, None)
            inverse(norms[3])
            dve.wait_ge(norms[3].rstd, norms[3].n + 1)
            for k in range(DT):
                STT(h2[:, k, :], h2[:, k, :], vecs[:, V_NF + k:V_NF + k + 1], rstd[:, :], mult, mult)\
                    .then_inc(norms[3].ready, 1)

        @block.tensor
        def _(pe):
            MM = nc.tensor.matmul

            def unit(name, s, i, xh, xl, kt=8, ready=None, mid=None):
                u = BASE[name][s] + i
                pe.wait_ge(w_ready[s], u + 1)
                wait(pe, acc_free[s], u)
                for b in range(2):
                    o = acc[s][:, HALF * b:HALF * b + HALF]
                    for k in range(kt):
                        if ready is not None and b == 0:
                            pe.wait_ge(ready[0], ready[1] + k + 1)
                        a, z = (t[:, k, HALF * b:HALF * b + HALF] for t in (xh, xl))
                        MM(o, w_hi[s][:, k, :], a, start=(k == 0), stop=False)
                        MM(o, w_hi[s][:, k, :], z, start=False, stop=False)
                        last = MM(o, w_lo[s][:, k, :], a, start=False, stop=(k == kt - 1))
                    if b == 0 and mid is not None:
                        mid()
                last.then_inc(acc_done[s], 1)

            def sums(nm):
                pe.wait_ge(nm.added, nm.tile + DT)
                for c in range(NC):
                    last = MM(aux[0][:, c:c + 1], s2[:, c * P:c * P + P], ones[:, 0:1], start=True, stop=True)
                last.then_inc(nm.sums, 1)

            def spread(nm):
                pe.wait_ge(nm.diag, nm.n + 1)
                for b in range(2):
                    last = MM(aux[0][:, HALF * b:HALF * b + HALF], ones[:, :], s2[:, HALF * b:HALF * b + HALF],
                              start=True, stop=True)
                last.then_inc(nm.bc, 1)

            def ffn(f, nm, hh, hl, xh, xl, n_ready):
                sg = ffns[f - 1]
                t0 = 0
                for g, n in enumerate(FF_GROUPS):
                    name = f"gu{f}_{g}"
                    def body(i):
                        f0 = g == 0 and isinstance(i, int) and i == 0
                        unit(name, 0, i, xh, xl, ready=(nm.ready, nm.tile) if f0 else None)
                        if f0:
                            sums(nm)
                        unit(name, 1, i, xh, xl, mid=(lambda: spread(nm)) if f0 else None)
                    loop(pe, n, body, first=(g == 0), last=False)
                    dname = f"down{f}_{g}"
                    def dbody(i):
                        for s in range(2):
                            f0 = isinstance(i, int) and s == 0
                            unit(dname, s, i, hh, hl, kt=n, ready=(sg.ready, sg.tile + t0) if f0 else None)
                    loop(pe, DT // 2, dbody, first=True, last=False)
                    t0 += n

            pe.wait_ge(setup, 7)
            pe.wait_ge(cst_in, 48)
            ffn(1, norms[0], hh1, hl1, xh1, xl1, None)

            def l2_sums(j):
                for b, t in enumerate((s1, s2)):
                    pe.wait_ge(sq_done, j * 2 + b + 1)
                    for hf in range(2):
                        last = MM(aux[b][:, HALF * hf:HALF * hf + HALF], ones[:, :], t[:, HALF * hf:HALF * hf + HALF],
                                  start=True, stop=True)
                    last.then_inc(l2_sum, 1)

            def qk(i):
                f0 = isinstance(i, int) and i == 0
                unit("qk", 0, i, xhm, xlm, ready=(norms[1].ready, norms[1].tile) if f0 else None)
                if f0:
                    sums(norms[1])
                else:
                    l2_sums(i - 1)
                unit("qk", 1, i, xhm, xlm, mid=(lambda: spread(norms[1])) if f0 else None)
            loop(pe, HEADS, qk, first=True, last=False)
            unit("ab", 0, 0, xhm, xlm)
            l2_sums(HEADS - 1)

            def v(i):
                f0 = isinstance(i, int)
                unit("v", 0, i, xhm, xlm)
                if f0:
                    pe.wait_ge(ab["dve"], 3)
                    pe.wait_ge(l2_ln, 2 * HEADS)
                    for c in range(NC):
                        last = nc.tensor.transpose(aux[0][:, 64 * c:64 * c + 64], s1[0:64, c * P:c * P + P],
                                                   ident[0:64, 0:64])
                    last.then_inc(ab["t"], 1)
                unit("v", 1, i, xhm, xlm)
                if f0:
                    pe.wait_ge(ab["cols"], 2)
                    MM(aux[1][:, 0:64], upper[:, :], la[:, 0:NC * HEADS], start=True, stop=True)
                    MM(aux[1][:, 64:128], ones[:, :], la[:, 0:NC * HEADS], start=True, stop=True).then_inc(ab["g"], 1)
            loop(pe, 4, v, first=True, last=False)

            pe.wait_ge(ab["gact"], 3)
            pe.wait_ge(ab["gv"], 2)

            def delta(c):
                B = lambda n, g: dn[n, g]
                piece = [0]

                def fill(n):
                    for j in range(piece[0], piece[0] + n):
                        s, b, k = j // 16, j // 8 % 2, j % 8
                        if j % 16 == 0:
                            pe.wait_ge(w_ready[s], BASE["uv"][s] + c + 1)
                            pe.wait_ge(acc_free[s], BASE["uv"][s] + c)
                        o = acc[s][:, HALF * b:HALF * b + HALF]
                        a, z = (t[:, k, HALF * b:HALF * b + HALF] for t in (xhm, xlm))
                        MM(o, w_hi[s][:, k, :], a, start=(k == 0), stop=False)
                        MM(o, w_hi[s][:, k, :], z, start=False, stop=False)
                        last = MM(o, w_lo[s][:, k, :], a, start=False, stop=(k == 7))
                        if j % 16 == 15:
                            last.then_inc(acc_done[s], 1)
                    piece[0] += n

                for g in range(2):
                    pe.wait_ge(dn_s["laU"], c * 2 + g + 2)
                    pe.wait_ge(dn_s["oc"], c * 2 + g + 1)
                    MM(bank[g, 1], ones[:, :], B("LU", g)[:, :, :], start=True, stop=True).then_inc(dn_s["G"], 1)
                fill(2)
                for g in range(2):
                    pe.wait_ge(k_in, c * 16 + 16)
                    pe.wait_ge(dn_s["S"], c * 2 + g + 1)
                    for h in range(HG):
                        last = nc.tensor.transpose(bank[g, 0][:, h, :], kc[:, HG * g + h, :], ident[:, :])
                    last.then_inc(dn_s["tk"], 1)
                fill(1)
                for g in range(2):
                    pe.wait_ge(dn_s["argA"], c * 2 + g + 1)
                    for h in range(HG):
                        last = MM(bank[g, 1][:, h, :], kc[:, HG * g + h, :], kc[:, HG * g + h, :], start=True, stop=True)
                    last.then_inc(dn_s["kk"], 1)
                for g in range(2):
                    pe.wait_ge(q_in, c * 16 + 16)
                    pe.wait_ge(dn_s["Kd"], c * 2 + g + 1)
                    for h in range(HG):
                        last = MM(bank[g, 0][:, h, :], kc[:, HG * g + h, :], qc[:, HG * g + h, :], start=True, stop=True)
                    last.then_inc(dn_s["qk"], 1)
                fill(2)
                for g in range(2):
                    pe.wait_ge(v_in, c * 16 + 16)
                    pe.wait_ge(dn_s["NTa"], c * 2 + g + 1)
                    for h in range(HG):
                        last = nc.tensor.transpose(bank[g, 1][:, h, :], vc[:, HG * g + h, :], ident[:, :])
                    last.then_inc(dn_s["tv"], 1)
                fill(1)
                for g in range(2):
                    pe.wait_ge(dn_s["AT"], c * 2 + g + 1)
                    for h in range(HG):
                        last = MM(bank[g, 0][:, h, :], kc[:, HG * g + h, :], B("S", g)[:, h, :], start=True, stop=True)
                    last.then_inc(dn_s["KS"], 1)
                fill(3)
                for l in range(1, 5):
                    for g in range(2):
                        pe.wait_ge(dn_s["T"], (c * 5 + l - 1) * 2 + g + 1)
                        if l == 1:
                            pe.wait_ge(dn_s["V"], c * 2 + g + 1)
                        carry(pe)
                        for h in range(HG):
                            for q in quad:
                                last = MM(bankc[g, 1][q, h, :], B("NT", g)[q, h, q], B("Tc", g)[q, h, :],
                                          start=True, stop=True)
                        last.then_inc(dn_s["xp"], 1)
                    fill((2, 2, 2, 1)[l - 1])
                    for g in range(2):
                        pe.wait_ge(dn_s["X"], (c * 4 + l - 1) * 2 + g + 1)
                        if l == 1:
                            pe.wait_ge(dn_s["eKS"], c * 2 + g + 1)
                        carry(pe)
                        for h in range(HG):
                            for q in quad:
                                last = MM(bankc[g, 0][q, h, :], B("Xc", g)[q, h, :], B("TTc", g)[q, h, :],
                                          start=True, stop=True)
                        last.then_inc(dn_s["up"], 1)
                    fill((3, 2, 2, 1)[l - 1])
                for g in range(2):
                    pe.wait_ge(dn_s["T"], (c * 5 + 4) * 2 + g + 1)
                    carry(pe)
                    for h in range(HG):
                        for lo, hi in ((0, 1), (2, 3)):
                            last = MM(bankc[g, 1][quad[hi], h, :], B("NT", g)[quad[lo], h, quad[hi]],
                                      B("Tc", g)[quad[lo], h, :], start=True, stop=True)
                    last.then_inc(dn_s["x5"], 1)
                fill(2)
                for g in range(2):
                    pe.wait_ge(dn_s["X5"], c * 2 + g + 1)
                    carry(pe)
                    for h in range(HG):
                        for lo, hi in ((0, 1), (2, 3)):
                            MM(bankc[g, 0][quad[lo], h, :], B("Xc", g)[quad[hi], h, :], B("TTc", g)[quad[hi], h, :],
                               start=True, stop=True)
                        last = MM(bankt[g, 0][quad[1], h, :], B("TTc", g)[quad[1], h, :], B("Xc", g)[quad[1], h, :],
                                  start=True, stop=True)
                    last.then_inc(dn_s["u5"], 1)
                fill(2)
                for g in range(2):
                    pe.wait_ge(dn_s["T5"], c * 2 + g + 1)
                    carry(pe)
                    for h in range(HG):
                        last = MM(bank64[g, 1][64:128, h, :], B("NT", g)[0:64, h, 64:128], B("Tf", g)[0:64, h, :],
                                  start=True, stop=True)
                    last.then_inc(dn_s["x6"], 1)
                fill(2)
                for g in range(2):
                    pe.wait_ge(dn_s["X6"], c * 2 + g + 1)
                    carry(pe)
                    for h in range(HG):
                        last = MM(bank64[g, 0][0:64, h, :], B("X6", g)[64:128, h, :], B("TT", g)[64:128, h, 64:128],
                                  start=True, stop=True)
                    last.then_inc(dn_s["u6"], 1)
                fill(2)
                for g in range(2):
                    pe.wait_ge(dn_s["Rr"], c * 2 + g + 1)
                    pe.wait_ge(dn_s["T6"], c * 2 + g + 1)
                    for h in range(HG):
                        last = MM(bank[g, 0][:, h, :], B("TT", g)[:, h, :], B("V", g)[:, h, :], start=True, stop=True)
                    last.then_inc(dn_s["TR"], 1)
                for g in range(2):
                    pe.wait_ge(dn_s["vn"], c * 2 + g + 1)
                    for h in range(HG):
                        MM(bank[g, 1][:, h, :], B("S", g)[:, h, :], B("D", g)[:, h, :], start=True, stop=False)
                        last = MM(bank[g, 1][:, h, :], B("X", g)[:, h, :], B("AT", g)[:, h, :], start=False, stop=True)
                    last.then_inc(dn_s["o"], 1)
                for g in range(2):
                    for h in range(HG):
                        last = MM(bank[g, 0][:, h, :], B("Ktm", g)[:, h, :], B("X", g)[:, h, :], start=True, stop=True)
                    last.then_inc(dn_s["Kv"], 1)
                assert piece[0] == 32, piece
            with pe.Fori(0, NC) as c:
                delta(c)
            pe.wait_ge(dn_done, 1)

            def gate(i):
                for s in range(2):
                    m = i * 2 + s
                    unit("g", s, i, xhm, xlm)
                    pe.wait_ge(g_s["sq"], m + 1)
                    for hf in range(2):
                        last = MM(aux[0][:, HALF * hf:HALF * hf + HALF], ones[:, :], s2[:, HALF * hf:HALF * hf + HALF],
                                  start=True, stop=True)
                    last.then_inc(g_s["sum"], 1)
            loop(pe, 4, gate, last=False)

            def gaya(i):
                f0 = isinstance(i, int)
                unit("gaya", 0, i, xhm, xlm)
                unit("gaya", 1, i, oh, ol, ready=(g_s["ready"], 0) if f0 else None)
                if f0:
                    pe.wait_ge(u_s["w"], 1)
                    ws = wsT[:, :, :].rearrange("p m t -> p (m t)")
                    for hf in range(2):
                        last = MM(aux[1][:, HALF * hf:HALF * hf + HALF], ones[:, :], ws[:, HALF * hf:HALF * hf + HALF],
                                  start=True, stop=True)
                    last.then_inc(u_s["rows"], 1)
            loop(pe, 8, gaya, first=True, last=False)

            def mix(n):
                pe.wait_ge(b_s_["z"], n + 1)
                if isinstance(n, int) and n == 0:
                    pe.wait_ge(u_s["bias"], 8)
                else:
                    pe.wait_ge(b_s_["prod"], n)
                for m in range(DT):
                    last = MM(aux[1][:, m * P:m * P + P], s1[:, m * P:m * P + P], wsT[:, m, :], start=True, stop=True)
                last.then_inc(b_s_["mix"], 1)

            def gb(i):
                for s in range(2):
                    n = i * 2 + s
                    unit("gb", s, i, xhm, xlm)
                    pe.wait_ge(b_s_["copy"], n + 1)
                    if not (isinstance(i, int) and n == 0):
                        pe.wait_ge(b_s_["z"], n)
                    for m in range(DT):
                        last = nc.tensor.transpose(aux[0][:, m * P:m * P + P], s0[:, m * P:m * P + P], ident[:, :])
                    last.then_inc(b_s_["tr"], 1)
                    if not (isinstance(i, int) and n == 0):
                        mix(n - 1)
            loop(pe, 4, gb, first=True, last=False)
            mix(7)

            def yb(i):
                for s in range(2):
                    if isinstance(i, int) and s == 0:
                        pe.wait_ge(b_s_["ready"], 8)
                    unit("yb", s, i, sh, sl)
            loop(pe, 4, yb, first=True, last=False)

            def wo(i):
                for s in range(2):
                    unit("wo", s, i, mh, ml, ready=(yb_s["ready"], 0) if isinstance(i, int) and s == 0 else None)
            loop(pe, 4, wo, first=True, last=False)

            ffn(2, norms[2], hh2, hl2, xh2, xl2, None)
            sums(norms[3])
            spread(norms[3])


def _level_masks():
    i = np.arange(P)
    later = (i[None, :] >= i[:, None]).astype(np.float32)
    bound = np.where(later > 0, 0.0, -1e30).astype(np.float32)
    r, c = (i % B32)[:, None], np.arange(B32)[None, :]
    def level(l):
        return (r >> (l + 1) == c >> (l + 1)) & ((r >> l) & 1 == 1) & ((c >> l) & 1 == 0)
    up = (r >> 1 == c >> 1) & (r & 1 == 0) & (c & 1 == 1)
    blocks = np.concatenate([(r == c)] + [up] + [level(l) for l in range(1, 5)], axis=1).astype(np.float32)
    blocks = np.pad(blocks, ((0, 0), (0, 2 * P - blocks.shape[1]))).reshape(P, 2, P)
    return np.ascontiguousarray(np.concatenate([np.stack([np.eye(P, dtype=np.float32), later, bound], axis=1), blocks],
                                               axis=1))


def _tiles(w):
    k, n = w.shape
    return np.ascontiguousarray(w.reshape(k // P, P, n // P, P).transpose(2, 1, 0, 3))


def kernel(**inputs):
    import concourse.bacc as bacc
    from concourse.bass_utils import run_bass_kernel_spmd

    a = {k: np.asarray(v) for k, v in inputs.items()}
    col = lambda v: v.reshape(-1, P).T
    vec = np.zeros((P, V_ALL), np.float32)
    for at, name in ((V_N1, "ffn1_norm_w"), (V_NM, "mix_norm_w"), (V_N2, "ffn2_norm_w"), (V_SW, "sgu_norm_w"),
                     (V_SB, "sgu_norm_b")):
        vec[:, at:at + DT] = col(a[name][0])
    vec[:, V_NF:V_NF + DT] = col(a["final_norm_w"])
    vec[:, V_DN] = a["dn_out_norm_w"][0]
    vec[LANE_A:LANE_A + HEADS, V_DT] = a["dn_dt_bias"][0]
    vec[LANE_A:LANE_A + HEADS, V_AL] = a["dn_a_log"][0]
    vec[:, V_CW:] = a["dn_conv_w"][0].reshape(TAPS, 3 * HEADS, P).transpose(2, 1, 0).reshape(P, -1)
    w_in = a["w_in"][0]
    nb = 4 * D
    w_ba = np.zeros((D, P), np.float32)
    w_ba[:, 0:HEADS] = w_in[:, nb:nb + HEADS]
    w_ba[:, LANE_A:LANE_A + HEADS] = w_in[:, nb + HEADS:nb + 2 * HEADS]
    arrays = {
        "x": np.ascontiguousarray(a["x"][0].T).reshape(DT, P, SEQ),
        "vec": vec, "cst": _level_masks(),
        "w_gate1": _tiles(a["ffn1_w_gate"][0]), "w_up1": _tiles(a["ffn1_w_up"][0]),
        "w_down1": _tiles(a["ffn1_w_down"][0]),
        "w_in": _tiles(np.concatenate([w_in[:, :nb], w_in[:, nb + 2 * HEADS:]], axis=1)),
        "w_ba": _tiles(w_ba), "w_ya": _tiles(a["dn_w_o"][0]), "w_yb": _tiles(a["gmlp_w_o"][0]),
        "w_out": _tiles(a["w_out"][0]),
        "w_s": np.ascontiguousarray(a["sgu_w_s"][0].transpose(2, 0, 1)),
        "b_s": np.ascontiguousarray(np.broadcast_to(a["sgu_b"][0].reshape(1, -1), (P, D))),
        "w_gate2": _tiles(a["ffn2_w_gate"][0]), "w_up2": _tiles(a["ffn2_w_up"][0]),
        "w_down2": _tiles(a["ffn2_w_down"][0]),
    }
    nc = bacc.Bacc("TRN2", target_bir_lowering=False, num_devices=1)
    f32 = mybir.dt.float32
    aps = [nc.dram_tensor(f"in_{k}", v.shape, f32, kind="ExternalInput").ap() for k, v in arrays.items()]
    h_spill = nc.dram_tensor("h_spill", (DT, P, SEQ), f32, kind="Internal").ap()
    m_spill = nc.dram_tensor("m_spill", (DT, P, SEQ), f32, kind="Internal").ap()
    more = [nc.dram_tensor(f"{n}_spill", (DT, P, SEQ), f32, kind="Internal").ap() for n in "qkvuo"]
    out = nc.dram_tensor("out", (DT, P, SEQ), f32, kind="ExternalOutput").ap()
    build(nc, *aps, h_spill, m_spill, *more, out)
    r = run_bass_kernel_spmd(nc, [{f"in_{k}": v for k, v in arrays.items()}], core_ids=[0])
    y = np.asarray(r.results[0]["out"]).reshape(D, SEQ)
    return np.ascontiguousarray(y.T).reshape(1, SEQ, D)
```

```python
import concourse.bass as bass
import numpy as np
from concourse import mybir
from contextlib import ExitStack

P = 128
SEQ = 1024
HALF = 512
D = 1024
DT = D // P
FF = 2816
FT = FF // P
FF_GROUPS = (8, 8, 6)
HEADS = 8
TAPS = 4
C = 128
NC = SEQ // C
HG = 4
AB = 64
LANE_A = 32
RMS_EPS, LN_EPS, L2_EPS = 1e-6, 1e-5, 1e-6

PHASES = []
for _g, _n in enumerate(FF_GROUPS):
    PHASES += [(f"gu1_{_g}", _n, _n), (f"down1_{_g}", DT // 2, DT // 2)]
PHASES += [("qk", HEADS, HEADS), ("v", HEADS // 2, HEADS // 2), ("uv", DT, DT),
           ("g", HEADS // 2, HEADS // 2), ("gaya", DT, DT), ("gb", DT // 2, DT // 2), ("yb", DT // 2, DT // 2),
           ("wo", DT // 2, DT // 2)]
for _g, _n in enumerate(FF_GROUPS):
    PHASES += [(f"gu2_{_g}", _n, _n), (f"down2_{_g}", DT // 2, DT // 2)]
BASE, _a, _b = {}, 0, 0
for _name, _na, _nb in PHASES:
    BASE[_name] = (_a, _b)
    _a, _b = _a + _na, _b + _nb

V_N1, V_NM, V_N2, V_NF, V_SW, V_SB, V_DN, V_DT, V_AL, V_CW = 0, 8, 16, 24, 32, 40, 48, 49, 50, 51
V_ALL = V_CW + 3 * HEADS * TAPS


X_GROUPS = ((0,), (1, 2), (3, 4), (5, 6), (7,))
B32 = 32


def build(nc, x, vec, cst, w_gate1, w_up1, w_down1, w_in, w_ba, w_ya, w_yb, w_out, w_s, b_s,
          w_gate2, w_up2, w_down2, h_spill, m_spill, q_spill, k_spill, v_spill, u_spill, o_spill, out):
    f32, f32r = mybir.dt.float32, mybir.dt.float32r
    ALU, ACT = mybir.AluOpType, mybir.ActivationFunctionType
    ds = bass.ds

    ctx = ExitStack()
    with ctx:
        KB = 1024
        start = (nc.sbuf_base + 63) // 64 * 64
        R = [start + 32 * KB * n for n in range(5)]
        W0 = start + 160 * KB
        S0 = W0 + 24 * KB
        S1 = S0 + 4128
        S2 = S1 + 4 * KB
        RS = S2 + 4 * KB
        DC = RS + 4 * KB
        SM = DC + 4 * KB

        def at(name, shape, dt, off):
            return nc.alloc_sbuf_tensor_at(name, shape, dt, offset=off)

        def big(name, dt, r):
            return at(name, [P, DT, SEQ], dt, R[r])

        h1 = big("h1", f32, 0)
        xh1, xl1 = big("xh1", f32r, 3), big("xl1", f32r, 4)
        hh1, hl1 = big("hh1", f32r, 1), big("hl1", f32r, 2)
        wab = [at(n, [P, DT, AB], dt, R[2] + 12 * KB + 2 * KB * j)
               for j, (n, dt) in enumerate((("wab_raw", f32), ("wab_hi", f32r), ("wab_lo", f32r)))]
        ab_z, ab_y, ab_t = (at(n, [P, SEQ], f32, R[2] + 20 * KB + 4 * KB * j) for j, n in enumerate(("ab_z", "ab_y", "ab_t")))
        qo, kk_, vv_ = big("qo", f32, 0), big("kfeat", f32, 1), big("vfeat", f32, 2)
        xhm, xlm = big("xhm", f32r, 3), big("xlm", f32r, 4)
        oo = big("oo", f32, 0)
        oh, ol = big("oh", f32r, 1), big("ol", f32r, 0)
        gv, uu = big("gv", f32, 2), big("uu", f32, 1)
        sh, sl = big("sh", f32r, 2), big("sl", f32r, 1)
        sig_b = big("sig_b", f32, 0)
        mh, ml = big("mh", f32r, 3), big("ml", f32r, 4)
        h2 = big("h2", f32, 0)
        xh2, xl2 = big("xh2", f32r, 1), big("xl2", f32r, 2)
        hh2, hl2 = big("hh2", f32r, 3), big("hl2", f32r, 4)
        w_raw = [at(f"w_raw{s}", [P, 8, P], f32, W0 + 4 * KB * s) for s in range(2)]
        w_hi = [at(f"w_hi{s}", [P, 8, P], f32r, W0 + 8 * KB + 4 * KB * s) for s in range(2)]
        w_lo = [at(f"w_lo{s}", [P, 8, P], f32r, W0 + 16 * KB + 4 * KB * s) for s in range(2)]
        s0p = at("s0p", [P, SEQ + 8], f32, S0)
        s0, s1, s2 = (at(n, [P, SEQ], f32, o) for n, o in (("s0", S0), ("s1", S1), ("s2", S2)))
        sc = [s0, s1]
        rstd = at("rstd", [P, SEQ], f32, RS)
        wsT = at("wsT", [P, 8, P], f32, DC)
        o_ = SM
        def small(name, shape):
            nonlocal o_
            n = int(np.prod(shape[1:])) * 4
            t = at(name, shape, f32, o_)
            o_ += (n + 31) // 32 * 32
            return t
        vecs = small("vecs", [P, V_ALL])
        ident = small("ident", [P, P])
        upper = small("upper", [P, P])
        ones = small("ones", [P, P])
        beta, gcol, eg, kd, gl = (small(n, [P, NC * HEADS]) for n in ("beta", "gcol", "eg", "kd", "gl"))
        la = small("la", [P, (NC + 1) * HEADS])
        st = small("st", [P, 16])
        bnst = small("bnst", [P, 16])
        consts = small("consts", [P, 8])
        assert o_ <= nc.sbuf_usable_end

        dn_at = R[0]
        def dn_tile(name, shape):
            nonlocal dn_at
            t = at(name, shape, f32, dn_at)
            dn_at += int(np.prod(shape[1:])) * 4
            return t
        qc, kc, vc, ost = (dn_tile(n, [P, HEADS, C]) for n in ("qc", "kc", "vc", "ost"))
        dn = {(n, g): dn_tile(f"dn_{n}{g}", [P, HG, w]) for g in range(2) for n, w in (
            ("S", P), ("Ktm", P), ("V", P), ("AT", P), ("NT", P), ("TT", P), ("X", P), ("D", P), ("LU", P),
            ("TTc", B32), ("Tc", B32), ("Xc", B32), ("Tf", 2 * B32), ("X6", 2 * B32))}
        bound = dn_tile("bound", [P, P])
        blocks = dn_tile("blocks", [P, 6, B32])
        assert dn_at <= R[2]

        acc = [ctx.enter_context(nc.psum_tensor(f"acc{s}", [P, SEQ], f32)) for s in range(2)]
        aux = [ctx.enter_context(nc.psum_tensor(f"aux{s}", [P, SEQ], f32)) for s in range(2)]
        bank = {(g, n): aux[g][:, HALF * n:HALF * n + HALF].rearrange("p (h i) -> p h i", h=HG)
                for g in range(2) for n in range(2)}
        bankc = {k: v.rearrange("p h i -> p (h i)")[:, 0:HG * B32].rearrange("p (h i) -> p h i", h=HG)
                 for k, v in bank.items()}
        bank64 = {k: v.rearrange("p h i -> p (h i)")[:, 0:HG * 2 * B32].rearrange("p (h i) -> p h i", h=HG)
                  for k, v in bank.items()}
        bankt = {k: v.rearrange("p h i -> p (h i)")[:, HALF // 2:HALF // 2 + HG * B32]
                 .rearrange("p (h i) -> p h i", h=HG) for k, v in bank.items()}
        quad = [slice(B32 * b, B32 * b + B32) for b in range(P // B32)]

        def sem(name):
            return ctx.enter_context(nc.semaphore(name))

        w_loaded = [sem(f"w_loaded{s}") for s in range(2)]
        w_hi_done = [sem(f"w_hi_done{s}") for s in range(2)]
        w_ready = [sem(f"w_ready{s}") for s in range(2)]
        acc_done = [sem(f"acc_done{s}") for s in range(2)]
        acc_free = [sem(f"acc_free{s}") for s in range(2)]
        cst_in = sem("cst_in")
        x_in = [sem(f"x_in{k}") for k in range(len(X_GROUPS))]
        spilled, h_back = sem("spilled"), sem("h_back")
        m_spilled = sem("m_spilled")
        m_back = [sem(f"m_back{s}") for s in range(2)]
        tables_in = sem("tables_in")
        bs_in = sem("bs_in")
        qk_spilled, v_out = sem("qk_spilled"), sem("v_out")
        q_in, k_in, v_in = sem("q_in"), sem("k_in"), sem("v_in")
        u_out, o_out = sem("u_out"), sem("o_out")
        u_freed, o_freed = sem("u_freed"), sem("o_freed")
        o_back = [sem(f"o_back{n}") for n in range(2)]
        u_back = [sem(f"u_back{n}") for n in range(2)]
        setup = sem("setup")
        out_sem = sem("out_sem")

        class Chain:
            def __init__(self, eng, s, i, per):
                self.eng, self.s, self.i, self.per, self.k = eng, s, i, per, 0
            def link(self, ins):
                self.k += 1
                ins.then_inc(self.s, 1)
                self.eng.wait_ge(self.s, self.i * self.per + self.k)
            def end(self):
                assert self.k == self.per, (self.k, self.per)

        norm_sems = {n: sem(f"norm_{n}") for n in (
            "hi",
            "ready",
            "h",
            "sq",
            "added",
            "sums",
            "root",
            "inv",
            "diag",
            "bc",
            "rstd",
            "zero",
        )}

        class Norm:
            def __init__(self, n):
                self.n, self.tile, self.h_tile = n, DT * n, DT * (n - 1)
                self.hi = norm_sems["hi"]
                self.ready = norm_sems["ready"]
                self.h = norm_sems["h"]
                self.sq = norm_sems["sq"]
                self.added = norm_sems["added"]
                self.sums = norm_sems["sums"]
                self.root = norm_sems["root"]
                self.inv = norm_sems["inv"]
                self.diag = norm_sems["diag"]
                self.bc = norm_sems["bc"]
                self.rstd = norm_sems["rstd"]
                self.zero = norm_sems["zero"]
        norms = [Norm(n) for n in range(4)]

        ffn_sems = {n: sem(f"ffn_{n}") for n in (
            "gate",
            "silu",
            "prod",
            "hi",
            "ready",
        )}

        class Ffn:
            def __init__(self, f):
                self.tile = FT * (f - 1)
                self.gate, self.silu, self.prod, self.hi, self.ready = ffn_sems.values()
        ffns = [Ffn(1), Ffn(2)]

        s_conv = sem("conv_chain")
        conv_done, silu_done, sq_done = sem("conv_done"), sem("silu_done"), sem("sq_done")
        l2_sum, l2_ln, l2_inv, l2_used = sem("l2_sum"), sem("l2_ln"), sem("l2_inv"), sem("l2_used")
        v_chain, v_conv, v_done = sem("v_chain"), sem("v_conv"), sem("v_done")
        ab = {n: sem(f"ab_{n}") for n in ("w_in", "w", "mm", "z", "act", "dve", "t", "cols", "g", "gv", "gact")}
        g_s = {n: sem(f"g_{n}") for n in ("sq", "sum", "ln", "inv", "gate", "silu", "norm", "prod", "hi", "ready")}
        y_s = {n: sem(f"y_{n}") for n in ("gate", "sig", "out")}
        u_s = {n: sem(f"u_{n}") for n in ("arg0", "arg1", "done0", "done1", "bias", "w", "rows")}
        b_s_ = {n: sem(f"b_{n}") for n in ("gate", "copy", "tr", "bn", "var", "root", "inv", "z", "mix",
                                           "chain", "prod", "hi", "ready")}
        yb_s = {n: sem(f"yb_{n}") for n in ("t", "m", "hi", "ready")}

        def wait(eng, s, v):
            if not isinstance(v, int) or v > 0:
                eng.wait_ge(s, v)

        def stand_alone(eng):
            eng.wait_ge(setup, 7)

        carrier = sem("carrier")

        def carry(eng):
            eng.sem_inc(carrier, 1)

        def loop(eng, n, body, first=False, last=True):
            lo, hi = int(first), n - int(last)
            if first:
                body(0)
            if hi - lo == 1:
                body(lo)
            elif hi > lo:
                with eng.Fori(lo, hi) as i:
                    body(i)
            if last and hi >= lo:
                body(n - 1)

        def wait_x(eng, k):
            n = [k in t for t in X_GROUPS].index(True)
            eng.wait_ge(x_in[n], 16 * (len(X_GROUPS[n]) + int(n == 0)))

        def is_last(i, n):
            return isinstance(i, int) and i == n - 1

        def bc_row(t, n):
            return t.unsqueeze(2).to_broadcast([P, n, P])

        def bc_mid(t, n):
            return t.unsqueeze(1).to_broadcast([P, n, P])

        def kt_next(name, s, i, n):
            if is_last(i, n):
                if name == f"down2_{len(FF_GROUPS) - 1}":
                    return 0
                if name.startswith("gu"):
                    return FF_GROUPS[int(name[-1])]
                return 8
            return FF_GROUPS[int(name[-1])] if name.startswith("down") else 8

        dn_s = {n: sem(f"dn_{n}") for n in (
            "laU", "G", "EG", "argA", "arg", "D", "kk", "qk", "qd", "tk", "tv", "NTa", "NT", "AT", "V", "KS",
            "eKS", "Rr", "L0", "TT", "T", "xp", "X", "up", "x5", "X5", "u5", "T5", "x6", "X6", "u6", "T6",
            "TR", "vn", "o", "oc", "Kd", "Kv", "Sg", "S")}
        dn_done = sem("dn_done")

        block = ctx.enter_context(nc.Block())

        @block.sync
        def _(sp):
            sp.dma_start(vecs[:, :], vec).then_inc(x_in[0], 16)
            def load_x(n):
                for k in X_GROUPS[n]:
                    sp.dma_start(h1[:, k, :], x[k]).then_inc(x_in[n], 16)
            load_x(0)
            for s, w in enumerate((w_gate1, w_up1)):
                sp.dma_start(w_raw[s][:, :, :], w[0]).then_inc(w_loaded[s], 16)
            for n in range(1, len(X_GROUPS)):
                load_x(n)

            def load(name, s, i, n, src, kt):
                u = BASE[name][s] + i
                wait(sp, w_ready[s], u)
                sp.dma_start(w_raw[s][:, 0:kt, :], src).then_inc(w_loaded[s], 16)

            def pick(w, t):
                return w[ds(t, 1)].rearrange("a p k m -> p (a k) m") if not isinstance(t, int) else w[t]

            def two(name, n, a, b, kt=8, done=0):
                def body(i):
                    load(name, 0, i, n, a(i), kt)
                    load(name, 1, i, n, b(i), kt)
                with sp.Fori(done, n) as i:
                    body(i)

            def ffn_loads(f, wg, wu, wd):
                t0 = 0
                for g, n in enumerate(FF_GROUPS):
                    two(f"gu{f}_{g}", n, lambda i: pick(wg, i + t0), lambda i: pick(wu, i + t0), done=int(f == 1 and g == 0))
                    def down(m):
                        return wd[ds(m, 1), :, t0:t0 + n, :].rearrange("a p k m -> p (a k) m")
                    two(f"down{f}_{g}", DT // 2, lambda i: down(i * 2), lambda i: down(i * 2 + 1), kt=n)
                    t0 += n

            ffn_loads(1, w_gate1, w_up1, w_down1)
            two("qk", HEADS, lambda i: pick(w_in, i), lambda i: pick(w_in, i + 8))
            two("v", 4, lambda i: pick(w_in, i * 2 + 16), lambda i: pick(w_in, i * 2 + 17))
            two("uv", 8, lambda i: pick(w_in, i + 32), lambda i: pick(w_in, i + 40))
            two("g", 4, lambda i: pick(w_in, i * 2 + 24), lambda i: pick(w_in, i * 2 + 25))
            two("gaya", 8, lambda i: pick(w_in, i + 48), lambda i: pick(w_ya, i))
            two("gb", 4, lambda i: pick(w_in, i * 2 + 56), lambda i: pick(w_in, i * 2 + 57))
            two("yb", 4, lambda i: pick(w_yb, i * 2), lambda i: pick(w_yb, i * 2 + 1))
            two("wo", 4, lambda i: pick(w_out, i * 2), lambda i: pick(w_out, i * 2 + 1))
            ffn_loads(2, w_gate2, w_up2, w_down2)
            sp.wait_ge(out_sem, 16 * DT)

        @block.gpsimd
        def _(pool):
            nc.gpsimd.memset(ones[:, :], 1.0).then_inc(setup, 1)
            for n, v in enumerate((RMS_EPS, LN_EPS, L2_EPS, -0.5 * float(np.log(P)), 1.0, 0.0)):
                nc.gpsimd.memset(consts[:, n:n + 1], v).then_inc(setup, 1)
            pool.dma_start(ident[:, :], cst[:, 0, :]).then_inc(cst_in, 16)
            pool.dma_start(upper[:, :], cst[:, 1, :]).then_inc(cst_in, 16)

            def spill(i):
                for b in range(2):
                    pool.wait_ge(norms[1].h, norms[1].h_tile + i * 2 + b + 1)
                    pool.dma_start(h_spill[ds(i * 2 + b, 1)].rearrange("a p t -> p (a t)"),
                                   h1[:, ds(i * 2 + b, 1), :].rearrange("p a t -> p (a t)")).then_inc(spilled, 16)
            loop(pool, 4, spill, last=False)

            def rows(t, m):
                return t[:, ds(m, 1), :].rearrange("p a t -> p (a t)")

            def dram(t, m):
                return t[ds(m, 1)].rearrange("a p t -> p (a t)")

            pool.wait_ge(acc_done[1], BASE["qk"][1])
            pool.dma_start(wab[0][:, :, :], w_ba).then_inc(ab["w_in"], 16)
            pool.dma_start(wsT[:, :, :], w_s).then_inc(tables_in, 16)

            def qk_out(i):
                pool.wait_ge(l2_used, i * 2 + 3)
                pool.dma_start(dram(q_spill, i), rows(qo, i)).then_inc(qk_spilled, 16)
                pool.wait_ge(l2_used, i * 2 + 4)
                pool.dma_start(dram(k_spill, i), rows(kk_, i)).then_inc(qk_spilled, 16)
            loop(pool, HEADS, qk_out, last=False)
            pool.wait_ge(qk_spilled, 2 * 16 * HEADS)
            pool.dma_start(bound[:, :], cst[:, 2, :]).then_inc(tables_in, 16)
            pool.dma_start(blocks[:, :, :].rearrange("p l i -> p (l i)"),
                           cst[:, 3:5, :].rearrange("p a i -> p (a i)")[:, 0:6 * B32]).then_inc(tables_in, 16)

            def chunk_in(c, buffers):
                pos = slice(None), slice(None), ds(c * C, C)
                for t, spilled_, here in buffers:
                    pool.dma_start(t[:, :, :], spilled_[pos].rearrange("h p t -> p h t")).then_inc(here, 16)
            k_, q_, v_ = (kc, k_spill, k_in), (qc, q_spill, q_in), (vc, v_spill, v_in)
            chunk_in(0, (k_, q_))

            def v_out_(n):
                pool.wait_ge(v_done, n + 1)
                pool.dma_start(dram(v_spill, n), rows(vv_, n)).then_inc(v_out, 16)
            loop(pool, HEADS, v_out_, last=False)
            pool.wait_ge(v_out, 16 * HEADS)
            chunk_in(0, (v_,))
            pool.sem_inc(u_freed, 1)
            pool.sem_inc(o_freed, 1)

            def o_to_dram(c):
                pool.wait_ge(dn_s["oc"], c * 2 + 4)
                pool.dma_start(o_spill[:, :, ds(c * C, C)].rearrange("h p t -> p h t"), ost[:, :, :]).then_inc(o_out, 16)
                pool.wait_ge(o_out, c * 16 + 16)
                pool.sem_inc(o_freed, 1)

            def u_to_dram(c):
                pool.wait_ge(u_s["done0"], c + 1)
                pool.dma_start(dram(u_spill, c), s0[:, :]).then_inc(u_out, 16)
                pool.wait_ge(u_out, c * 16 + 16)
                pool.sem_inc(u_freed, 1)

            with pool.Fori(0, NC - 1) as c:
                pool.wait_ge(dn_s["KS"], c * 2 + 2)
                pool.wait_ge(dn_s["qd"], c * 2 + 2)
                pool.wait_ge(dn_s["tv"], c * 2 + 2)
                chunk_in(c + 1, (k_, q_, v_))
                o_to_dram(c)
                u_to_dram(c)
            o_to_dram(NC - 1)

            pool.wait_ge(dn_done, 1)
            for n, hs in enumerate((slice(0, 2), slice(2, HEADS))):
                pool.dma_start(oo[:, hs, :], o_spill[hs].rearrange("h p t -> p h t")).then_inc(o_back[n], 16)
            u_to_dram(NC - 1)

            pool.wait_ge(g_s["norm"], HEADS)
            pool.dma_start(s2[:, :], b_s).then_inc(bs_in, 16)

            def spill_m(i):
                pool.wait_ge(y_s["out"], i + 1)
                pool.dma_start(dram(m_spill, i), s1[:, :]).then_inc(m_spilled, 16)
            loop(pool, 8, spill_m, last=False)
            pool.wait_ge(acc_done[1], BASE["gb"][1])
            for b in range(2):
                pool.dma_start(uu[:, :, HALF * b:HALF * b + HALF],
                               u_spill[:, :, HALF * b:HALF * b + HALF].rearrange("h p t -> p h t")).then_inc(u_back[b], 16)
            pool.wait_ge(m_spilled, 16 * 8)
            pool.wait_ge(b_s_["ready"], 8)

            def back_m(i):
                for b in range(2):
                    if not isinstance(i, int):
                        pool.wait_ge(yb_s["ready"], i * 2 + b - 1)
                    pool.dma_start(sc[b][:, :], m_spill[ds(i * 2 + b, 1)].rearrange("a p t -> p (a t)"))\
                        .then_inc(m_back[b], 16)
            loop(pool, 4, back_m, first=True, last=False)

            def back_h(m):
                pool.wait_ge(yb_s["m"], m + 1)
                pool.dma_start(h2[:, ds(m, 1), :].rearrange("p a t -> p (a t)"),
                               h_spill[ds(m, 1)].rearrange("a p t -> p (a t)")).then_inc(h_back, 16)
            pool.wait_ge(spilled, 16 * DT)
            loop(pool, 8, back_h, last=False)

        @block.scalar
        def _(act):
            A = nc.scalar.activation

            def split_hi(name, s, i, n):
                kt = kt_next(name, s, i, n)
                if kt:
                    u = BASE[name][s] + i
                    act.wait_ge(acc_done[s], u + 1)
                    act.wait_ge(w_loaded[s], (u + 2) * 16)
                    A(w_hi[s][:, 0:kt, :], w_raw[s][:, 0:kt, :], ACT.Copy).then_inc(w_hi_done[s], 1)

            def first_split(name):
                for s in range(2):
                    u = BASE[name][s]
                    act.wait_ge(w_loaded[s], 16 * (u + 1))
                    A(w_hi[s][:, :, :], w_raw[s][:, :, :], ACT.Copy).then_inc(w_hi_done[s], 1)

            def square_and_hi(nm, h, m, xh, vcol):
                stand_alone(act)
                act.wait_ge(nm.h, nm.h_tile + m + 1)
                if xh is not None:
                    A(xh[:, ds(m, 1), :].rearrange("p a t -> p (a t)"), h[:, ds(m, 1), :].rearrange("p a t -> p (a t)"),
                      ACT.Copy, scale=vecs[:, ds(m + vcol, 1)]).then_inc(nm.hi, 1)
                    stand_alone(act)
                wait(act, nm.added, nm.tile + m)
                A(s1[:, :], h[:, ds(m, 1), :].rearrange("p a t -> p (a t)"), ACT.Square).then_inc(nm.sq, 1)

            def root(nm):
                act.wait_ge(nm.sums, nm.n + 1)
                A(st[:, 0:DT], aux[0][:, 0:DT], ACT.Sqrt, bias=consts[:, 0:1], scale=1.0 / D).then_inc(nm.root, 1)

            def broadcast(nm):
                act.wait_ge(nm.bc, nm.n + 1)
                A(rstd[:, :], aux[0][:, :], ACT.Copy).then_inc(nm.rstd, 1)

            act.wait_ge(setup, 7)
            for k in range(DT):
                wait_x(act, k)
                A(xh1[:, k, :], h1[:, k, :], ACT.Copy, scale=vecs[:, V_N1 + k:V_N1 + k + 1]).then_inc(norms[0].hi, 1)
                if k == 0:
                    first_split("gu1_0")
                wait(act, norms[0].added, k)
                A(s1[:, :], h1[:, k, :], ACT.Square).then_inc(norms[0].sq, 1)

            def ffn(f, nm, nm_next, hh, h, xh, vcol):
                sg = ffns[f - 1]
                t0 = 0
                for g, n in enumerate(FF_GROUPS):
                    name = f"gu{f}_{g}"
                    def body(i):
                        t = i + t0
                        if g == 0 and isinstance(i, int) and i == 0:
                            root(nm)
                        split_hi(name, 0, i, n)
                        if g == 0 and isinstance(i, int) and i == 0:
                            broadcast(nm)
                        act.wait_ge(sg.gate, sg.tile + t + 1)
                        A(s0[:, :], s0[:, :], ACT.Silu).then_inc(sg.silu, 1)
                        split_hi(name, 1, i, n)
                        stand_alone(act)
                        act.wait_ge(sg.prod, sg.tile + t + 1)
                        A(hh[:, ds(i, 1), :].rearrange("p a t -> p (a t)"), s1[:, :], ACT.Copy).then_inc(sg.hi, 1)
                    loop(act, n, body, first=(g == 0))
                    t0 += n
                    dname = f"down{f}_{g}"
                    lastg = g == len(FF_GROUPS) - 1
                    def dbody(i):
                        for s in range(2):
                            split_hi(dname, s, i, DT // 2)
                            if lastg:
                                square_and_hi(nm_next, h, i * 2 + s, xh, vcol)
                    loop(act, DT // 2, dbody, first=lastg)

            ffn(1, norms[0], norms[1], hh1, h1, xhm, V_NM)

            def l2_inverse(j):
                for b in range(2):
                    act.wait_ge(l2_sum, j * 2 + b + 1)
                    A(sc2[b][:, :], aux[b][:, :], ACT.Ln, bias=consts[:, 2:3]).then_inc(l2_ln, 1)
                for b in range(2):
                    act.wait_ge(l2_ln, j * 2 + b + 1)
                    A(sc2[b][:, :], sc2[b][:, :], ACT.Exp, scale=-0.5,
                      bias=consts[:, 3:4] if b == 0 else 0.0).then_inc(l2_inv, 1)

            sc2 = [s1, s2]

            def beta_decay():
                act.wait_ge(ab["z"], 1)
                lane = slice(LANE_A, LANE_A + HEADS)
                A(ab_y[0:AB, :], ab_z[0:AB, :], ACT.Copy).then_inc(ab["act"], 1)
                A(ab_t[lane, :], ab_z[lane, :], ACT.Abs, bias=vecs[lane, V_DT:V_DT + 1]).then_inc(ab["act"], 1)
                A(st[lane, 0:1], vecs[lane, V_AL:V_AL + 1], ACT.Exp).then_inc(ab["act"], 1)
                act.wait_ge(ab["act"], 3)
                A(ab_t[lane, :], ab_t[lane, :], ACT.Exp, scale=-1.0).then_inc(ab["act"], 1)
                act.wait_ge(ab["act"], 4)
                A(ab_t[lane, :], ab_t[lane, :], ACT.Ln, bias=consts[lane, 4:5]).then_inc(ab["act"], 1)
                A(ab_y[0:HEADS, :], ab_y[0:HEADS, :], ACT.Sigmoid).then_inc(ab["act"], 1)

            def qk(i):
                f0 = isinstance(i, int) and i == 0
                if f0:
                    root(norms[1])
                split_hi("qk", 0, i, HEADS)
                if f0:
                    act.wait_ge(ab["w_in"], 16)
                    A(wab[1][:, :, :], wab[0][:, :, :], ACT.Copy).then_inc(ab["w"], 1)
                    broadcast(norms[1])
                else:
                    l2_inverse(i - 1)
                for b, dst in enumerate((qo, kk_)):
                    if b:
                        split_hi("qk", 1, i, HEADS)
                        if is_last(i, HEADS):
                            beta_decay()
                    row = dst[:, ds(i, 1), :].rearrange("p a t -> p (a t)")
                    stand_alone(act)
                    act.wait_ge(conv_done, i * 2 + b + 1)
                    A(row, row, ACT.Silu).then_inc(silu_done, 1)
                    stand_alone(act)
                    act.wait_ge(silu_done, i * 2 + b + 1)
                    act.wait_ge(l2_used, i * 2 + b + 1)
                    A(sc2[b][:, :], row, ACT.Square).then_inc(sq_done, 1)
            loop(act, HEADS, qk, first=True)

            act.sem_inc(dn_s["oc"], 2)

            def v(i):
                for s in range(2):
                    if not (s == 1 and is_last(i, 4)):
                        split_hi("v", s, i, 4)
                    if isinstance(i, int) and i == 0 and s == 0:
                        l2_inverse(HEADS - 1)
                    if not (isinstance(i, int) and i == 0 and s == 0):
                        silu_v(i * 2 + s - 1)
                if isinstance(i, int) and i == 0:
                    act.wait_ge(ab["gv"], 2)
                    A(eg[:, :], aux[1][:, 0:64], ACT.Exp).then_inc(ab["gact"], 1)
                    A(gl[:, :], aux[1][:, 64:128], ACT.Exp).then_inc(ab["gact"], 1)
                    A(kd[:, :], kd[:, :], ACT.Exp).then_inc(ab["gact"], 1)
            def silu_v(n):
                row = vv_[:, ds(n, 1), :].rearrange("p a t -> p (a t)")
                stand_alone(act)
                act.wait_ge(v_conv, n + 1)
                A(row, row, ACT.Silu).then_inc(v_done, 1)

            loop(act, 4, v, first=True)
            silu_v(HEADS - 1)

            def gelus(c):
                stand_alone(act)
                act.wait_ge(u_s["arg0"], c + 1)
                A(s0[:, :], s0[:, :], ACT.Gelu).then_inc(u_s["done0"], 1)
                stand_alone(act)
                act.wait_ge(u_s["arg1"], c + 1)
                A(gv[:, ds(c, 1), :].rearrange("p a t -> p (a t)"), s1[:, :], ACT.Gelu).then_inc(u_s["done1"], 1)

            def split_hi_1(c):
                act.wait_ge(acc_done[1], BASE["uv"][1] + c)
                act.wait_ge(w_loaded[1], (BASE["uv"][1] + c + 1) * 16)
                A(w_hi[1][:, :, :], w_raw[1][:, :, :], ACT.Copy).then_inc(w_hi_done[1], 1)

            def delta(c):
                B = lambda n, g: dn[n, g][:, :, :]
                for g in range(2):
                    act.wait_ge(dn_s["G"], c * 2 + g + 1)
                    A(B("V", g), bank[g, 1], ACT.Exp).then_inc(dn_s["EG"], 1)
                split_hi_1(c)
                for g in range(2):
                    act.wait_ge(dn_s["arg"], c * 2 + g + 1)
                    A(B("D", g), B("X", g), ACT.Exp).then_inc(dn_s["D"], 1)
                for g in range(2):
                    act.wait_ge(dn_s["tv"], c * 2 + g + 1)
                    act.wait_ge(dn_s["qd"], c * 2 + g + 1)
                    A(B("V", g), bank[g, 1], ACT.Copy).then_inc(dn_s["V"], 1)
                if not (isinstance(c, int) and c == 0):
                    gelus(c - 1)
                for g in range(2):
                    act.wait_ge(dn_s["x5"], c * 2 + g + 1)
                    for b in (1, 3):
                        last = A(dn["Xc", g][quad[b], :, :], bankc[g, 1][quad[b], :, :], ACT.Copy)
                    last.then_inc(dn_s["X5"], 1)
                for g in range(2):
                    act.wait_ge(dn_s["T"], (c * 5 + 4) * 2 + g + 1)
                    for b, q in enumerate(quad):
                        A(dn["TT", g][q, :, q], dn["TTc", g][q, :, :], ACT.Copy)
                    for b in range(2):
                        A(dn["Tf", g][quad[b], :, quad[b]], dn["Tc", g][quad[b], :, :], ACT.Copy)
                for g in range(2):
                    act.wait_ge(dn_s["u5"], c * 2 + g + 1)
                    A(dn["TT", g][quad[0], :, quad[1]], bankc[g, 0][quad[0], :, :], ACT.Copy, scale=-1.0)
                    A(dn["TT", g][quad[2], :, quad[3]], bankc[g, 0][quad[2], :, :], ACT.Copy, scale=-1.0)
                    A(dn["Tf", g][quad[1], :, quad[0]], bankt[g, 0][quad[1], :, :], ACT.Copy, scale=-1.0)\
                        .then_inc(dn_s["T5"], 1)
                for g in range(2):
                    act.wait_ge(dn_s["x6"], c * 2 + g + 1)
                    A(dn["X6", g][64:128, :, :], bank64[g, 1][64:128, :, :], ACT.Copy).then_inc(dn_s["X6"], 1)
                for g in range(2):
                    act.wait_ge(dn_s["u6"], c * 2 + g + 1)
                    A(dn["TT", g][0:64, :, 64:128], bank64[g, 0][0:64, :, :], ACT.Copy, scale=-1.0)\
                        .then_inc(dn_s["T6"], 1)
                split_hi("uv", 0, c, 0)
                act.wait_ge(o_freed, c + 1)
                for g in range(2):
                    act.wait_ge(dn_s["o"], c * 2 + g + 1)
                    A(ost[:, HG * g:HG * g + HG, :], bank[g, 1], ACT.Copy).then_inc(dn_s["oc"], 1)
            delta(0)
            act.wait_ge(v_out, 16 * HEADS)
            with act.Fori(1, NC) as c:
                delta(c)
            split_hi("uv", 1, NC - 1, 0)
            gelus(NC - 1)

            def square_o(m):
                if not (isinstance(m, int) and m == 0):
                    stand_alone(act)
                    act.wait_ge(g_s["norm"], m)
                A(s2[:, :], oo[:, ds(m, 1), :].rearrange("p a t -> p (a t)"), ACT.Square).then_inc(g_s["sq"], 1)

            def gate(i):
                for s in range(2):
                    m = i * 2 + s
                    split_hi("g", s, i, 4)
                    act.wait_ge(g_s["sum"], m + 1)
                    A(s2[:, :], aux[0][:, :], ACT.Ln, scale=1.0 / P, bias=consts[:, 0:1]).then_inc(g_s["ln"], 1)
                    act.wait_ge(g_s["ln"], m + 1)
                    A(s2[:, :], s2[:, :], ACT.Exp, scale=-0.5).then_inc(g_s["inv"], 1)
                    act.wait_ge(g_s["gate"], m + 1)
                    A(sc[s][:, :], sc[s][:, :], ACT.Silu).then_inc(g_s["silu"], 1)
                    if isinstance(i, int) and m == 0:
                        act.wait_ge(o_back[1], 16)
                    if not (isinstance(i, int) and m == HEADS - 1):
                        square_o(m + 1)
                    stand_alone(act)
                    act.wait_ge(g_s["prod"], m + 1)
                    A(oh[:, ds(m, 1), :].rearrange("p a t -> p (a t)"), sc[s][:, :], ACT.Copy).then_inc(g_s["hi"], 1)
            act.wait_ge(o_back[0], 16)
            square_o(0)
            loop(act, 4, gate, first=True)

            def gaya(i):
                split_hi("gaya", 0, i, 8)
                act.wait_ge(y_s["gate"], i + 1)
                A(s0[:, :], s0[:, :], ACT.Sigmoid).then_inc(y_s["sig"], 1)
                split_hi("gaya", 1, i, 8)
            loop(act, 8, gaya)

            def gb(i):
                for s in range(2):
                    n = i * 2 + s
                    split_hi("gb", s, i, 4)
                    stand_alone(act)
                    act.wait_ge(b_s_["gate"], n + 1)
                    row = sig_b[:, ds(n, 1), :].rearrange("p a t -> p (a t)")
                    A(row, row, ACT.Sigmoid)
                    act.wait_ge(b_s_["var"], n + 1)
                    A(st[:, 10:11], st[:, 9:10], ACT.Sqrt, bias=consts[:, 1:2]).then_inc(b_s_["root"], 1)
                    if not is_last(n, 2 * 4):
                        copy_v(n + 1)
                    if not (isinstance(n, int) and n == 0):
                        mix_hi(n - 1)

            def copy_v(n):
                if not (isinstance(n, int) and n == 0):
                    stand_alone(act)
                    act.wait_ge(b_s_["tr"], n)
                A(s0[:, :].rearrange("p (m t) -> p m t", m=DT), gv[:, :, ds(n * C, C)], ACT.Copy)\
                    .then_inc(b_s_["copy"], 1)

            def mix_hi(n):
                stand_alone(act)
                act.wait_ge(b_s_["prod"], n + 1)
                A(sh[:, :, ds(n * C, C)], uu[:, :, ds(n * C, C)], ACT.Copy).then_inc(b_s_["hi"], 1)
            act.wait_ge(u_s["done1"], 8)
            act.wait_ge(y_s["out"], 8)
            copy_v(0)
            loop(act, 4, gb, first=True)
            mix_hi(7)

            def yb(i):
                for s in range(2):
                    n = i * 2 + s
                    split_hi("yb", s, i, 4)
                    stand_alone(act)
                    act.wait_ge(yb_s["m"], n + 1)
                    A(mh[:, ds(n, 1), :].rearrange("p a t -> p (a t)"), sc[s][:, :], ACT.Copy).then_inc(yb_s["hi"], 1)
            loop(act, 4, yb)

            def wo(i):
                for s in range(2):
                    split_hi("wo", s, i, 4)
                    square_and_hi(norms[2], h2, i * 2 + s, xh2, V_N2)
            loop(act, 4, wo, first=True)

            ffn(2, norms[2], norms[3], hh2, h2, None, None)
            root(norms[3])
            broadcast(norms[3])
            for k in range(DT):
                act.wait_ge(norms[3].ready, norms[3].tile + k + 1)
                act.dma_start(out[k], h2[:, k, :]).then_inc(out_sem, 16)

        @block.vector
        def _(dve):
            TT, TS, STT = nc.vector.tensor_tensor, nc.vector.tensor_scalar, nc.vector.scalar_tensor_tensor
            mult, add, sub = ALU.mult, ALU.add, ALU.subtract

            def split_lo(name, s, i, n):
                kt = kt_next(name, s, i, n)
                if kt:
                    u = BASE[name][s] + i
                    dve.wait_ge(w_hi_done[s], u + 2)
                    TT(w_lo[s][:, 0:kt, :], w_raw[s][:, 0:kt, :], w_hi[s][:, 0:kt, :].bitcast(f32), sub)\
                        .then_inc(w_ready[s], 1)

            def first_split(name):
                for s in range(2):
                    dve.wait_ge(w_hi_done[s], BASE[name][s] + 1)
                    TT(w_lo[s][:, :, :], w_raw[s][:, :, :], w_hi[s][:, :, :].bitcast(f32), sub)\
                        .then_inc(w_ready[s], 1)

            def row(t, m):
                return t[:, ds(m, 1), :].rearrange("p a t -> p (a t)")

            def statistics(nm, h, m, vcol, xh, xl):
                if xh is not None:
                    dve.wait_ge(nm.hi, nm.tile + m + 1)
                    STT(row(xl, m), row(h, m), vecs[:, ds(m + vcol, 1)], row(xh, m).bitcast(f32), mult, sub)\
                        .then_inc(nm.ready, 1)
                dve.wait_ge(nm.sq, nm.tile + m + 1)
                wait(dve, nm.added, nm.tile + m)
                TT(s2[:, :], s2[:, :], s1[:, :], add).then_inc(nm.added, 1)

            def zero_sum(nm):
                nc.vector.memset(s2[:, :], 0.0).then_inc(nm.zero, 1)
                dve.wait_ge(nm.zero, nm.n + 1)

            def inverse(nm):
                dve.wait_ge(nm.root, nm.n + 1)
                nc.vector.reciprocal(st[:, 0:DT], st[:, 0:DT]).then_inc(nm.inv, 1)
                dve.wait_ge(nm.inv, nm.n + 1)
                TT(s2[:, :].rearrange("p (c i) -> p c i", c=NC), bc_mid(ident[:, :], NC), bc_row(st[:, 0:DT], DT), mult)\
                    .then_inc(nm.diag, 1)

            zero_sum(norms[0])

            def add_square(k):
                dve.wait_ge(norms[0].sq, k + 1)
                wait(dve, norms[0].added, k)
                TT(s2[:, :], s2[:, :], s1[:, :], add).then_inc(norms[0].added, 1)
            for k in range(DT):
                wait_x(dve, k)
                dve.wait_ge(norms[0].hi, k + 1)
                STT(xl1[:, k, :], h1[:, k, :], vecs[:, V_N1 + k:V_N1 + k + 1], xh1[:, k, :].bitcast(f32), mult, sub)\
                    .then_inc(norms[0].ready, 1)
                if k == 0:
                    first_split("gu1_0")
                add_square(k)
            dve.wait_ge(cst_in, 32)

            def ffn(f, nm, nm_next, hh, hl, h, vcol, xh, xl):
                sg = ffns[f - 1]
                t0 = 0
                for g, n in enumerate(FF_GROUPS):
                    name = f"gu{f}_{g}"
                    def body(i):
                        t = i + t0
                        u = [BASE[name][s] + i for s in range(2)]
                        f0 = g == 0 and isinstance(i, int) and i == 0
                        if f0:
                            inverse(nm)
                        split_lo(name, 0, i, n)
                        if f0:
                            dve.wait_ge(nm.rstd, nm.n + 1)
                        dve.wait_ge(acc_done[0], u[0] + 1)
                        TT(s0[:, :], acc[0][:, :], rstd[:, :], mult).then_inc(sg.gate, 1)
                        dve.wait_ge(sg.gate, sg.tile + t + 1)
                        dve.sem_inc(acc_free[0], 1)
                        split_lo(name, 1, i, n)
                        dve.wait_ge(acc_done[1], u[1] + 1)
                        wait(dve, sg.ready, sg.tile + t)
                        TT(s1[:, :], acc[1][:, :], rstd[:, :], mult).then_inc(acc_free[1], 1)
                        dve.wait_ge(acc_free[1], u[1] + 1)
                        dve.wait_ge(sg.silu, sg.tile + t + 1)
                        TT(s1[:, :], s0[:, :], s1[:, :], mult).then_inc(sg.prod, 1)
                        dve.wait_ge(sg.hi, sg.tile + t + 1)
                        TT(row(hl, i), s1[:, :], row(hh, i).bitcast(f32), sub).then_inc(sg.ready, 1)
                    loop(dve, n, body, first=(g == 0))
                    t0 += n
                    dname = f"down{f}_{g}"
                    lastg = g == len(FF_GROUPS) - 1
                    if lastg:
                        zero_sum(nm_next)
                    def dbody(i):
                        for s in range(2):
                            m = i * 2 + s
                            u = BASE[dname][s] + i
                            split_lo(dname, s, i, DT // 2)
                            dve.wait_ge(acc_done[s], u + 1)
                            ins = STT(row(h, m), acc[s][:, :], 0.5, row(h, m), mult, add)
                            ins.then_inc(acc_free[s], 1)
                            if lastg:
                                dve.wait_ge(acc_free[s], u + 1)
                                dve.sem_inc(nm_next.h, 1)
                                statistics(nm_next, h, m, vcol, xh, xl)
                    loop(dve, DT // 2, dbody, first=lastg)

            ffn(1, norms[0], norms[1], hh1, hl1, h1, V_NM, xhm, xlm)

            def conv(ch, s, dst, wrow):
                ch.link(TT(s0p[:, 3:3 + SEQ], acc[s][:, :], rstd[:, :], mult))
                dve.sem_inc(acc_free[s], 1)
                ch.link(TS(dst, s0p[:, 3:3 + SEQ], vecs[:, ds(wrow * TAPS + (V_CW + TAPS - 1), 1)], None, mult))
                for j in range(TAPS - 2, -1, -1):
                    ins = STT(dst, s0p[:, j:j + SEQ], vecs[:, ds(wrow * TAPS + (V_CW + j), 1)], dst, mult, add)
                    if j:
                        ch.link(ins)
                return ins

            def l2_scale(j):
                for b, dst in enumerate((qo, kk_)):
                    dve.wait_ge(l2_inv, j * 2 + b + 1)
                    dve.wait_ge(silu_done, j * 2 + b + 1)
                    TT(row(dst, j), row(dst, j), sc2[b][:, :], mult).then_inc(l2_used, 1)

            sc2 = [s1, s2]

            def log_alpha():
                lane = slice(LANE_A, LANE_A + HEADS)
                dve.wait_ge(ab["z"], 1)
                dve.wait_ge(ab["act"], 6)
                TS(ab_y[lane, :], ab_z[lane, :], vecs[lane, V_DT:V_DT + 1], 0.0, add, ALU.max).then_inc(ab["dve"], 1)
                dve.wait_ge(ab["dve"], 2)
                TT(ab_y[lane, :], ab_y[lane, :], ab_t[lane, :], add).then_inc(ab["dve"], 1)
                dve.wait_ge(ab["dve"], 3)
                TS(ab_y[lane, :], ab_y[lane, :], st[lane, 0:1], -1.0, mult, mult).then_inc(ab["dve"], 1)

            def qk(i):
                f0 = isinstance(i, int) and i == 0
                ch = Chain(dve, s_conv, i, 8)
                if f0:
                    inverse(norms[1])
                split_lo("qk", 0, i, HEADS)
                if f0:
                    dve.wait_ge(spilled, 16 * DT)
                    nc.vector.memset(s0p[:, 0:3], 0.0).then_inc(ab["dve"], 1)
                    dve.wait_ge(ab["dve"], 1)
                    dve.wait_ge(ab["w"], 1)
                    TT(wab[2][:, :, :], wab[0][:, :, :], wab[1][:, :, :].bitcast(f32), sub).then_inc(ab["w"], 1)
                    dve.sem_inc(l2_used, 2)
                    dve.wait_ge(norms[1].rstd, norms[1].n + 1)
                dve.wait_ge(acc_done[0], BASE["qk"][0] + i + 1)
                conv(ch, 0, row(qo, i), i).then_inc(conv_done, 1)
                if not f0:
                    l2_scale(i - 1)
                split_lo("qk", 1, i, HEADS)
                dve.wait_ge(acc_done[1], BASE["qk"][1] + i + 1)
                conv(ch, 1, row(kk_, i), i + HEADS).then_inc(conv_done, 1)
                ch.end()
                if is_last(i, HEADS):
                    log_alpha()
                if f0:
                    dve.wait_ge(ab["mm"], 1)
                    TT(ab_z[0:AB, :], aux[0][0:AB, :], rstd[0:AB, :], mult).then_inc(ab["z"], 1)
            loop(dve, HEADS, qk, first=True)

            def cols(t, g, c):
                return t[:, ds(c * HEADS + HG * g, HG)].unsqueeze(2).to_broadcast([P, HG, P])

            def log_decay(c):
                for g in range(2):
                    TT(dn["LU", g][:, :, :], bc_mid(upper[:, :], HG), cols(la, g, c), mult).then_inc(dn_s["laU"], 1)

            def delta_setup():
                dve.wait_ge(qk_spilled, 2 * 16 * HEADS)
                for g in range(2):
                    nc.vector.memset(dn["TT", g][:, :, :], 0.0)
                    nc.vector.memset(dn["Tf", g][0:64, :, :], 0.0)
                    nc.vector.memset(dn["S", g][:, :, :], 0.0).then_inc(dn_s["S"], 1)
                nc.vector.memset(la[:, NC * HEADS:], 0.0).then_inc(dn_s["laU"], 1)
                log_decay(0)
                dve.wait_ge(dn_s["S"], 2)
                dve.wait_ge(dn_s["laU"], 1)

            def v(i):
                for s in range(2):
                    ch = Chain(dve, v_chain, i * 2 + s, 4)
                    if not (s == 1 and is_last(i, 4)):
                        split_lo("v", s, i, 4)
                    dve.wait_ge(acc_done[s], BASE["v"][s] + i + 1)
                    conv(ch, s, row(vv_, i * 2 + s), i * 2 + s + 2 * HEADS).then_inc(v_conv, 1)
                    dve.wait_ge(v_conv, i * 2 + s + 1)
                    ch.end()
                    if isinstance(i, int) and i == 0 and s == 0:
                        l2_scale(HEADS - 1)
                        dve.wait_ge(ab["t"], 1)
                        t = aux[0][:, 0:512].rearrange("p (c x) -> p c x", c=NC)
                        nc.vector.tensor_copy(beta[:, :].rearrange("p (c h) -> p c h", c=NC), t[:, :, 0:HEADS])\
                            .then_inc(ab["cols"], 1)
                        nc.vector.tensor_copy(la[:, 0:NC * HEADS].rearrange("p (c h) -> p c h", c=NC), t[:, :, LANE_A:LANE_A + HEADS])\
                            .then_inc(ab["cols"], 1)
                if isinstance(i, int) and i == 0:
                    dve.wait_ge(ab["g"], 1)
                    nc.vector.tensor_copy(gcol[:, :], aux[1][:, 0:64]).then_inc(ab["gv"], 1)
                    dve.wait_ge(ab["gv"], 1)
                    TT(kd[:, :], aux[1][:, 64:128], gcol[:, :], sub).then_inc(ab["gv"], 1)
                    delta_setup()
            loop(dve, 4, v, first=True)

            def split_lo_1(c):
                dve.wait_ge(w_hi_done[1], BASE["uv"][1] + c + 1)
                TT(w_lo[1][:, :, :], w_raw[1][:, :, :], w_hi[1][:, :, :].bitcast(f32), sub).then_inc(w_ready[1], 1)

            def block(n, part=slice(0, P)):
                w = part.stop - part.start
                return blocks[part, n, :].unsqueeze(1).to_broadcast([w, HG, B32])

            def heads(g):
                return slice(HG * g, HG * g + HG)

            def delta(c):
                B = lambda n, g: dn[n, g][:, :, :]
                for g in range(2):
                    dve.wait_ge(dn_s["EG"], c * 2 + g + 1)
                    TT(B("X", g), bank[g, 1], cols(gcol, g, c), sub).then_inc(dn_s["argA"], 1)
                for g in range(2):
                    dve.wait_ge(dn_s["argA"], c * 2 + g + 1)
                    TT(B("X", g), B("X", g), bc_mid(bound[:, :], HG), ALU.min).then_inc(dn_s["arg"], 1)
                for g in range(2):
                    dve.wait_ge(dn_s["tk"], c * 2 + g + 1)
                    TT(B("Ktm", g), bank[g, 0], cols(kd, g, c), mult).then_inc(dn_s["Kd"], 1)
                for g in range(2):
                    dve.wait_ge(dn_s["D"], c * 2 + g + 1)
                    dve.wait_ge(dn_s["kk"], c * 2 + g + 1)
                    TT(B("NT", g), bank[g, 1], B("D", g), mult).then_inc(dn_s["NTa"], 1)
                for g in range(2):
                    dve.wait_ge(dn_s["qk"], c * 2 + g + 1)
                    TT(B("AT", g), bank[g, 0], B("D", g), mult).then_inc(dn_s["AT"], 1)
                for g in range(2):
                    dve.wait_ge(dn_s["NTa"], c * 2 + g + 1)
                    TT(B("NT", g), B("NT", g), cols(beta, g, c), mult).then_inc(dn_s["NT"], 1)
                for g in range(2):
                    dve.wait_ge(dn_s["AT"], c * 2 + g + 1)
                    TT(B("D", g), qc[:, heads(g), :], B("V", g), mult).then_inc(dn_s["qd"], 1)
                for g in range(2):
                    dve.wait_ge(dn_s["NT"], c * 2 + g + 1)
                    for q in quad:
                        last = TT(dn["TTc", g][q, :, :], dn["NT", g][q, :, q], block(1, q), mult)
                    last.then_inc(dn_s["L0"], 1)
                for g in range(2):
                    dve.wait_ge(dn_s["L0"], c * 2 + g + 1)
                    TT(B("TTc", g), block(0), B("TTc", g), sub).then_inc(dn_s["TT"], 1)
                for g in range(2):
                    dve.wait_ge(dn_s["TT"], c * 10 + g + 1)
                    nc.vector.transpose(flat(dn["Tc", g]), flat(dn["TTc", g])).then_inc(dn_s["T"], 1)
                for g in range(2):
                    dve.wait_ge(dn_s["KS"], c * 2 + g + 1)
                    TT(B("X", g), bank[g, 0], cols(eg, g, c), mult).then_inc(dn_s["eKS"], 1)
                for g in range(2):
                    dve.wait_ge(dn_s["eKS"], c * 2 + g + 1)
                    dve.wait_ge(dn_s["V"], c * 2 + g + 1)
                    TT(B("V", g), B("V", g), B("X", g), sub).then_inc(dn_s["Rr"], 1)
                for l in range(1, 5):
                    for g in range(2):
                        dve.wait_ge(dn_s["xp"], (c * 4 + l - 1) * 2 + g + 1)
                        TT(B("Xc", g), bankc[g, 1], block(1 + l), mult).then_inc(dn_s["X"], 1)
                    for g in range(2):
                        dve.wait_ge(dn_s["up"], (c * 4 + l - 1) * 2 + g + 1)
                        dve.wait_ge(dn_s["T"], (c * 5 + l - 1) * 2 + g + 1)
                        TT(B("TTc", g), B("TTc", g), bankc[g, 0], sub).then_inc(dn_s["TT"], 1)
                    for g in range(2):
                        dve.wait_ge(dn_s["TT"], (c * 5 + l) * 2 + g + 1)
                        nc.vector.transpose(flat(dn["Tc", g]), flat(dn["TTc", g])).then_inc(dn_s["T"], 1)
                    if l == 1:
                        split_lo_1(c)
                    if l == 2:
                        log_decay(c + 1)
                dve.wait_ge(acc_done[0], BASE["uv"][0] + c + 1)
                dve.wait_ge(u_freed, c + 1)
                TT(s0[:, :], acc[0][:, :], rstd[:, :], mult).then_inc(u_s["arg0"], 1)
                dve.wait_ge(u_s["arg0"], c + 1)
                dve.sem_inc(acc_free[0], 1)
                for g in range(2):
                    dve.wait_ge(dn_s["TR"], c * 2 + g + 1)
                    TT(B("X", g), bank[g, 0], cols(beta, g, c), mult).then_inc(dn_s["vn"], 1)
                split_lo("uv", 0, c, 0)
                for g in range(2):
                    dve.wait_ge(dn_s["o"], c * 2 + g + 1)
                    dve.wait_ge(dn_s["S"], c * 2 + g + 1)
                    TT(B("S", g), B("S", g), cols(gl, g, c), mult).then_inc(dn_s["Sg"], 1)
                for g in range(2):
                    dve.wait_ge(dn_s["Sg"], c * 2 + g + 1)
                    dve.wait_ge(dn_s["Kv"], c * 2 + g + 1)
                    TT(B("S", g), B("S", g), bank[g, 0], add).then_inc(dn_s["S"], 1)
                dve.wait_ge(acc_done[1], BASE["uv"][1] + c + 1)
                if not (isinstance(c, int) and c == 0):
                    dve.wait_ge(u_s["done1"], c)
                TT(s1[:, :], acc[1][:, :], rstd[:, :], mult).then_inc(u_s["arg1"], 1)
                dve.wait_ge(u_s["arg1"], c + 1)
                dve.sem_inc(acc_free[1], 1)

            def flat(t):
                return t[:, :, :].rearrange("p h i -> p (h i)")
            dve.wait_ge(tables_in, 48)
            delta(0)
            with dve.Fori(1, NC) as c:
                delta(c)
            split_lo("uv", 1, NC - 1, 0)
            dve.wait_ge(dn_s["S"], 2 * NC + 2)
            dve.wait_ge(dn_s["oc"], 2 * NC + 2)
            dve.sem_inc(dn_done, 1)
            dve.wait_ge(u_freed, NC + 1)
            dve.wait_ge(u_s["done1"], NC)


            def gate(i):
                for s in range(2):
                    m = i * 2 + s
                    split_lo("g", s, i, 4)
                    dve.wait_ge(acc_done[s], BASE["g"][s] + i + 1)
                    TT(sc[s][:, :], acc[s][:, :], rstd[:, :], mult).then_inc(g_s["gate"], 1)
                    dve.wait_ge(g_s["gate"], m + 1)
                    dve.sem_inc(acc_free[s], 1)
                    dve.wait_ge(g_s["inv"], m + 1)
                    TT(row(oo, m), row(oo, m), s2[:, :], mult).then_inc(g_s["norm"], 1)
                    dve.wait_ge(g_s["norm"], m + 1)
                    dve.wait_ge(g_s["silu"], m + 1)
                    STT(sc[s][:, :], row(oo, m), vecs[:, V_DN:V_DN + 1], sc[s][:, :], mult, mult).then_inc(g_s["prod"], 1)
                    dve.wait_ge(g_s["hi"], m + 1)
                    TT(row(ol, m), sc[s][:, :], row(oh, m).bitcast(f32), sub).then_inc(g_s["ready"], 1)
            loop(dve, 4, gate, first=True)
            dve.wait_ge(g_s["ready"], 8)

            def gaya(i):
                split_lo("gaya", 0, i, 8)
                dve.wait_ge(acc_done[0], BASE["gaya"][0] + i + 1)
                TT(s0[:, :], acc[0][:, :], rstd[:, :], mult).then_inc(y_s["gate"], 1)
                dve.wait_ge(y_s["gate"], i + 1)
                dve.sem_inc(acc_free[0], 1)
                split_lo("gaya", 1, i, 8)
                dve.wait_ge(acc_done[1], BASE["gaya"][1] + i + 1)
                dve.wait_ge(y_s["sig"], i + 1)
                if isinstance(i, int) and i == 0:
                    dve.wait_ge(tables_in, 48)
                    nc.vector.memset(wsT[CH:P, :, 0:CH], 0.0).then_inc(u_s["w"], 1)
                else:
                    dve.wait_ge(m_spilled, i * 16)
                TT(s1[:, :], acc[1][:, :], s0[:, :], mult).then_inc(y_s["out"], 1)
                dve.wait_ge(y_s["out"], i + 1)
                dve.sem_inc(acc_free[1], 1)
                if isinstance(i, int) and i == 7:
                    dve.wait_ge(bs_in, 16)
                    dve.wait_ge(u_s["rows"], 1)
                    for m in range(DT):
                        STT(s2[:, m * P:m * P + P], aux[1][:, m * P:m * P + P], vecs[:, V_SB + m:V_SB + m + 1],
                            s2[:, m * P:m * P + P], mult, add).then_inc(u_s["bias"], 1)

            CH = 64
            loop(dve, 8, gaya, first=True)
            dve.wait_ge(u_s["bias"], 8)
            dve.wait_ge(m_spilled, 16 * 8)

            def mix_out(n):
                at_n = slice(None), slice(None), ds(n * C, C)
                ch = Chain(dve, b_s_["chain"], n, 2)
                dve.wait_ge(b_s_["mix"], n + 1)
                ch.link(TT(gv[at_n], aux[1][:, :].rearrange("p (m t) -> p m t", m=DT),
                           bc_row(vecs[:, V_SW:V_SW + DT], DT), mult))
                ch.link(TT(gv[at_n], gv[at_n], s2[:, :].rearrange("p (m t) -> p m t", m=DT), add))
                if isinstance(n, int) and n == 0:
                    dve.wait_ge(u_back[0], 16)
                    dve.wait_ge(u_back[1], 16)
                TT(uu[at_n], gv[at_n], uu[at_n], mult).then_inc(b_s_["prod"], 1)
                dve.wait_ge(b_s_["hi"], n + 1)
                TT(sl[at_n], uu[at_n], sh[at_n].bitcast(f32), sub).then_inc(b_s_["ready"], 1)

            def gb(i):
                for s in range(2):
                    n = i * 2 + s
                    f0 = isinstance(i, int) and n == 0
                    dve.wait_ge(acc_done[s], BASE["gb"][s] + i + 1)
                    TT(row(sig_b, n), acc[s][:, :], rstd[:, :], mult).then_inc(b_s_["gate"], 1)
                    dve.wait_ge(b_s_["gate"], n + 1)
                    dve.sem_inc(acc_free[s], 1)
                    dve.wait_ge(b_s_["tr"], n + 1)
                    for b in range(2):
                        last = nc.vector.bn_stats(bnst[:, 6 * b:6 * b + 6], aux[0][:, HALF * b:HALF * b + HALF])
                    last.then_inc(b_s_["bn"], 1)
                    stand_alone(dve)
                    dve.wait_ge(b_s_["bn"], n + 1)
                    nc.vector.bn_aggr(st[:, 8:10], bnst[:, 0:12]).then_inc(b_s_["var"], 1)
                    split_lo("gb", s, i, 4)
                    dve.wait_ge(b_s_["root"], n + 1)
                    nc.vector.reciprocal(st[:, 10:11], st[:, 10:11]).then_inc(b_s_["inv"], 1)
                    dve.wait_ge(b_s_["inv"], n + 1)
                    dve.wait_ge(b_s_["var"], n + 1)
                    if not f0:
                        dve.wait_ge(b_s_["mix"], n)
                    TS(s1[:, :], aux[0][:, :], st[:, 8:9], st[:, 10:11], sub, mult).then_inc(b_s_["z"], 1)
                    if not f0:
                        mix_out(n - 1)
            loop(dve, 4, gb, first=True)
            mix_out(7)
            dve.wait_ge(b_s_["ready"], 8)

            def yb(i):
                for s in range(2):
                    n = i * 2 + s
                    split_lo("yb", s, i, 4)
                    dve.wait_ge(acc_done[s], BASE["yb"][s] + i + 1)
                    TT(row(sig_b, n), row(sig_b, n), acc[s][:, :], mult).then_inc(yb_s["t"], 1)
                    dve.wait_ge(yb_s["t"], n + 1)
                    dve.sem_inc(acc_free[s], 1)
                    dve.wait_ge(m_back[s], i * 16 + 16)
                    TT(sc[s][:, :], sc[s][:, :], row(sig_b, n), add).then_inc(yb_s["m"], 1)
                    dve.wait_ge(yb_s["hi"], n + 1)
                    TT(row(ml, n), sc[s][:, :], row(mh, n).bitcast(f32), sub).then_inc(yb_s["ready"], 1)
            loop(dve, 4, yb)
            dve.wait_ge(yb_s["ready"], 8)
            zero_sum(norms[2])

            def wo(i):
                for s in range(2):
                    m = i * 2 + s
                    split_lo("wo", s, i, 4)
                    dve.wait_ge(acc_done[s], BASE["wo"][s] + i + 1)
                    dve.wait_ge(h_back, 16 * DT)
                    TT(row(h2, m), row(h2, m), acc[s][:, :], add).then_inc(norms[2].h, 1)
                    dve.wait_ge(norms[2].h, norms[2].h_tile + m + 1)
                    dve.sem_inc(acc_free[s], 1)
                    statistics(norms[2], h2, m, V_N2, xh2, xl2)
            loop(dve, 4, wo, first=True)

            ffn(2, norms[2], norms[3], hh2, hl2, h2, 0, None, None)
            inverse(norms[3])
            dve.wait_ge(norms[3].rstd, norms[3].n + 1)
            for k in range(DT):
                STT(h2[:, k, :], h2[:, k, :], vecs[:, V_NF + k:V_NF + k + 1], rstd[:, :], mult, mult)\
                    .then_inc(norms[3].ready, 1)

        @block.tensor
        def _(pe):
            MM = nc.tensor.matmul

            def products(s, b, k, kt, xh, xl):
                o = acc[s][:, HALF * b:HALF * b + HALF]
                a, z = (t[:, k, HALF * b:HALF * b + HALF] for t in (xh, xl))
                MM(o, w_hi[s][:, k, :], a, start=(k == 0), stop=False)
                MM(o, w_hi[s][:, k, :], z, start=False, stop=False)
                return MM(o, w_lo[s][:, k, :], a, start=False, stop=(k == kt - 1))

            def unit(name, s, i, xh, xl, kt=8, ready=None, between={}):
                u = BASE[name][s] + i
                pe.wait_ge(w_ready[s], u + 1)
                wait(pe, acc_free[s], u)
                if ready is not None:
                    for k in range(kt):
                        pe.wait_ge(ready[0], ready[1] + k + 1)
                        for b in range(2):
                            last = products(s, b, k, kt, xh, xl)
                else:
                    for b in range(2):
                        for k in range(kt):
                            if (b, k) in between:
                                between[b, k]()
                            last = products(s, b, k, kt, xh, xl)
                last.then_inc(acc_done[s], 1)

            def sums(nm):
                pe.wait_ge(nm.added, nm.tile + DT)
                for c in range(NC):
                    last = MM(aux[0][:, c:c + 1], s2[:, c * P:c * P + P], ones[:, 0:1], start=True, stop=True)
                last.then_inc(nm.sums, 1)

            def spread(nm):
                pe.wait_ge(nm.diag, nm.n + 1)
                for b in range(2):
                    last = MM(aux[0][:, HALF * b:HALF * b + HALF], ones[:, :], s2[:, HALF * b:HALF * b + HALF],
                              start=True, stop=True)
                last.then_inc(nm.bc, 1)

            def norm_between(nm):
                return {(0, 3): lambda: sums(nm), (1, 3): lambda: spread(nm)}

            def first_units(nm, xh, xl):
                for s in range(2):
                    pe.wait_ge(w_ready[s], 1)
                for k in range(DT):
                    pe.wait_ge(nm.ready, k + 1)
                    for s in range(2):
                        for b in range(2):
                            last = products(s, b, k, DT, xh, xl)
                        if k == DT - 1:
                            last.then_inc(acc_done[s], 1)
                sums(nm)
                spread(nm)

            def ffn(f, nm, hh, hl, xh, xl):
                sg = ffns[f - 1]
                t0 = 0
                for g, n in enumerate(FF_GROUPS):
                    name = f"gu{f}_{g}"
                    def body(i):
                        f0 = g == 0 and isinstance(i, int) and i == 0
                        if f0 and f == 1:
                            first_units(nm, xh, xl)
                            return
                        unit(name, 0, i, xh, xl, ready=(nm.ready, nm.tile) if f0 else None)
                        unit(name, 1, i, xh, xl, between=norm_between(nm) if f0 else {})
                    loop(pe, n, body, first=(g == 0), last=False)
                    dname = f"down{f}_{g}"
                    def dbody(i):
                        for s in range(2):
                            f0 = isinstance(i, int) and s == 0
                            unit(dname, s, i, hh, hl, kt=n, ready=(sg.ready, sg.tile + t0) if f0 else None)
                    loop(pe, DT // 2, dbody, first=True, last=False)
                    t0 += n

            pe.wait_ge(setup, 7)
            pe.wait_ge(cst_in, 32)
            ffn(1, norms[0], hh1, hl1, xh1, xl1)

            def l2_sums(j):
                pe.wait_ge(ab["z"], 1)
                for b, t in enumerate((s1, s2)):
                    pe.wait_ge(sq_done, j * 2 + b + 1)
                    for hf in range(2):
                        last = MM(aux[b][:, HALF * hf:HALF * hf + HALF], ones[:, :], t[:, HALF * hf:HALF * hf + HALF],
                                  start=True, stop=True)
                    last.then_inc(l2_sum, 1)

            def qk(i):
                f0 = isinstance(i, int) and i == 0
                unit("qk", 0, i, xhm, xlm, ready=(norms[1].ready, norms[1].tile) if f0 else None)
                unit("qk", 1, i, xhm, xlm, between=norm_between(norms[1]) if f0 else {(0, 3): lambda: l2_sums(i - 1)})
                if f0:
                    pe.wait_ge(ab["w"], 2)
                    pe.wait_ge(norms[1].rstd, norms[1].n + 1)
                    for b in range(2):
                        o = aux[0][0:AB, HALF * b:HALF * b + HALF]
                        for k in range(DT):
                            a, z = (t[:, k, HALF * b:HALF * b + HALF] for t in (xhm, xlm))
                            MM(o, wab[1][:, k, :], a, start=(k == 0), stop=False)
                            MM(o, wab[1][:, k, :], z, start=False, stop=False)
                            last = MM(o, wab[2][:, k, :], a, start=False, stop=(k == DT - 1))
                    last.then_inc(ab["mm"], 1)
            loop(pe, HEADS, qk, first=True, last=False)

            def ab_columns():
                pe.wait_ge(ab["dve"], 4)
                pe.wait_ge(l2_ln, 2 * HEADS)
                for c in range(NC):
                    last = nc.tensor.transpose(aux[0][:, AB * c:AB * c + AB], ab_y[0:AB, c * P:c * P + P],
                                               ident[0:AB, 0:AB])
                last.then_inc(ab["t"], 1)

            def v(i):
                f0 = isinstance(i, int)
                unit("v", 0, i, xhm, xlm, between={(1, 7): lambda: l2_sums(HEADS - 1)} if f0 else {})
                unit("v", 1, i, xhm, xlm, between={(0, 6): ab_columns} if f0 else {})
                if f0:
                    pe.wait_ge(ab["cols"], 2)
                    MM(aux[1][:, 0:64], upper[:, :], la[:, 0:NC * HEADS], start=True, stop=True)
                    MM(aux[1][:, 64:128], ones[:, :], la[:, 0:NC * HEADS], start=True, stop=True).then_inc(ab["g"], 1)
            loop(pe, 4, v, first=True, last=False)

            pe.wait_ge(ab["gact"], 3)
            pe.wait_ge(ab["gv"], 2)

            def delta(c):
                B = lambda n, g: dn[n, g]
                piece = [0]

                def fill(n):
                    for j in range(piece[0], piece[0] + n):
                        s, b, k = j // 16, j // 8 % 2, j % 8
                        if j % 16 == 0:
                            pe.wait_ge(w_ready[s], BASE["uv"][s] + c + 1)
                            pe.wait_ge(acc_free[s], BASE["uv"][s] + c)
                        last = products(s, b, k, DT, xhm, xlm)
                        if j % 16 == 15:
                            last.then_inc(acc_done[s], 1)
                    piece[0] += n

                for g in range(2):
                    pe.wait_ge(dn_s["laU"], c * 2 + g + 2)
                    pe.wait_ge(dn_s["oc"], c * 2 + g + 1)
                    MM(bank[g, 1], ones[:, :], B("LU", g)[:, :, :], start=True, stop=True).then_inc(dn_s["G"], 1)
                fill(2)
                for g in range(2):
                    pe.wait_ge(k_in, c * 16 + 16)
                    pe.wait_ge(dn_s["S"], c * 2 + g + 1)
                    for h in range(HG):
                        last = nc.tensor.transpose(bank[g, 0][:, h, :], kc[:, HG * g + h, :], ident[:, :])
                    last.then_inc(dn_s["tk"], 1)
                fill(1)
                for g in range(2):
                    pe.wait_ge(dn_s["argA"], c * 2 + g + 1)
                    for h in range(HG):
                        last = MM(bank[g, 1][:, h, :], kc[:, HG * g + h, :], kc[:, HG * g + h, :], start=True, stop=True)
                    last.then_inc(dn_s["kk"], 1)
                for g in range(2):
                    pe.wait_ge(q_in, c * 16 + 16)
                    pe.wait_ge(dn_s["Kd"], c * 2 + g + 1)
                    for h in range(HG):
                        last = MM(bank[g, 0][:, h, :], kc[:, HG * g + h, :], qc[:, HG * g + h, :], start=True, stop=True)
                    last.then_inc(dn_s["qk"], 1)
                fill(2)
                for g in range(2):
                    pe.wait_ge(v_in, c * 16 + 16)
                    pe.wait_ge(dn_s["NTa"], c * 2 + g + 1)
                    for h in range(HG):
                        last = nc.tensor.transpose(bank[g, 1][:, h, :], vc[:, HG * g + h, :], ident[:, :])
                    last.then_inc(dn_s["tv"], 1)
                fill(1)
                for g in range(2):
                    pe.wait_ge(dn_s["AT"], c * 2 + g + 1)
                    for h in range(HG):
                        last = MM(bank[g, 0][:, h, :], kc[:, HG * g + h, :], B("S", g)[:, h, :], start=True, stop=True)
                    last.then_inc(dn_s["KS"], 1)
                fill(3)
                for l in range(1, 5):
                    for g in range(2):
                        pe.wait_ge(dn_s["T"], (c * 5 + l - 1) * 2 + g + 1)
                        if l == 1:
                            pe.wait_ge(dn_s["V"], c * 2 + g + 1)
                        carry(pe)
                        for h in range(HG):
                            for q in quad:
                                last = MM(bankc[g, 1][q, h, :], B("NT", g)[q, h, q], B("Tc", g)[q, h, :],
                                          start=True, stop=True)
                        last.then_inc(dn_s["xp"], 1)
                    fill((2, 2, 2, 1)[l - 1])
                    for g in range(2):
                        pe.wait_ge(dn_s["X"], (c * 4 + l - 1) * 2 + g + 1)
                        if l == 1:
                            pe.wait_ge(dn_s["eKS"], c * 2 + g + 1)
                        carry(pe)
                        for h in range(HG):
                            for q in quad:
                                last = MM(bankc[g, 0][q, h, :], B("Xc", g)[q, h, :], B("TTc", g)[q, h, :],
                                          start=True, stop=True)
                        last.then_inc(dn_s["up"], 1)
                    fill((3, 2, 2, 1)[l - 1])
                for g in range(2):
                    pe.wait_ge(dn_s["T"], (c * 5 + 4) * 2 + g + 1)
                    carry(pe)
                    for h in range(HG):
                        for lo, hi in ((0, 1), (2, 3)):
                            last = MM(bankc[g, 1][quad[hi], h, :], B("NT", g)[quad[lo], h, quad[hi]],
                                      B("Tc", g)[quad[lo], h, :], start=True, stop=True)
                    last.then_inc(dn_s["x5"], 1)
                fill(2)
                for g in range(2):
                    pe.wait_ge(dn_s["X5"], c * 2 + g + 1)
                    carry(pe)
                    for h in range(HG):
                        for lo, hi in ((0, 1), (2, 3)):
                            MM(bankc[g, 0][quad[lo], h, :], B("Xc", g)[quad[hi], h, :], B("TTc", g)[quad[hi], h, :],
                               start=True, stop=True)
                        last = MM(bankt[g, 0][quad[1], h, :], B("TTc", g)[quad[1], h, :], B("Xc", g)[quad[1], h, :],
                                  start=True, stop=True)
                    last.then_inc(dn_s["u5"], 1)
                fill(2)
                for g in range(2):
                    pe.wait_ge(dn_s["T5"], c * 2 + g + 1)
                    carry(pe)
                    for h in range(HG):
                        last = MM(bank64[g, 1][64:128, h, :], B("NT", g)[0:64, h, 64:128], B("Tf", g)[0:64, h, :],
                                  start=True, stop=True)
                    last.then_inc(dn_s["x6"], 1)
                fill(2)
                for g in range(2):
                    pe.wait_ge(dn_s["X6"], c * 2 + g + 1)
                    carry(pe)
                    for h in range(HG):
                        last = MM(bank64[g, 0][0:64, h, :], B("X6", g)[64:128, h, :], B("TT", g)[64:128, h, 64:128],
                                  start=True, stop=True)
                    last.then_inc(dn_s["u6"], 1)
                fill(2)
                for g in range(2):
                    pe.wait_ge(dn_s["Rr"], c * 2 + g + 1)
                    pe.wait_ge(dn_s["T6"], c * 2 + g + 1)
                    for h in range(HG):
                        last = MM(bank[g, 0][:, h, :], B("TT", g)[:, h, :], B("V", g)[:, h, :], start=True, stop=True)
                    last.then_inc(dn_s["TR"], 1)
                for g in range(2):
                    pe.wait_ge(dn_s["vn"], c * 2 + g + 1)
                    for h in range(HG):
                        MM(bank[g, 1][:, h, :], B("S", g)[:, h, :], B("D", g)[:, h, :], start=True, stop=False)
                        last = MM(bank[g, 1][:, h, :], B("X", g)[:, h, :], B("AT", g)[:, h, :], start=False, stop=True)
                    last.then_inc(dn_s["o"], 1)
                for g in range(2):
                    for h in range(HG):
                        last = MM(bank[g, 0][:, h, :], B("Ktm", g)[:, h, :], B("X", g)[:, h, :], start=True, stop=True)
                    last.then_inc(dn_s["Kv"], 1)
                assert piece[0] == 32, piece
            with pe.Fori(0, NC) as c:
                delta(c)

            def o_sums(m):
                pe.wait_ge(g_s["sq"], m + 1)
                for hf in range(2):
                    last = MM(aux[0][:, HALF * hf:HALF * hf + HALF], ones[:, :], s2[:, HALF * hf:HALF * hf + HALF],
                              start=True, stop=True)
                last.then_inc(g_s["sum"], 1)

            def gate(i):
                for s in range(2):
                    m = i * 2 + s
                    unit("g", s, i, xhm, xlm,
                         between={} if isinstance(m, int) and m == 0 else {(0, 6): lambda: o_sums(m - 1)})
            loop(pe, 4, gate, first=True, last=False)

            def gaya(i):
                f0 = isinstance(i, int)
                unit("gaya", 0, i, xhm, xlm, between={(0, 7): lambda: o_sums(HEADS - 1)} if f0 else {})
                unit("gaya", 1, i, oh, ol, ready=(g_s["ready"], 0) if f0 else None)
                if f0:
                    pe.wait_ge(u_s["w"], 1)
                    ws = wsT[:, :, :].rearrange("p m t -> p (m t)")
                    for hf in range(2):
                        last = MM(aux[1][:, HALF * hf:HALF * hf + HALF], ones[:, :], ws[:, HALF * hf:HALF * hf + HALF],
                                  start=True, stop=True)
                    last.then_inc(u_s["rows"], 1)
            loop(pe, 8, gaya, first=True, last=False)

            def mix(n):
                pe.wait_ge(b_s_["z"], n + 1)
                if isinstance(n, int) and n == 0:
                    pe.wait_ge(u_s["bias"], 8)
                else:
                    pe.wait_ge(b_s_["prod"], n)
                for m in range(DT):
                    last = MM(aux[1][:, m * P:m * P + P], s1[:, m * P:m * P + P], wsT[:, m, :], start=True, stop=True)
                last.then_inc(b_s_["mix"], 1)

            def gb(i):
                for s in range(2):
                    n = i * 2 + s
                    unit("gb", s, i, xhm, xlm)
                    pe.wait_ge(b_s_["copy"], n + 1)
                    if not (isinstance(i, int) and n == 0):
                        pe.wait_ge(b_s_["z"], n)
                    for m in range(DT):
                        last = nc.tensor.transpose(aux[0][:, m * P:m * P + P], s0[:, m * P:m * P + P], ident[:, :])
                    last.then_inc(b_s_["tr"], 1)
                    if not (isinstance(i, int) and n == 0):
                        mix(n - 1)
            loop(pe, 4, gb, first=True, last=False)

            for s in range(2):
                pe.wait_ge(w_ready[s], BASE["yb"][s] + 1)
                pe.wait_ge(acc_free[s], BASE["yb"][s])
                pe.wait_ge(b_s_["ready"], NC // 2)
                for k in range(DT):
                    products(s, 0, k, DT, sh, sl)
                if s == 0:
                    mix(NC - 1)
            pe.wait_ge(b_s_["ready"], NC)
            for s in range(2):
                for k in range(DT):
                    last = products(s, 1, k, DT, sh, sl)
                last.then_inc(acc_done[s], 1)

            def yb(i):
                for s in range(2):
                    unit("yb", s, i, sh, sl)
            with pe.Fori(1, 4) as i:
                yb(i)

            def wo(i):
                for s in range(2):
                    unit("wo", s, i, mh, ml, ready=(yb_s["ready"], 0) if isinstance(i, int) and s == 0 else None)
            loop(pe, 4, wo, first=True, last=False)

            ffn(2, norms[2], hh2, hl2, xh2, xl2)
            sums(norms[3])
            spread(norms[3])


def _level_masks():
    i = np.arange(P)
    later = (i[None, :] >= i[:, None]).astype(np.float32)
    bound = np.where(later > 0, 0.0, -1e30).astype(np.float32)
    r, c = (i % B32)[:, None], np.arange(B32)[None, :]
    def level(l):
        return (r >> (l + 1) == c >> (l + 1)) & ((r >> l) & 1 == 1) & ((c >> l) & 1 == 0)
    up = (r >> 1 == c >> 1) & (r & 1 == 0) & (c & 1 == 1)
    blocks = np.concatenate([(r == c)] + [up] + [level(l) for l in range(1, 5)], axis=1).astype(np.float32)
    blocks = np.pad(blocks, ((0, 0), (0, 2 * P - blocks.shape[1]))).reshape(P, 2, P)
    return np.ascontiguousarray(np.concatenate([np.stack([np.eye(P, dtype=np.float32), later, bound], axis=1), blocks],
                                               axis=1))


def _tiles(w):
    k, n = w.shape
    return np.ascontiguousarray(w.reshape(k // P, P, n // P, P).transpose(2, 1, 0, 3))


def kernel(**inputs):
    import concourse.bacc as bacc
    from concourse.bass_utils import run_bass_kernel_spmd

    a = {k: np.asarray(v) for k, v in inputs.items()}
    col = lambda v: v.reshape(-1, P).T
    vec = np.zeros((P, V_ALL), np.float32)
    for at, name in ((V_N1, "ffn1_norm_w"), (V_NM, "mix_norm_w"), (V_N2, "ffn2_norm_w"), (V_SW, "sgu_norm_w"),
                     (V_SB, "sgu_norm_b")):
        vec[:, at:at + DT] = col(a[name][0])
    vec[:, V_NF:V_NF + DT] = col(a["final_norm_w"])
    vec[:, V_DN] = a["dn_out_norm_w"][0]
    vec[LANE_A:LANE_A + HEADS, V_DT] = a["dn_dt_bias"][0]
    vec[LANE_A:LANE_A + HEADS, V_AL] = a["dn_a_log"][0]
    vec[:, V_CW:] = a["dn_conv_w"][0].reshape(TAPS, 3 * HEADS, P).transpose(2, 1, 0).reshape(P, -1)
    w_in = a["w_in"][0]
    nb = 4 * D
    w_ba = np.zeros((D, AB), np.float32)
    w_ba[:, 0:HEADS] = w_in[:, nb:nb + HEADS]
    w_ba[:, LANE_A:LANE_A + HEADS] = w_in[:, nb + HEADS:nb + 2 * HEADS]
    arrays = {
        "x": np.ascontiguousarray(a["x"][0].T).reshape(DT, P, SEQ),
        "vec": vec, "cst": _level_masks(),
        "w_gate1": _tiles(a["ffn1_w_gate"][0]), "w_up1": _tiles(a["ffn1_w_up"][0]),
        "w_down1": _tiles(a["ffn1_w_down"][0]),
        "w_in": _tiles(np.concatenate([w_in[:, :nb], w_in[:, nb + 2 * HEADS:]], axis=1)),
        "w_ba": np.ascontiguousarray(w_ba.reshape(DT, P, AB).transpose(1, 0, 2)), "w_ya": _tiles(a["dn_w_o"][0]), "w_yb": _tiles(a["gmlp_w_o"][0]),
        "w_out": _tiles(a["w_out"][0]),
        "w_s": np.ascontiguousarray(a["sgu_w_s"][0].transpose(2, 0, 1)),
        "b_s": np.ascontiguousarray(np.broadcast_to(a["sgu_b"][0].reshape(1, -1), (P, D))),
        "w_gate2": _tiles(a["ffn2_w_gate"][0]), "w_up2": _tiles(a["ffn2_w_up"][0]),
        "w_down2": _tiles(a["ffn2_w_down"][0]),
    }
    nc = bacc.Bacc("TRN2", target_bir_lowering=False, num_devices=1)
    f32 = mybir.dt.float32
    aps = [nc.dram_tensor(f"in_{k}", v.shape, f32, kind="ExternalInput").ap() for k, v in arrays.items()]
    h_spill = nc.dram_tensor("h_spill", (DT, P, SEQ), f32, kind="Internal").ap()
    m_spill = nc.dram_tensor("m_spill", (DT, P, SEQ), f32, kind="Internal").ap()
    more = [nc.dram_tensor(f"{n}_spill", (DT, P, SEQ), f32, kind="Internal").ap() for n in "qkvuo"]
    out = nc.dram_tensor("out", (DT, P, SEQ), f32, kind="ExternalOutput").ap()
    build(nc, *aps, h_spill, m_spill, *more, out)
    r = run_bass_kernel_spmd(nc, [{f"in_{k}": v for k, v in arrays.items()}], core_ids=[0])
    y = np.asarray(r.results[0]["out"]).reshape(D, SEQ)
    return np.ascontiguousarray(y.T).reshape(1, SEQ, D)
```
